# Optimizing a Trainium2 kernel written in Bass

```python
import jax, jax.numpy as jnp
from jax import lax
import numpy as np

D_MODEL = 1024
BATCH = 1
SEQ = 1024
DEPTH = 1
DEC_BATCH = 8
DEC_SEQ = 1
PAST_LEN = 8192
PAGE_SIZE = 128

A_WIDTH = D_MODEL // 2
A_GROUPS = 8
A_GROUP_DIM = A_WIDTH // A_GROUPS
CHUNK = 128
B_WIDTH = D_MODEL - A_WIDTH
RWKV_HEAD = 64
RWKV_HEADS = B_WIDTH // RWKV_HEAD
DECAY_LORA = 64
AAA_LORA = 64
GATE_LORA = 160
B_PROJ = 3 * B_WIDTH + DECAY_LORA + AAA_LORA + GATE_LORA
IN_PROJ = 2 * A_WIDTH + B_PROJ
MIX_WIDTH = A_WIDTH + B_WIDTH
D_FF = 2816
N_MEM = 256
XA_HEADS = 4
XA_HEAD_DIM = D_MODEL // XA_HEADS
NORM_EPS = 1e-6
LN_EPS = 1e-5
GN_EPS = 64e-5

kernel_name = "hymba_gmlp_rwkv7_macaron_memxattn_step"

def rms_norm(x, g):
    xf = x.astype(jnp.float32)
    y = xf * lax.rsqrt(jnp.mean(xf * xf, axis=-1, keepdims=True) + NORM_EPS)
    return (y * g).astype(x.dtype)

def layer_norm(x, g, b):
    xf = x.astype(jnp.float32)
    mu = jnp.mean(xf, axis=-1, keepdims=True)
    var = jnp.mean(jnp.square(xf - mu), axis=-1, keepdims=True)
    return ((xf - mu) * lax.rsqrt(var + LN_EPS) * g + b).astype(x.dtype)

def swiglu(x, w_gate, w_up, w_down):
    return ((jax.nn.silu(x @ w_gate) * (x @ w_up)) @ w_down).astype(x.dtype)

def chunk_mix(v, w_s, b_s):
    bsz, t = v.shape[0], v.shape[1]
    n_c = -(-t // CHUNK)
    vp = jnp.pad(v, ((0, 0), (0, n_c * CHUNK - t), (0, 0), (0, 0)))
    vp = vp.reshape(bsz, n_c, CHUNK, A_GROUPS, A_GROUP_DIM)
    mask = jnp.tril(jnp.ones((CHUNK, CHUNK), dtype=bool))
    w = jnp.where(mask[None], w_s, 0).astype(v.dtype)
    mixed = jnp.einsum('gts,bcsgd->bctgd', w, vp) + jnp.swapaxes(b_s, 0, 1)[None, None, :, :, None]
    return mixed.reshape(bsz, n_c * CHUNK, A_GROUPS, A_GROUP_DIM)[:, :t]

def rwkv7_scan(state0, r, w, k, v, kk, a):
    def step(S, inp):
        r_t, w_t, k_t, v_t, kk_t, a_t = inp
        sa = jnp.einsum('bhvk,bhk->bhv', S, -kk_t)
        S = (S * w_t[:, :, None, :] + sa[..., None] * (kk_t * a_t)[:, :, None, :]
             + v_t[..., None] * k_t[:, :, None, :])
        return S, jnp.einsum('bhvk,bhk->bhv', S, r_t)
    xs = tuple(jnp.swapaxes(z, 0, 1) for z in (r, w, k, v, kk, a))
    S, out = lax.scan(step, state0, xs)
    return S, jnp.swapaxes(out, 0, 1)

def token_mix(h, shift_prev, rwkv_state, w_in, w_out, sgu_w, sgu_b, sgu_ln_g, sgu_ln_b,
              rwkv_mu, rwkv_w0, rwkv_w2, rwkv_a0, rwkv_a2, rwkv_g2, rwkv_k_k, rwkv_k_a,
              rwkv_r_k, rwkv_gn_g, rwkv_gn_b):
    f32 = jnp.float32
    bsz, t, _ = h.shape
    z = h @ w_in
    za = jax.nn.gelu(z[..., :2 * A_WIDTH])
    u, va = za[..., :A_WIDTH], za[..., A_WIDTH:]
    va = layer_norm(va, sgu_ln_g, sgu_ln_b)
    mixed = chunk_mix(va.reshape(bsz, t, A_GROUPS, A_GROUP_DIM), sgu_w, sgu_b)
    ya = (u * mixed.reshape(bsz, t, A_WIDTH)).astype(h.dtype)
    zb = z[..., 2 * A_WIDTH:]
    zb_prev = jnp.concatenate([shift_prev.astype(zb.dtype), zb[:, :-1]], axis=1)
    new_shift = zb[:, -1:]
    zs = (zb + (zb_prev - zb) * rwkv_mu).astype(f32)
    o1, o2, o3 = B_WIDTH, 2 * B_WIDTH, 3 * B_WIDTH
    o4, o5 = o3 + DECAY_LORA, o3 + DECAY_LORA + AAA_LORA
    r, k, v = zs[..., :o1], zs[..., o1:o2], zs[..., o2:o3]
    wd, ad, gd = zs[..., o3:o4], zs[..., o4:o5], zs[..., o5:]
    w_log = -jax.nn.softplus(-(rwkv_w0 + jnp.tanh(wd) @ rwkv_w2)) - 0.5
    decay = jnp.exp(-jnp.exp(w_log))
    a = jax.nn.sigmoid(rwkv_a0 + ad @ rwkv_a2)
    g = jax.nn.sigmoid(gd) @ rwkv_g2
    heads = lambda q: q.reshape(bsz, t, RWKV_HEADS, RWKV_HEAD)
    kk = heads(k * rwkv_k_k)
    kk = kk * lax.rsqrt(jnp.maximum(jnp.sum(kk * kk, axis=-1, keepdims=True), 1e-24))
    k = k * (1.0 + (a - 1.0) * rwkv_k_a)
    rh, kh, vh = heads(r), heads(k), heads(v)
    new_state, o = rwkv7_scan(rwkv_state.astype(f32), rh, heads(decay), kh, vh, kk, heads(a))
    mu = jnp.mean(o, axis=-1, keepdims=True)
    var = jnp.mean(jnp.square(o - mu), axis=-1, keepdims=True)
    o = ((o - mu) * lax.rsqrt(var + GN_EPS)).reshape(bsz, t, B_WIDTH) * rwkv_gn_g + rwkv_gn_b
    bonus = (jnp.sum(rh * kh * rwkv_r_k, axis=-1, keepdims=True) * vh).reshape(bsz, t, B_WIDTH)
    yb = ((o + bonus) * g).astype(h.dtype)
    y = jnp.concatenate([ya, yb], axis=-1) @ w_out
    return y.astype(h.dtype), new_state.astype(h.dtype), new_shift, va

def memory_kv(mem, mem_norm_g, w_k, w_v):
    m = rms_norm(mem, mem_norm_g)
    bsz = mem.shape[0]
    mk = (m @ w_k).reshape(bsz, N_MEM, XA_HEADS, XA_HEAD_DIM)
    mv = (m @ w_v).reshape(bsz, N_MEM, XA_HEADS, XA_HEAD_DIM)
    return mk, mv

def cross_attn(h, mk, mv, w_q, w_o):
    bsz, t, _ = h.shape
    q = (h @ w_q).reshape(bsz, t, XA_HEADS, XA_HEAD_DIM)
    s = jnp.einsum('bthd,bmhd->bhtm', q, mk).astype(jnp.float32) * (XA_HEAD_DIM ** -0.5)
    p = jax.nn.softmax(s, axis=-1).astype(h.dtype)
    o = jnp.einsum('bhtm,bmhd->bthd', p, mv.astype(h.dtype)).reshape(bsz, t, D_MODEL)
    return (o @ w_o).astype(h.dtype)

def decoder_layer(x, mem_k, mem_v, shift_prev, rwkv_state, *, ln_ffn1, ffn1_gate, ffn1_up,
                  ffn1_down, ln_mix, w_in, w_out, sgu_w, sgu_b, sgu_ln_g, sgu_ln_b, rwkv_mu,
                  rwkv_w0, rwkv_w2, rwkv_a0, rwkv_a2, rwkv_g2, rwkv_k_k, rwkv_k_a, rwkv_r_k,
                  rwkv_gn_g, rwkv_gn_b, ln_xattn, xa_q, xa_o, ln_ffn2, ffn2_gate, ffn2_up,
                  ffn2_down):
    x = x + 0.5 * swiglu(rms_norm(x, ln_ffn1), ffn1_gate, ffn1_up, ffn1_down)
    y, new_state, new_shift, va = token_mix(
        rms_norm(x, ln_mix), shift_prev, rwkv_state, w_in, w_out, sgu_w, sgu_b, sgu_ln_g,
        sgu_ln_b, rwkv_mu, rwkv_w0, rwkv_w2, rwkv_a0, rwkv_a2, rwkv_g2, rwkv_k_k, rwkv_k_a,
        rwkv_r_k, rwkv_gn_g, rwkv_gn_b)
    x = x + y
    x = x + cross_attn(rms_norm(x, ln_xattn), mem_k, mem_v, xa_q, xa_o)
    x = x + 0.5 * swiglu(rms_norm(x, ln_ffn2), ffn2_gate, ffn2_up, ffn2_down)
    return x, new_state, new_shift, va

def setup_inputs(seed: int = 0) -> dict:
    key = jax.random.key(seed)
    ks = iter(jax.random.split(key, 64))
    f32 = jnp.float32
    nrm = lambda shape, scale: jax.random.normal(next(ks), shape, f32) * scale
    gain = lambda shape: 1.0 + jax.random.normal(next(ks), shape, f32) * 0.05
    L = DEPTH
    return {
        "x_prompt": nrm((BATCH, SEQ, D_MODEL), 1.0),
        "x_sample": nrm((DEC_BATCH, DEC_SEQ, D_MODEL), 1.0),
        "state_rwkv": nrm((L, DEC_BATCH, RWKV_HEADS, RWKV_HEAD, RWKV_HEAD), 0.5),
        "state_shift": nrm((L, DEC_BATCH, 1, B_PROJ), 1.0),
        "cache_mem_k": nrm((L, DEC_BATCH, N_MEM, XA_HEADS, XA_HEAD_DIM), 1.0),
        "cache_mem_v": nrm((L, DEC_BATCH, N_MEM, XA_HEADS, XA_HEAD_DIM), 1.0),
        "mem_prompt": nrm((BATCH, N_MEM, D_MODEL), 1.0),
        "ln_ffn1": gain((L, D_MODEL)),
        "ffn1_gate": nrm((L, D_MODEL, D_FF), D_MODEL ** -0.5),
        "ffn1_up": nrm((L, D_MODEL, D_FF), D_MODEL ** -0.5),
        "ffn1_down": nrm((L, D_FF, D_MODEL), D_FF ** -0.5),
        "ln_mix": gain((L, D_MODEL)),
        "w_in": nrm((L, D_MODEL, IN_PROJ), D_MODEL ** -0.5),
        "w_out": nrm((L, MIX_WIDTH, D_MODEL), MIX_WIDTH ** -0.5),
        "sgu_w": nrm((L, A_GROUPS, CHUNK, CHUNK), 0.5 * CHUNK ** -0.5),
        "sgu_b": gain((L, A_GROUPS, CHUNK)),
        "sgu_ln_g": gain((L, A_WIDTH)),
        "sgu_ln_b": nrm((L, A_WIDTH), 0.01),
        "rwkv_mu": jax.random.uniform(next(ks), (L, B_PROJ), f32),
        "rwkv_w0": nrm((L, B_WIDTH), 0.5),
        "rwkv_w2": nrm((L, DECAY_LORA, B_WIDTH), DECAY_LORA ** -0.5),
        "rwkv_a0": nrm((L, B_WIDTH), 0.1),
        "rwkv_a2": nrm((L, AAA_LORA, B_WIDTH), AAA_LORA ** -0.5),
        "rwkv_g2": nrm((L, GATE_LORA, B_WIDTH), GATE_LORA ** -0.5),
        "rwkv_k_k": 0.85 + nrm((L, B_WIDTH), 0.05),
        "rwkv_k_a": gain((L, B_WIDTH)),
        "rwkv_r_k": nrm((L, RWKV_HEADS, RWKV_HEAD), 0.1),
        "rwkv_gn_g": gain((L, B_WIDTH)),
        "rwkv_gn_b": nrm((L, B_WIDTH), 0.01),
        "ln_xattn": gain((L, D_MODEL)),
        "mem_norm": gain((L, D_MODEL)),
        "xa_q": nrm((L, D_MODEL, D_MODEL), D_MODEL ** -0.5),
        "xa_k": nrm((L, D_MODEL, D_MODEL), D_MODEL ** -0.5),
        "xa_v": nrm((L, D_MODEL, D_MODEL), D_MODEL ** -0.5),
        "xa_o": nrm((L, D_MODEL, D_MODEL), D_MODEL ** -0.5),
        "ln_ffn2": gain((L, D_MODEL)),
        "ffn2_gate": nrm((L, D_MODEL, D_FF), D_MODEL ** -0.5),
        "ffn2_up": nrm((L, D_MODEL, D_FF), D_MODEL ** -0.5),
        "ffn2_down": nrm((L, D_FF, D_MODEL), D_FF ** -0.5),
        "final_norm": gain((D_MODEL,)),
    }

def reference(x_prompt, x_sample, state_rwkv, state_shift, cache_mem_k, cache_mem_v, mem_prompt,
              ln_ffn1, ffn1_gate, ffn1_up, ffn1_down, ln_mix, w_in, w_out, sgu_w, sgu_b,
              sgu_ln_g, sgu_ln_b, rwkv_mu, rwkv_w0, rwkv_w2, rwkv_a0, rwkv_a2, rwkv_g2,
              rwkv_k_k, rwkv_k_a, rwkv_r_k, rwkv_gn_g, rwkv_gn_b, ln_xattn, mem_norm, xa_q,
              xa_k, xa_v, xa_o, ln_ffn2, ffn2_gate, ffn2_up, ffn2_down, final_norm):
    hp, hs = x_prompt, x_sample
    bp = x_prompt.shape[0]
    sp_l, shp_l, mkp_l, mvp_l, ss_l, shs_l, vs_l = [], [], [], [], [], [], []
    for l in range(DEPTH):
        lp = dict(ln_ffn1=ln_ffn1[l], ffn1_gate=ffn1_gate[l], ffn1_up=ffn1_up[l],
                  ffn1_down=ffn1_down[l], ln_mix=ln_mix[l], w_in=w_in[l], w_out=w_out[l],
                  sgu_w=sgu_w[l], sgu_b=sgu_b[l], sgu_ln_g=sgu_ln_g[l], sgu_ln_b=sgu_ln_b[l],
                  rwkv_mu=rwkv_mu[l], rwkv_w0=rwkv_w0[l], rwkv_w2=rwkv_w2[l],
                  rwkv_a0=rwkv_a0[l], rwkv_a2=rwkv_a2[l], rwkv_g2=rwkv_g2[l],
                  rwkv_k_k=rwkv_k_k[l], rwkv_k_a=rwkv_k_a[l], rwkv_r_k=rwkv_r_k[l],
                  rwkv_gn_g=rwkv_gn_g[l], rwkv_gn_b=rwkv_gn_b[l], ln_xattn=ln_xattn[l],
                  xa_q=xa_q[l], xa_o=xa_o[l], ln_ffn2=ln_ffn2[l], ffn2_gate=ffn2_gate[l],
                  ffn2_up=ffn2_up[l], ffn2_down=ffn2_down[l])
        mk_p, mv_p = memory_kv(mem_prompt, mem_norm[l], xa_k[l], xa_v[l])
        zero_state = jnp.zeros((bp, RWKV_HEADS, RWKV_HEAD, RWKV_HEAD), jnp.float32)
        zero_shift = jnp.zeros((bp, 1, B_PROJ), hp.dtype)
        hp, s_p, sh_p, _ = decoder_layer(hp, mk_p, mv_p, zero_shift, zero_state, **lp)
        hs, s_s, sh_s, v_s = decoder_layer(hs, cache_mem_k[l], cache_mem_v[l], state_shift[l],
                                           state_rwkv[l], **lp)
        sp_l.append(s_p); shp_l.append(sh_p); mkp_l.append(mk_p); mvp_l.append(mv_p)
        ss_l.append(s_s); shs_l.append(sh_s); vs_l.append(v_s)
    y_prompt = rms_norm(hp, final_norm)
    y_sample = rms_norm(hs, final_norm)
    return (y_prompt, y_sample, jnp.stack(sp_l), jnp.stack(shp_l), jnp.stack(mkp_l),
            jnp.stack(mvp_l), jnp.stack(ss_l), jnp.stack(shs_l), jnp.stack(vs_l))


_drawn_inputs = setup_inputs


def setup_inputs(seed=0):
    import zlib

    import numpy as np

    out = dict(_drawn_inputs(seed))
    spreads = {}
    factors = {'sgu_b': 2.938,
     'sgu_ln_b': 5.951,
     'rwkv_k_k': 4.776,
     'rwkv_gn_g': 3.974,
     'rwkv_gn_b': 8.0,
     'ln_xattn': 8.0,
     'ln_ffn2': 3.418}
    for name, (base, spread) in spreads.items():
        noise = np.random.default_rng([zlib.crc32(name.encode()), seed]).standard_normal(out[name].shape)
        drawn = base * np.exp(spread * noise) if base else spread * noise
        out[name] = __import__('jax').numpy.asarray(drawn.astype(out[name].dtype))
    for name, factor in factors.items():
        out[name] = (out[name] * factor).astype(out[name].dtype)
    return out
```

```python
import numpy as np
import concourse.bass as bass
from concourse import mybir
from contextlib import ExitStack

P = 128
D, SEQ, NS = 1024, 1024, 8
T = SEQ + NS
KD = D // P
TOK = [(0, 344), (344, 344), (688, 344)]
DFF = 2816
FT = DFF // P
GROUPS = [8, 8, 6]
AW = BW = 512
HEADS, HN = 8, 64
NB = 3 * BW + 64 + 64 + 160
INP = 2 * AW + NB
NBT = -(-NB // P)
CH = 64
NMEM, XH, XD = 256, 4, 256
DECAY = float(np.exp(-0.5))

LOG_SHIFT = 20 * float(np.log(2.0))

VROWS = [("ln_ffn1", 8), ("ln_mix", 8), ("ln_xattn", 8), ("mem_norm", 8), ("ln_ffn2", 8),
         ("final_norm", 8), ("rwkv_w0", 4), ("rwkv_a0", 4), ("rwkv_k_k", 4), ("rwkv_k_a", 4),
         ("rwkv_r_k", 4), ("rwkv_gn_g", 4), ("rwkv_gn_b", 4), ("rwkv_mu", NBT)]
VAT, _n = {}, 0
for _name, _k in VROWS:
    VAT[_name] = _n
    _n += _k
NVEC = _n

C_ID, C_ONE, C_BLK, C_STR, C_INC, C_TRI, C_LVL = 0, 1, 2, 3, 4, 5, 6
NCST = 12
LEVELS = 6


def constants():
    s, t = np.arange(P)[:, None], np.arange(P)[None, :]
    same = s // CH == t // CH
    tabs = [s == t, s == s + 0 * t, same / HN, same & (s < t), same & (s <= t), s <= t]
    tabs += [(s >> (l + 1) == t >> (l + 1)) & (s >> l < t >> l) for l in range(LEVELS)]
    return np.stack([np.asarray(m, np.float32) for m in tabs], 1)


def program(nc, A, O):
    F, R = mybir.dt.float32, mybir.dt.float32r
    ALU, ACT, AX = mybir.AluOpType, mybir.ActivationFunctionType, mybir.AxisListType
    ds = bass.ds
    ctx = ExitStack()
    with ctx:
        base = [-(-int(nc.sbuf_base) // 32) * 32]

        def take(nbytes):
            at = base[0]
            base[0] += -(-nbytes // 32) * 32
            return at

        def at(name, shape, off, dt=F):
            return nc.alloc_sbuf_tensor_at(name, shape, dt, offset=off)

        ROW = T * 4
        arena_z = take(24 * ROW)
        arena_h = take(16 * ROW)
        arena_w = take(3 * 4 * 4 * P * 4)
        arena_c = take(NCST * P * 4)
        arena_v = take(NVEC * 4)
        arena_g = take(3 * 344 * 4)
        arena_t = take(3 * 344 * 4)
        arena_m = take(8192)
        cap = int(nc.sbuf_usable_end) if not callable(nc.sbuf_usable_end) else int(nc.sbuf_usable_end())
        assert base[0] <= cap, (base[0], cap)

        x = at("x", [P, KD, T], arena_z)
        z = at("z", [P, 24, T], arena_z)
        xnat = at("xnat", [P, 8, D], arena_z + 8 * ROW)
        xnat_s = at("xnat_s", [P, D], arena_z + 16 * ROW)
        hid_hi = at("hid_hi", [P, 8, T], arena_z + 8 * ROW, R)
        hid_lo = at("hid_lo", [P, 8, T], arena_z + 16 * ROW, R)
        h_hi = at("h_hi", [P, KD, T], arena_h, R)
        h_lo = at("h_lo", [P, KD, T], arena_h + 8 * ROW, R)
        raw = at("raw", [P, 4, 4, P], arena_w)
        w_hi = at("w_hi", [P, 4, 4, P], arena_w + 8192, R)
        w_lo = at("w_lo", [P, 4, 4, P], arena_w + 16384, R)
        cst = at("cst", [P, NCST, P], arena_c)
        vec = at("vec", [P, NVEC], arena_v)
        vnat = at("vnat", [P, P], arena_g)
        gate_s = at("gate_s", [P, 3, 344], arena_g)
        tmp = at("tmp", [P, 3, 344], arena_t)
        rstd = at("rstd", [P, 3, 344], arena_m)
        bank = [ctx.enter_context(nc.psum_tensor(f"bank{i}", [P, 512], F)) for i in range(8)]
        ident = cst[:, C_ID, :]

        mem_hi = at("mem_hi", [P, KD, NMEM], arena_z + 8 * ROW, R)
        mem_lo = at("mem_lo", [P, KD, NMEM], arena_z + 8 * ROW + 8192, R)
        qT = at("qT", [P, KD, T], arena_z + 8 * ROW)
        kT = at("kT", [P, KD, NMEM], arena_z + 16 * ROW)
        v_n = at("v_n", [P, 2, D], arena_z + 16 * ROW + 8192)
        vT = at("vT", [P, KD, NMEM], arena_z + 16 * ROW + 16384)
        mk_n = at("mk_n", [P, 2, D], arena_z + 16 * ROW + 24576)
        mem_n = at("mem_n", [P, 2, D], arena_z + 16 * ROW + 24576)
        mem_sq = at("mem_sq", [P, D], arena_z + 16 * ROW + 16384)
        cache = [at("cache0", [P, 2, D], arena_z + 16 * ROW + 16384),
                 at("cache1", [P, 2, D], arena_z + 16 * ROW + 24576)]
        prob = [at("prob0", [P, XH, NMEM], arena_g), at("prob1", [P, XH, NMEM], arena_m)]
        probT = [at("probT0", [P, XH * 2, P], arena_t), at("probT1", [P, XH * 2, P], arena_m + 4096)]
        att = at("att", [P, 2, 4, XH], arena_c + C_LVL * 512)
        mem_st = at("mem_st", [P, 2, 4], arena_c + C_LVL * 512 + 128)
        s_smp = at("s_smp", [P, NS * XH, 2], arena_c + C_LVL * 512 + 256)
        s_row = at("s_row", [NS * XH, 4], arena_c + C_LVL * 512 + 512)
        p_smp = at("p_smp", [NS * XH, NMEM], arena_c + C_LVL * 512 + 544)
        pT_smp = [at("pT_smp0", [P, NS, 33], arena_c + C_BLK * 512),
                  at("pT_smp1", [P, NS, 33], arena_c + C_LVL * 512 + 2016)]
        s_junk = at("s_junk", [P, XD], arena_c + C_STR * 512)
        o_rows = at("o_rows", [NS, D], arena_z + 16 * ROW + 16384)
        o_hi = at("o_hi", [P, KD, T], arena_h, R)
        o_lo = at("o_lo", [P, KD, T], arena_h + 8 * ROW, R)
        y_nat = at("y_nat", [P, 9, D], arena_z + 8 * ROW)

        gw_nat = at("gw_nat", [P, 8, P], arena_z + 7 * ROW)
        gwT = at("gwT", [P, 8, P], arena_t)
        ln_gb = at("ln_gb", [P, 2, AW], arena_g)
        g_bias = at("g_bias", [P, 4, P], arena_m)
        g_w00 = at("g_w00", [P, 4], arena_m + 2048)
        g_stat = at("g_stat", [P, 2, 8], arena_m + 2048 + 32)
        vn = at("vn", [P, 3, AW], arena_h)
        g_mix = at("g_mix", [P, 2, AW], arena_h + 2 * ROW)
        shift_out = at("shift_out", [NS + 1, NB], arena_h + 4 * ROW)
        shift_in = at("shift_in", [NS, NB], arena_h + 6 * ROW)
        shiftT = at("shiftT", [P, NBT, NS], arena_h + 8 * ROW)
        diff = at("diff", [P, 8, T], arena_z + 8 * ROW)
        lora_w = at("lora_w", [P, BW], arena_g)
        nkk = at("nkk", [P, 4, T], arena_h)
        bvec = at("bvec", [P, 4, T], arena_h + 4 * ROW)
        sg = at("sg", [P, 4, T], arena_h + 8 * ROW)
        cum = at("cum", [P, 4, T], arena_h + 12 * ROW)
        scan_mask = at("scan_mask", [P, T], arena_z + 7 * ROW)
        mats = [{n: at(f"{n}{q}", [P, 4, P], arena_z + 8 * ROW + (8 * q + j) * 2048)
                 for j, n in enumerate(("MT", "QKT", "TT", "Ti", "Y", "LoT"), 2)}
                for q in (0, 1)]
        LQ = [at(f"LQ{q}", [P, 2, 4, P], arena_z + 8 * ROW + 8 * q * 2048) for q in (0, 1)]
        for q in (0, 1):
            mats[q]["LT"], mats[q]["QBT"] = LQ[q][:, 0], LQ[q][:, 1]
        AR = [at("AR0", [P, 2, 4, P], arena_g),
              at("AR1", [P, 2, 4, P], arena_w + 14336)]
        BK = at("BK", [P, 2, 4, P], arena_t)
        dec = at("dec", [P, 4, P], arena_z + 7 * ROW)
        ext = at("ext", [P, 4, P], arena_z + 7 * ROW + 2048)
        Bt = at("Bt", [P, BW], arena_z + 4 * ROW)
        Kt = at("Kt", [P, BW], arena_z + 4 * ROW + 2048)
        Vt = at("Vt", [P, BW], arena_m)
        vstage = at("vstage", [P, 4, P], arena_w + 18432)
        Xs = at("Xs", [P, BW], arena_m + 2048)
        Us = at("Us", [P, BW], arena_m + 4096)
        smp_n = at("smp_n", [NS, 6, BW], arena_z + 8 * ROW)
        smp_S = at("smp_S", [P, 32, HN], arena_z + 8 * ROW + 12288)
        smp_t = at("smp_t", [P, 32, HN], arena_z + 8 * ROW + 20480)
        smp_v = at("smp_v", [P, 6, HN], arena_z + 8 * ROW + 28672)
        smp_o = at("smp_o", [P, 2, 32], arena_z + 8 * ROW + 30208)
        gn_sq = at("gn_sq", [P, 3, 344], arena_t)
        smp_on = at("smp_on", [NS, BW], arena_z + 8 * ROW + 30464)
        smp_w = at("smp_w", [P, 4, NS], arena_z + 8 * ROW + 32512)
        st_out = at("st_out", [P, 4, P], arena_w + 12288)
        g2_w = at("g2_w", [P, 2, BW], arena_z + 7 * ROW)
        ya_in = at("ya_in", [P, 4, T], arena_h + 4 * ROW)
        y_hi = at("y_hi", [P, KD, T], arena_z + 8 * ROW, R)
        y_lo = at("y_lo", [P, KD, T], arena_h + 8 * ROW, R)
        st_T = at("st_T", [P, 3, 4, P], arena_w)
        decm = at("decm", [P, 2, 4, P], arena_w + 6144)

        links = [0]

        def link(ins, wait=True):
            links[0] += 1
            ins.then_inc(S("link"), 1)
            if wait:
                nc.vector.wait_ge(S("link"), links[0])

        def v_col(name, k):
            return vec[:, VAT[name] + k:VAT[name] + k + 1]

        sems = {}

        def S(name):
            if name not in sems:
                sems[name] = ctx.enter_context(nc.semaphore(name))
            return sems[name]

        raw_in = [S(f"raw_in{i}") for i in range(4)]
        hi_done = [S(f"hi_done{i}") for i in range(4)]
        split_done = [S(f"split_done{i}") for i in range(4)]
        w_used = [S(f"w_used{i}") for i in range(2)]
        mm = [S("mm0"), S("mm1")]
        evac = [S("evac0"), S("evac1")]

        phases = []
        total = {"unit": 0, "mm": [0, 0], "f": 0}

        def phase(name, units, kt, src, hi, lo, toks=TOK, width=P):
            ph = dict(name=name, units=units, kt=kt, src=src, hi=hi, lo=lo, toks=toks, width=width,
                      u0=total["unit"], mm0=list(total["mm"]), f0=total["f"])
            total["unit"] += units
            for u in range(units):
                total["mm"][(ph["u0"] + u) % 2] += len(toks)
            ph["mm1"] = list(total["mm"])
            phases.append(ph)
            return ph

        def kview(w):
            return w.rearrange("(k p) c -> p k c", p=P)

        def ffn(n):
            wg, wu, wd = (kview(A[f"ffn{n}_{m}"][0]) for m in ("gate", "up", "down"))
            out, f = [], 0
            for g in GROUPS:
                gu = phase(f"gu{n}_{f}", 2 * g, 8,
                           lambda s, i, f=f: ((wg, wu)[s], (i + f) * P), h_hi, h_lo)
                total["f"] += g
                dn = phase(f"dn{n}_{f}", 8, g,
                           lambda s, i, f=f, g=g: (wd[:, f:f + g, :], (2 * i + s) * P), hid_hi, hid_lo)
                dn["f1"] = total["f"]
                out.append((gu, dn))
                f += g
            return out

        w_in = kview(A["w_in"][0])
        ffn1 = ffn(1)
        win_a = phase("win_a", 16, 8, lambda s, i: (w_in, (2 * i + s) * P), h_hi, h_lo)
        win_b = phase("win_b", 6, 8, lambda s, i: (w_in, (2 * i + s + 16) * P), h_hi, h_lo)
        win_c = phase("win_c", 1, 8, lambda s, i: (w_in, 22 * P), h_hi, h_lo, width=NB - 14 * P)
        win = [win_a, win_b, win_c]
        wo = kview(A["w_out"][0])
        wout = phase("wout", 8, 8, lambda s, i: (wo, (2 * i + s) * P), y_hi, y_lo)
        xk, xv, xq, xo = (kview(A[n][0]) for n in ("xa_k", "xa_v", "xa_q", "xa_o"))
        MTOK = [(0, NMEM)]
        memk = phase("memk", 8, 8, lambda s, i: (xk, (2 * i + s) * P), mem_hi, mem_lo, toks=MTOK)
        memv = phase("memv", 8, 8, lambda s, i: (xv, (2 * i + s) * P), mem_hi, mem_lo, toks=MTOK)
        xaq = phase("xaq", 8, 8, lambda s, i: (xq, (2 * i + s) * P), h_hi, h_lo)
        xao = phase("xao", 8, 8, lambda s, i: (xo, (2 * i + s) * P), o_hi, o_lo)
        ffn2 = ffn(2)

        def pairs(eng, ph, step):
            first = 0
            if ph["u0"] == 0:
                step(0)
                first = 1
            if ph["units"] // 2 > first:
                with eng.Fori(first, ph["units"] // 2) as i:
                    step(i)

        def unit_steps(eng, ph, body):
            def run(i, s):
                for_u = ph["u0"] + s
                body(i, s, [((2 * for_u + h) % 4, (2 * for_u + h) // 4 + i) for h in (0, 1)])
            pairs(eng, ph, lambda i: [run(i, s) for s in (0, 1)])
            if ph["units"] % 2:
                i = ph["units"] // 2
                run(i, 0)

        def split_k(kt):
            return [(0, min(4, kt)), (4, kt - 4)]

        def load_weights(sp, ph):
            def body(i, s, turns):
                w, col = ph["src"](s, i)
                for (slot, turn), (k0, nk) in zip(turns, split_k(ph["kt"])):
                    sp.wait_ge(split_done[slot], turn)
                    sp.dma_start(raw[:, slot, 0:nk, 0:ph["width"]],
                                 w[:, k0:k0 + nk, ds(col, ph["width"])]).then_inc(raw_in[slot], 16)
            unit_steps(sp, ph, body)

        def split_weights(g, ph):
            def body(i, s, turns):
                st = (ph["u0"] + s) % 2
                for h, ((slot, turn), (k0, nk)) in enumerate(zip(turns, split_k(ph["kt"]))):
                    part = (slice(None), slot, slice(0, nk), slice(0, ph["width"]))
                    if h == 0:
                        g.wait_ge(w_used[st], turn)
                    else:
                        g.wait_ge(mm[st], i * len(ph["toks"]) + ph["mm0"][st])
                    g.wait_ge(raw_in[slot], turn * 16 + 16)
                    nc.gpsimd.tensor_tensor(w_hi[part], raw[part],
                                            cst[:, C_ONE:C_ONE + 1, 0:ph["width"]].to_broadcast(
                                                [P, nk, ph["width"]]), ALU.mult)\
                        .then_inc(hi_done[slot], 1)
                    g.wait_ge(hi_done[slot], turn + 1)
                    nc.gpsimd.tensor_tensor(w_lo[part], raw[part], w_hi[part].bitcast(F),
                                            ALU.subtract).then_inc(split_done[slot], 1)
            unit_steps(g, ph, body)

        def multiply(pe, ph, piece_ready=None):
            nt, width, kt = len(ph["toks"]), ph["width"], ph["kt"]

            def body(i, s, turns):
                st = (ph["u0"] + s) % 2
                pe.wait_ge(evac[st], i * nt + ph["mm0"][st])
                for h, ((slot, turn), (k0, nk)) in enumerate(zip(turns, split_k(kt))):
                    if piece_ready and s == 0:
                        piece_ready(h)
                    pe.wait_ge(split_done[slot], turn + 1)
                    for t, (t0, tn) in enumerate(ph["toks"]):
                        out = bank[3 * st + t][0:width, 0:tn]
                        for k in range(nk):
                            a, b = w_hi[:, slot, k, 0:width], w_lo[:, slot, k, 0:width]
                            hi, lo = ph["hi"][:, k0 + k, t0:t0 + tn], ph["lo"][:, k0 + k, t0:t0 + tn]
                            first, last = k0 + k == 0, k0 + k == kt - 1
                            nc.tensor.matmul(out, b, hi, start=first, stop=False)
                            nc.tensor.matmul(out, a, lo, start=False, stop=False)
                            m = nc.tensor.matmul(out, a, hi, start=False, stop=last)
                        if h == 1:
                            m.then_inc(mm[st], 1)
                        elif t == nt - 1:
                            m.then_inc(w_used[slot // 2], 1)
            unit_steps(pe, ph, body)

        def each_tile(eng, ph, fn):
            nt = len(ph["toks"])

            def body(i, s, turns):
                st = (ph["u0"] + s) % 2
                for t in range(nt):
                    fn(i, s, st, t, i * nt + ph["mm0"][st] + t + 1)
            unit_steps(eng, ph, body)

        def tslice(t):
            return slice(TOK[t][0], TOK[t][0] + TOK[t][1])

        def gu_scalar(act, ph, prev_down):
            st = ph["u0"] % 2
            if prev_down:
                for j in (0, 1):
                    act.wait_ge(mm[j], prev_down["mm1"][j])
            def step(i):
                for t in range(3):
                    act.wait_ge(mm[st], i * 3 + ph["mm0"][st] + t + 1)
                    act.wait_ge(S("prod"), i * 3 + 3 * ph["f0"])
                    nc.scalar.activation(gate_s[:, t, :], bank[3 * st + t][:, 0:344], ACT.Silu)\
                        .then_inc(evac[st], 1)
                for t in range(3):
                    act.wait_ge(S("prod"), i * 3 + 3 * ph["f0"] + t + 1)
                    nc.scalar.activation(hid_hi[:, ds(i, 1), tslice(t)],
                                         tmp[:, t:t + 1, :], ACT.Copy).then_inc(S("hid_hi"), 1)
            pairs(act, ph, step)

        def gu_vector(dve, ph):
            sg, su = ph["u0"] % 2, (ph["u0"] + 1) % 2
            def step(i):
                def prod(t):
                    dve.wait_ge(evac[sg], i * 3 + ph["mm0"][sg] + t + 1)
                    dve.wait_ge(mm[su], i * 3 + ph["mm0"][su] + t + 1)
                    dve.wait_ge(S("hid_lo"), i * 3 + 3 * ph["f0"])
                    nc.vector.tensor_tensor(tmp[:, t, :], gate_s[:, t, :],
                                            bank[3 * su + t][:, 0:344], ALU.mult)\
                        .then_inc(S("prod"), 1)

                def low(t):
                    dve.wait_ge(S("hid_hi"), i * 3 + 3 * ph["f0"] + t + 1)
                    nc.vector.tensor_tensor(hid_lo[:, ds(i, 1), tslice(t)], tmp[:, t:t + 1, :],
                                            hid_hi[:, ds(i, 1), tslice(t)].bitcast(F),
                                            ALU.subtract).then_inc(S("hid_lo"), 1)
                prod(0)
                prod(1)
                low(0)
                prod(2)
                low(1)
                low(2)
                dve.wait_ge(S("prod"), i * 3 + 3 * ph["f0"] + 3)
                dve.sem_inc(evac[su], 3)
            pairs(dve, ph, step)

        def add_to_x(dve, ph, scale):
            for j in (0, 1):
                dve.wait_ge(evac[j], ph["mm0"][j])

            def one(i, s, st, t, count):
                dve.wait_ge(mm[st], count)
                xs = x[:, ds(2 * i + s, 1), tslice(t)]
                nc.vector.scalar_tensor_tensor(
                    out=xs, in0=bank[3 * st + t][:, 0:344].rearrange("p (a n) -> p a n", a=1),
                    scalar=scale, in1=xs, op0=ALU.mult, op1=ALU.add).then_inc(evac[st], 1)
            each_tile(dve, ph, one)

        def norm_scalar(act, n, ready):
            ready(act)
            for t in range(3):
                for k in range(KD):
                    j = KD * t + k
                    act.wait_ge(S("sq_used"), KD * 3 * n + max(j - 2, 0))
                    nc.scalar.activation(gate_s[:, j % 3, :], x[:, k, tslice(t)], ACT.Square)\
                        .then_inc(S("sq"), 1)
                act.wait_ge(S("sq_used"), KD * (3 * n + t + 1))
                act.wait_ge(S("const"), 4)
                nc.scalar.activation(rstd[:, t, :], bank[6 + t % 2][:, 0:344], ACT.Sqrt,
                                     bias=eps_col, scale=1.0 / D).then_inc(S("rms"), 1)
            for t in range(3 if n < 4 else 0):
                for k in range(KD):
                    j = KD * t + k
                    act.wait_ge(S("nval"), KD * 3 * n + j + 1)
                    if True:
                        nc.scalar.activation(h_hi[:, k, tslice(t)], tmp[:, j % 3, :], ACT.Copy)\
                            .then_inc(S("n_hi"), 1)

        def norm_tensor(pe, n):
            for t in range(3):
                if t == 2:
                    pe.wait_ge(S("rms"), 3 * n + 1)
                for k in range(KD):
                    j = KD * t + k
                    pe.wait_ge(S("sq"), KD * 3 * n + j + 1)
                    m = nc.tensor.matmul(bank[6 + t % 2][:, 0:344], cst[:, C_ONE, :],
                                         gate_s[:, j % 3, :], start=k == 0, stop=k == KD - 1)
                    m.then_inc(S("sq_used"), 1)

        def norm_vector(dve, n, gain):
            for t in range(3):
                dve.wait_ge(S("rms"), 3 * n + t + 1)
                link(nc.vector.reciprocal(rstd[:, t, :], rstd[:, t, :]))
                if n == 4:
                    for k in range(KD):
                        xs = x[:, k, tslice(t)]
                        nc.vector.scalar_tensor_tensor(out=xs, in0=xs, scalar=v_col(gain, k),
                                                       in1=rstd[:, t, :], op0=ALU.mult,
                                                       op1=ALU.mult).then_inc(S("y_norm"), 1)
                    continue
                for k in range(KD + 1):
                    j = KD * t + k
                    if k < KD:
                        dve.wait_ge(S("n_lo"), KD * 3 * n + max(j - 2, 0))
                        nc.vector.scalar_tensor_tensor(
                            out=tmp[:, j % 3, :], in0=x[:, k, tslice(t)], scalar=v_col(gain, k),
                            in1=rstd[:, t, :], op0=ALU.mult, op1=ALU.mult).then_inc(S("nval"), 1)
                    if k > 0:
                        j -= 1
                        dve.wait_ge(S("n_hi"), KD * 3 * n + j + 1)
                        nc.vector.tensor_tensor(h_lo[:, k - 1, tslice(t)], tmp[:, j % 3, :],
                                                h_hi[:, k - 1, tslice(t)].bitcast(F),
                                                ALU.subtract).then_inc(S("n_lo"), 1)

        eps_t = at("eps_t", [P, 8], take(32))
        eps_col = eps_t[:, 0:1]


        ZB = [8 + u for u in range(8, 16)] + list(range(0, 7))
        WIN_END = win_c["mm1"]

        def z_evac(eng, is_act):
            for ph, z0 in zip(win, (8, 0, 6)):
                if ph is win_b:
                    eng.wait_ge(S("x_out"), 16)
                w = ph["width"]

                def one(i, s, st, t, count, z0=z0, w=w):
                    if (s == 0) != is_act:
                        return
                    eng.wait_ge(mm[st], count)
                    dst = z[0:w, ds(2 * i + s + z0, 1), tslice(t)]
                    src = bank[3 * st + t][0:w, 0:344].rearrange("p (a n) -> p a n", a=1)
                    if is_act:
                        nc.scalar.activation(dst, src, ACT.Copy).then_inc(evac[st], 1)
                    else:
                        nc.vector.tensor_copy(dst, src).then_inc(evac[st], 1)
                each_tile(eng, ph, one)

        def win_done(eng):
            for j in (0, 1):
                eng.wait_ge(evac[j], WIN_END[j])

        def gmlp_loads(sp):
            sp.wait_ge(S("x_out"), 16)
            sp.dma_start(gw_nat[:, :, :], A["sgu_w"][0].rearrange("g t s -> t g s"))\
                .then_inc(S("gw_in"), 16)
            sp.wait_ge(S("n_lo"), 48)
            for j, n in enumerate(("sgu_ln_g", "sgu_ln_b")):
                sp.dma_start(ln_gb[:, j, :], A[n][0].partition_broadcast(P)).then_inc(S("ln_in"), 16)
            for hp in (0, 1):
                rows = slice(64 * hp, 64 * hp + 64)
                sp.dma_start(g_bias[rows, :, :], A["sgu_b"][0][hp::2, :].partition_broadcast(64))\
                    .then_inc(S("ln_in"), 16)
                sp.dma_start(g_w00[rows, :], A["sgu_w"][0][hp::2, 0, 0].partition_broadcast(64),
                             allow_slow_non_contiguous=True)\
                    .then_inc(S("ln_in"), 16)

        def gmlp_tensor(pe):
            pe.wait_ge(S("gw_in"), 16)
            pe.wait_ge(S("rms"), 6)
            for g in range(8):
                m = nc.tensor.transpose(bank[6 + g // 4][:, (g % 4) * P:(g % 4 + 1) * P],
                                        gw_nat[:, g, :], ident)
                if g % 4 == 3:
                    m.then_inc(S("gwt"), 1)
            win_done(pe)
            pe.wait_ge(S("gelu"), 1)

            def mixing(n):
                pe.wait_ge(S("vn"), n + 1)
                pe.wait_ge(S("gwT"), 2)
                pe.wait_ge(S("gmix"), max(n - 1, 0))
                for g in range(8):
                    m = nc.tensor.matmul(
                        bank[2 + n % 2][64 * (g % 2):64 * (g % 2) + 64, (g // 2) * P:(g // 2 + 1) * P],
                        vn[:, n % 2, 64 * g:64 * g + 64], gwT[:, g, :], start=True, stop=True)
                m.then_inc(S("mixed"), 1)
            for n in range(9):
                tn = P if n < 8 else NS
                pe.wait_ge(S("vn0"), max(n - 1, 0))
                for j in range(4):
                    m = nc.tensor.transpose(bank[n % 2][0:tn, j * P:(j + 1) * P],
                                            z[:, 12 + j, n * P:n * P + tn], ident)
                m.then_inc(S("vtok"), 1)
                if n > 0:
                    mixing(n - 1)
            pe.wait_ge(S("vn"), 9)
            pe.wait_ge(S("gmix"), 7)
            for j in range(4):
                m = nc.tensor.transpose(bank[2][:, j * NS:(j + 1) * NS],
                                        vn[0:NS, 2, j * P:(j + 1) * P], ident[0:NS, 0:NS])
            m.then_inc(S("mixed"), 1)

        def gmlp_scalar(act):
            win_done(act)
            nc.scalar.activation(z[:, 12:16, :], z[:, 12:16, :], ACT.Gelu_apprx_tanh).then_inc(S("gelu"), 1)
            nc.scalar.activation(z[:, 8:12, :], z[:, 8:12, :], ACT.Gelu_apprx_tanh).then_inc(S("gelu"), 1)
            for n in range(9):
                tn = P if n < 8 else NS
                act.wait_ge(S("gvar"), n + 1)
                nc.scalar.activation(g_stat[0:tn, n % 2, 6:7], g_stat[0:tn, n % 2, 7:8], ACT.Sqrt,
                                     bias=eps_t[0:tn, 1:2]).then_inc(S("gstd"), 1)

        def gmlp_vector(dve):
            dve.wait_ge(S("ln_in"), 96)
            for b in (0, 1):
                dve.wait_ge(S("gwt"), b + 1)
                nc.vector.tensor_tensor(gwT[:, 4 * b:4 * b + 4, :],
                                        bank[6 + b][:, :].rearrange("p (g t) -> p g t", g=4),
                                        cst[:, C_TRI:C_TRI + 1, :].to_broadcast([P, 4, P]), ALU.mult)\
                    .then_inc(S("gwT"), 1)
            dve.wait_ge(S("gelu"), 2)

            def mixed(n):
                dve.wait_ge(S("mixed"), n + 1)
                b = n % 2
                if n < 8:
                    link(nc.vector.tensor_tensor(
                        g_mix[:, b, :], bank[2 + b][:, :], g_bias[:, :, :].rearrange("p k t -> p (k t)"),
                        ALU.add))
                    us = z[:, 8:12, n * P:(n + 1) * P]
                    nc.vector.tensor_tensor(us, g_mix[:, b, :].rearrange("p (k t) -> p k t", k=4), us,
                                            ALU.mult).then_inc(S("gmix"), 1)
                else:
                    gm = g_mix[:, b, 0:4 * NS].rearrange("p (k t) -> p k t", k=4)
                    link(nc.vector.tensor_tensor(
                        gm, bank[2][:, 0:4 * NS].rearrange("p (k t) -> p k t", k=4),
                        g_w00[:, :].unsqueeze(2).to_broadcast([P, 4, NS]), ALU.mult))
                    link(nc.vector.tensor_tensor(
                        gm, gm, g_bias[:, :, 0:1].to_broadcast([P, 4, NS]), ALU.add))
                    us = z[:, 8:12, SEQ:T]
                    nc.vector.tensor_tensor(us, gm, us, ALU.mult).then_inc(S("gmix"), 1)
            for n in range(9):
                tn, b = (P if n < 8 else NS), n % 2
                v = vn[0:tn, b if n < 8 else 2, :]
                dve.wait_ge(S("vtok"), n + 1)
                link(nc.vector.bn_stats(g_stat[0:tn, b, 0:6], bank[b][0:tn, :]))
                link(nc.vector.bn_aggr(g_stat[0:tn, b, 6:8], g_stat[0:tn, b, 0:6]))
                nc.vector.tensor_copy(g_stat[0:tn, b, 0:1], g_stat[0:tn, b, 6:7]).then_inc(S("gvar"), 1)
                dve.wait_ge(S("gstd"), n + 1)
                link(nc.vector.reciprocal(g_stat[0:tn, b, 1:2], g_stat[0:tn, b, 6:7]))
                if 2 <= n < 8:
                    dve.wait_ge(S("mixed"), n - 1)
                nc.vector.tensor_scalar(v, bank[b][0:tn, :], g_stat[0:tn, b, 0:1], g_stat[0:tn, b, 1:2],
                                        ALU.subtract, ALU.mult).then_inc(S("vn0"), 1)
                dve.wait_ge(S("vn0"), n + 1)
                link(nc.vector.tensor_tensor(v, v, ln_gb[0:tn, 0, :], ALU.mult))
                nc.vector.tensor_tensor(v, v, ln_gb[0:tn, 1, :], ALU.add).then_inc(S("vn"), 1)
                if n > 0:
                    mixed(n - 1)
            mixed(8)

        def pw(j):
            return P if j < NBT - 1 else NB - (NBT - 1) * P

        def prep_tensor(pe):
            pe.wait_ge(S("gmix"), 9)
            pe.wait_ge(S("vn0"), 9)
            for j in range(NBT):
                m = nc.tensor.transpose(bank[j // 4][0:NS + 1, (j % 4) * P:(j % 4) * P + pw(j)],
                                        z[0:pw(j), ZB[j], SEQ - 1:T], ident[0:pw(j), 0:pw(j)])
                if j % 4 == 3 or j == NBT - 1:
                    m.then_inc(S("sho"), 1)
            pe.wait_ge(S("prep_in"), 48)
            for j in range(NBT):
                m = nc.tensor.transpose(bank[4][0:pw(j), j * NS:(j + 1) * NS],
                                        shift_in[:, j * P:j * P + pw(j)], ident[0:NS, 0:NS])
            m.then_inc(S("sho"), 1)
            pe.wait_ge(S("prep_in"), 48)
            pe.wait_ge(S("sho_ev"), 5)
            pe.wait_ge(S("shTc"), 2)
            for m in range(24):
                which, ht, t = m // 12, m % 12 // 3, m % 3
                rows = slice(64 * which, 64 * which + 64)
                pe.wait_ge(S("lora_ev"), max(m - 7, 0))
                nc.tensor.matmul(bank[m % 8][:, 0:344], lora_w[rows, ht * P:(ht + 1) * P],
                                 z[rows, 4, tslice(t)], start=True, stop=True).then_inc(S("lora"), 1)
            for m in range(12):
                ht, t = m // 3, m % 3
                pe.wait_ge(S("ksq"), ht + 1)
                pe.wait_ge(S("lora_ev"), min(24, m + 17))
                pe.wait_ge(S("kmax"), max(m - 7, 0))
                nc.tensor.matmul(bank[m % 8][:, 0:344], cst[:, C_BLK, :], diff[:, ht, tslice(t)],
                                 start=True, stop=True).then_inc(S("ksum"), 1)

        def prep_scalar(act):
            for b in range(4):
                act.wait_ge(S("sho"), b + 1)
                wd = 512 if b < 3 else NB - 3 * 512
                nc.scalar.activation(shift_out[:, b * 512:b * 512 + wd], bank[b][0:NS + 1, 0:wd],
                                     ACT.Copy).then_inc(S("sho_ev"), 1)
            act.wait_ge(S("shifted"), NBT)
            nc.scalar.activation(z[0:64, 4, :], z[0:64, 4, :], ACT.Tanh).then_inc(S("sho_ev"), 1)
            for ht in range(4):
                act.wait_ge(S("kk0"), ht + 1)
                nc.scalar.activation(diff[:, ht, :], nkk[:, ht, :], ACT.Square).then_inc(S("ksq"), 1)
            act.wait_ge(S("rwkv_out"), 32)
            for m in range(24):
                which, ht, t = m // 12, m % 12 // 3, m % 3
                act.wait_ge(S("lora"), m + 1)
                dst, b = ((sg, "rwkv_w0"), (bvec, "rwkv_a0"))[which]
                nc.scalar.activation(dst[:, ht, tslice(t)], bank[m % 8][:, 0:344], ACT.Sigmoid,
                                     bias=v_col(b, ht)).then_inc(S("lora_ev"), 1)
            act.wait_ge(S("kmax"), 12)
            nc.scalar.activation(diff[:, 4:8, :], diff[:, 4:8, :], ACT.Ln, scale=float(2 ** 20))\
                .then_inc(S("kln"), 1)
            act.wait_ge(S("kln"), 1)
            nc.scalar.activation(diff[:, 4:8, :], diff[:, 4:8, :], ACT.Exp, scale=-0.5,
                                 bias=eps_t[:, 3:4]).then_inc(S("kln"), 1)

        def prep_vector(dve):
            dve.wait_ge(S("sho"), 5)
            nc.vector.tensor_copy(shiftT[:, 0:NBT - 1, :],
                                  bank[4][:, 0:(NBT - 1) * NS].rearrange("p (k t) -> p k t", t=NS))\
                .then_inc(S("shTc"), 1)
            nc.vector.tensor_copy(shiftT[0:32, NBT - 1, :], bank[4][0:32, (NBT - 1) * NS:NBT * NS])\
                .then_inc(S("shTc"), 1)
            dve.wait_ge(S("shTc"), 2)
            dve.wait_ge(S("sho"), 4)
            dve.wait_ge(S("y_out"), 16)
            done = 0
            for j0, nt, rows in ((0, 8, P), (8, 6, P), (14, 1, 32)):
                z0 = ZB[j0]
                d, zz = diff[0:rows, 0:nt, :], z[0:rows, z0:z0 + nt, :]
                dve.wait_ge(S("shifted"), done)
                link(nc.vector.tensor_tensor(d[:, :, 1:SEQ], zz[:, :, 0:SEQ - 1], zz[:, :, 1:SEQ],
                                             ALU.subtract), False)
                link(nc.vector.tensor_scalar(d[:, :, 0:1], zz[:, :, 0:1], -1.0, None, ALU.mult), False)
                link(nc.vector.tensor_tensor(d[:, :, SEQ:T], shiftT[0:rows, j0:j0 + nt, :],
                                             zz[:, :, SEQ:T], ALU.subtract))
                for j in range(nt):
                    nc.vector.scalar_tensor_tensor(
                        out=z[0:rows, z0 + j, :], in0=diff[0:rows, j, :],
                        scalar=v_col("rwkv_mu", j0 + j)[0:rows], in1=z[0:rows, z0 + j, :],
                        op0=ALU.mult, op1=ALU.add).then_inc(S("shifted"), 1)
                    done += 1
            dve.wait_ge(S("shifted"), done)
            dve.wait_ge(S("out"), 16)
            for ht in range(4):
                nc.vector.tensor_scalar(nkk[:, ht, :], z[:, 20 + ht, :], v_col("rwkv_k_k", ht), None,
                                        ALU.mult).then_inc(S("kk0"), 1)
            dve.wait_ge(S("gwt"), 2)
            link(nc.vector.memset(scan_mask[:, :], 1.0))
            link(nc.vector.memset(scan_mask[:, 0:SEQ:CH], 0.0), False)
            link(nc.vector.memset(scan_mask[:, SEQ:T], 0.0))
            for m in range(12):
                ht, t = m // 3, m % 3
                dve.wait_ge(S("ksum"), m + 1)
                nc.vector.tensor_scalar(diff[:, 4 + ht, tslice(t)], bank[m % 8][:, 0:344], float(HN),
                                        1e-24, ALU.mult, ALU.max).then_inc(S("kmax"), 1)
            dve.wait_ge(S("lora_ev"), 24)
            for ht in range(4):
                link(nc.vector.tensor_tensor_scan(cum[:, ht, :], scan_mask[:, :], sg[:, ht, :], 0.0,
                                                  ALU.mult, ALU.add), False)
                link(nc.vector.tensor_scalar(diff[:, ht, :], bvec[:, ht, :], 1.0,
                                             v_col("rwkv_k_a", ht), ALU.subtract, ALU.mult))
                link(nc.vector.scalar_tensor_tensor(out=z[:, 20 + ht, :], in0=diff[:, ht, :],
                                                    scalar=1.0, in1=z[:, 20 + ht, :], op0=ALU.add,
                                                    op1=ALU.mult), False)
            dve.wait_ge(S("kln"), 2)
            link(nc.vector.scalar_tensor_tensor(out=nkk[:, :, :], in0=nkk[:, :, :], scalar=-1.0,
                                                in1=diff[:, 4:8, :], op0=ALU.mult, op1=ALU.mult))
            link(nc.vector.scalar_tensor_tensor(out=bvec[:, :, :], in0=nkk[:, :, :], scalar=-1.0,
                                                in1=bvec[:, :, :], op0=ALU.mult, op1=ALU.mult))

        NLV = LEVELS - 1

        def part(name, g):
            return mats[g // 2][name][:, 2 * (g % 2):2 * (g % 2) + 2, :]

        def pair(b):
            return bank[b][:, 0:256].rearrange("p (j t) -> p j t", j=2)

        def scale_scalar(act, n):
            c = slice(n * P, (n + 1) * P)
            act.wait_ge(S("ediff"), n + 1)
            nc.scalar.activation(ext[:, :, :], ext[:, :, :], ACT.Exp, scale=-DECAY)\
                .then_inc(S("exps"), 1)
            act.wait_ge(S("decm"), 2 * n)
            act.wait_ge(S("stR"), n)
            nc.scalar.activation(dec[:, :, :], cum[:, :, c], ACT.Exp, scale=-DECAY).then_inc(S("exps"), 1)
            act.wait_ge(S("tok"), 3 * n)
            nc.scalar.activation(vstage[:, :, :], z[:, 0:4, c], ACT.Copy).then_inc(S("vst"), 1)
            act.wait_ge(S("stA"), n + 1)
            nc.scalar.activation(ext[:, :, :], cum[:, :, c], ACT.Exp, scale=DECAY).then_inc(S("exps"), 1)

        def chunk_scalar(act, n):
            c = slice(n * P, (n + 1) * P)
            if n == 0:
                scale_scalar(act, 0)
            act.wait_ge(S("tok"), 3 * n + 3)
            act.wait_ge(S("SN"), 4 * n)
            act.wait_ge(S("O"), 2 * n)
            nc.scalar.activation(Vt[:, :], bank[6][:, :], ACT.Copy).then_inc(S("tokc"), 1)
            for q in (0, 1):
                for b in (0, 1):
                    act.wait_ge(S("pair"), 8 * n + 4 * q + b + 1)
                    if b == 0:
                        act.wait_ge(S("LoT"), max(2 * NLV * n + q - 1, 0))
                        act.wait_ge(S("TT0"), 4 * n)
                    nc.scalar.activation(
                        LQ[q][:, :, b::2, :],
                        bank[4 * q + b][:, :].rearrange("p (j a t) -> p a j t", j=2, a=2),
                        ACT.Copy).then_inc(S("LTc"), 1)
            for lv in range(NLV):
                for g in range(4):
                    act.wait_ge(S("pY"), 4 * (NLV * n + lv) + g + 1)
                    nc.scalar.activation(part("Y", g), pair(2 * g + 1 - lv % 2), ACT.Copy)\
                        .then_inc(S("Yc"), 1)
            if n < 7:
                scale_scalar(act, n + 1)
            for ck in (0, 1):
                r, e0 = slice(64 * ck, 64 * ck + 64), 4 * n + 2 * ck
                for q in (0, 1):
                    cols = slice(q * 256, q * 256 + 256)
                    act.wait_ge(S("X"), e0 + q + 1)
                    nc.scalar.activation(Xs[r, cols], bank[4 * q + 3][r, 0:256], ACT.Copy)\
                        .then_inc(S("Xc"), 1)
                for q in (0, 1):
                    cols = slice(q * 256, q * 256 + 256)
                    act.wait_ge(S("U"), e0 + q + 1)
                    act.wait_ge(S("O"), 2 * n)
                    nc.scalar.activation(Us[r, cols], bank[4 * q][r, 0:256], ACT.Copy)\
                        .then_inc(S("Uc"), 1)
            for q in (0, 1):
                act.wait_ge(S("O"), 2 * n + q + 1)
                nc.scalar.activation(
                    nkk[:, 2 * q:2 * q + 2, c],
                    bank[4 * q + 2][:, 0:256].rearrange("p (k t) -> p k t", k=2),
                    ACT.Copy).then_inc(S("Oc"), 1)

        def chunk_pool(g, n):
            for ck in (0, 1):
                g.wait_ge(S("exps"), 3 * n + 2)
                g.wait_ge(S("Sup1"), 4 * n)
                end = 64 * ck + 63
                nc.gpsimd.tensor_tensor(decm[:, ck], dec[:, :, end:end + 1].to_broadcast([P, 4, P]),
                                        cst[:, C_BLK:C_BLK + 1, :].to_broadcast([P, 4, P]),
                                        ALU.mult).then_inc(S("decm"), 1)
            for lv in range(1, NLV + 1):
                for q in (0, 1):
                    if lv == 1:
                        g.wait_ge(S("LTc"), 4 * n + 2 * q + 2)
                    if lv == 2:
                        nc.gpsimd.tensor_tensor(mats[q]["QBT"], mats[q]["QBT"],
                                                cst[:, C_INC:C_INC + 1, :].to_broadcast([P, 4, P]),
                                                ALU.mult).then_inc(S("QBm"), 1)
                    if NLV * n + lv > 1:
                        g.wait_ge(S("pY"), 4 * (NLV * n + lv - 2) + 2 * q + 2)
                    nc.gpsimd.tensor_tensor(mats[q]["LoT"][:, :, :], mats[q]["LT"][:, :, :],
                                            cst[:, C_LVL + lv:C_LVL + lv + 1, :].to_broadcast([P, 4, P]),
                                            ALU.mult).then_inc(S("LoT"), 1)

        def scale_vector(dve, n):
            c = slice(n * P, (n + 1) * P)
            TT = nc.vector.tensor_tensor
            dve.wait_ge(S("stB"), 2 * n)
            TT(ext[:, :, :], cum[:, :, c], sg[:, :, c], ALU.subtract).then_inc(S("ediff"), 1)
            dve.wait_ge(S("exps"), 3 * n + 1)
            dve.wait_ge(S("pair"), 8 * n)
            dve.wait_ge(S("tok"), 3 * n)
            dve.wait_ge(S("O"), max(2 * n - 2, 0))
            TT(AR[n % 2][:, 0, :, :], nkk[:, :, c], ext[:, :, :], ALU.mult).then_inc(S("stA"), 1)
            dve.wait_ge(S("exps"), 3 * n + 2)
            TT(AR[n % 2][:, 1, :, :], z[:, 16:20, c], dec[:, :, :], ALU.mult).then_inc(S("stR"), 1)
            dve.wait_ge(S("exps"), 3 * n + 3)
            TT(BK[:, 0, :, :], bvec[:, :, c], ext[:, :, :], ALU.mult).then_inc(S("stB"), 1)
            TT(BK[:, 1, :, :], z[:, 20:24, c], ext[:, :, :], ALU.mult).then_inc(S("stB"), 1)

        def chunk_vector(dve, n):
            TT = nc.vector.tensor_tensor
            if n == 0:
                scale_vector(dve, 0)
            for j, dst in enumerate((Bt, Kt)):
                dve.wait_ge(S("tok"), 3 * n + j + 1)
                dve.wait_ge(S("SN"), 4 * n)
                nc.vector.tensor_copy(dst[:, :], bank[4 + j][:, :]).then_inc(S("tokc"), 1)

            def pv(b, a):
                return bank[b][:, :].rearrange("p (j a t) -> p j a t", j=2, a=2)[:, :, a, :]
            for q in (0, 1):
                m = mats[q]
                msk = lambda k: cst[:, k:k + 1, :].to_broadcast([P, 2, P])
                for b in (0, 1):
                    hs = slice(b, 4, 2)
                    dve.wait_ge(S("LTc"), 4 * n + 2 * q + b + 1)
                    if b == 0:
                        dve.wait_ge(S("U"), 4 * n)
                        dve.wait_ge(S("X"), 4 * n)
                        dve.wait_ge(S("TTa"), 4 * NLV * n)
                    TT(m["TT"][:, hs, :], m["LT"][:, hs, :], msk(C_LVL), ALU.mult)\
                        .then_inc(S("TT0"), 1)
                    dve.wait_ge(S("TT0"), 4 * n + 2 * q + b + 1)
                    TT(m["TT"][:, hs, :], m["TT"][:, hs, :], msk(C_ID), ALU.add).then_inc(S("TT1"), 1)
                for b in (0, 1):
                    hs = slice(b, 4, 2)
                    dve.wait_ge(S("pair"), 8 * n + 4 * q + 2 + b + 1)
                    TT(m["MT"][:, hs, :], pv(4 * q + 2 + b, 0), msk(C_STR), ALU.mult)\
                        .then_inc(S("pKr"), 1)
                    TT(m["QKT"][:, hs, :], pv(4 * q + 2 + b, 1), msk(C_INC), ALU.mult)\
                        .then_inc(S("pKr"), 1)
            for lv in range(NLV):
                for g in range(4):
                    dve.wait_ge(S("Tt"), 4 * (NLV * n + lv) + g + 1)
                    nc.vector.tensor_copy(part("Ti", g), pair(2 * g + lv % 2)).then_inc(S("Tc"), 1)
                for g in range(4):
                    dve.wait_ge(S("pD"), 4 * (NLV * n + lv) + g + 1)
                    TT(part("TT", g), part("TT", g), pair(2 * g + lv % 2), ALU.add)\
                        .then_inc(S("TTa"), 1)
            if n < 7:
                scale_vector(dve, n + 1)
            for ck in (0, 1):
                e0 = 4 * n + 2 * ck
                for q in (0, 1):
                    hs = slice(2 * q, 2 * q + 2)
                    dve.wait_ge(S("SN"), e0 + q + 1)
                    dve.wait_ge(S("Sup1"), max(e0 + q - 1, 0))
                    dve.wait_ge(S("O"), 2 * n)
                    TT(st_T[:, (2 * n + ck + 1) % 3, hs, :], st_T[:, (2 * n + ck) % 3, hs, :],
                       bank[4 * q + 1][:, 0:256].rearrange("p (k v) -> p k v", k=2), ALU.add)\
                        .then_inc(S("Sup0"), 1)
                for q in (0, 1):
                    hs = slice(2 * q, 2 * q + 2)
                    new = st_T[:, (2 * n + ck + 1) % 3, hs, :]
                    dve.wait_ge(S("Sup0"), e0 + q + 1)
                    dve.wait_ge(S("decm"), 2 * n + ck + 1)
                    nc.vector.scalar_tensor_tensor(out=new, in0=new, scalar=float(HN),
                                                   in1=decm[:, ck, hs, :], op0=ALU.mult,
                                                   op1=ALU.mult).then_inc(S("Sup1"), 1)

        def chunk_tensor(pe, n):
            mmul = nc.tensor.matmul
            heads = lambda q: [(j, (4 * q + j) // 2, (4 * q + j) % 2) for j in range(4)]
            pe.wait_ge(S("stB"), 2 * n + 2)
            pe.wait_ge(S("Oc"), 2 * n)
            pe.wait_ge(S("Sup0"), 4 * n)
            for j, src in enumerate((BK[:, 0], BK[:, 1], vstage[:, :, :])):
                if j == 2:
                    pe.wait_ge(S("vst"), n + 1)
                for ht in range(4):
                    m = nc.tensor.transpose(bank[4 + j][:, ht * P:(ht + 1) * P], src[:, ht, :], ident)
                m.then_inc(S("tok"), 1)
            for q in (0, 1):
                if q == 1:
                    pe.wait_ge(S("tokc"), 3 * n + 3)
                for side in (0, 1):
                    for j, ht, hp in sorted(heads(q), key=lambda x: x[2]):
                        r = slice(64 * hp, 64 * hp + 64)
                        m = mmul(bank[4 * q + 2 * side + hp][:, (j // 2) * 256:(j // 2) * 256 + 256],
                                 BK[r, side, ht, :], AR[n % 2][r, :, ht, :], start=True, stop=True)
                        if j >= 2:
                            m.then_inc(S("pair"), 1)
            for lv in range(NLV):
                for g in range(4):
                    q = g // 2
                    if lv == 0:
                        pe.wait_ge(S("TT1"), 4 * n + 2 * q + 2)
                        pe.wait_ge(S("pKr"), 8 * n + 4 * q + 4)
                        pe.wait_ge(S("LTc"), 4 * n + 2 * q + 2)
                    else:
                        pe.wait_ge(S("TTa"), 4 * (NLV * n + lv - 1) + g + 1)
                    for j in (0, 1):
                        m = nc.tensor.transpose(bank[2 * g + lv % 2][:, j * P:(j + 1) * P],
                                                part("TT", g)[:, j, :], ident)
                    m.then_inc(S("Tt"), 1)
                for g in range(4):
                    pe.wait_ge(S("LoT"), 2 * (NLV * n + lv) + g // 2 + 1)
                    pe.wait_ge(S("Tc"), 4 * (NLV * n + lv) + g + 1)
                    for j in (0, 1):
                        m = mmul(bank[2 * g + 1 - lv % 2][:, j * P:(j + 1) * P],
                                 part("LoT", g)[:, j, :], part("Ti", g)[:, j, :], start=True, stop=True)
                    m.then_inc(S("pY"), 1)
                for g in range(4):
                    pe.wait_ge(S("Yc"), 4 * (NLV * n + lv) + g + 1)
                    for j in (0, 1):
                        m = mmul(bank[2 * g + lv % 2][:, j * P:(j + 1) * P],
                                 part("Y", g)[:, j, :], part("TT", g)[:, j, :], start=True, stop=True)
                    m.then_inc(S("pD"), 1)
            pe.wait_ge(S("TTa"), 4 * NLV * (n + 1))

            def out_v(q):
                pe.wait_ge(S("Oc"), max(2 * n + q - 1, 0))
                for j, ht, hp in heads(q):
                    hc = slice((4 * q + j) * 64, (4 * q + j + 1) * 64)
                    mmul(bank[4 * q + 2][64 * hp:64 * hp + 64, (j // 2) * P:(j // 2 + 1) * P],
                         Vt[:, hc], mats[q]["QKT"][:, j, :], start=j < 2, stop=False,
                         skip_group_check=True)

            def out_u(q):
                pe.wait_ge(S("QBm"), 2 * n + q + 1)
                for j, ht, hp in heads(q):
                    hc = slice((4 * q + j) * 64, (4 * q + j + 1) * 64)
                    mmul(bank[4 * q + 2][64 * hp:64 * hp + 64, (j // 2) * P:(j // 2 + 1) * P],
                         Us[:, hc], mats[q]["QBT"][:, j, :], start=False, stop=False,
                         skip_group_check=True)

            def out_state(q, ck):
                for k in (0, 1):
                    m = mmul(bank[4 * q + 2][:, k * P + 64 * ck:k * P + 64 * ck + 64],
                             st_T[:, (2 * n + ck) % 3, 2 * q + k, :],
                             AR[n % 2][:, 1, 2 * q + k, 64 * ck:64 * ck + 64],
                             start=False, stop=ck == 1, skip_group_check=True)
                return m
            for ck in (0, 1):
                t, e0 = slice(64 * ck, 64 * ck + 64), 4 * n + 2 * ck
                for q in (0, 1):
                    pe.wait_ge(S("Sup1"), max(e0 + q - 1, 0))
                    pe.wait_ge(S("Xc"), max(e0 - 1 + q, 0))
                    if n == 0 and ck == 0:
                        pe.wait_ge(S("st0"), 2)
                    for k in (0, 1):
                        ht = 2 * q + k
                        mmul(bank[4 * q + 3][t, k * P:(k + 1) * P], AR[n % 2][:, 0, ht, t],
                             st_T[:, (2 * n + ck) % 3, ht, :], start=True, stop=False)
                        for hp in (0, 1):
                            j = 2 * k + hp
                            hc = slice((2 * ht + hp) * 64, (2 * ht + hp + 1) * 64)
                            m = mmul(bank[4 * q + 3][t, j * 64:(j + 1) * 64], mats[q]["MT"][:, j, t],
                                     Vt[:, hc], start=False, stop=hp == 1)
                    m.then_inc(S("X"), 1)
                if ck == 0:
                    out_v(0)
                for q in (0, 1):
                    pe.wait_ge(S("Xc"), e0 + q + 1)
                    pe.wait_ge(S("Uc"), max(e0 + q - 1, 0))
                    for j, ht, hp in heads(q):
                        hc = slice((4 * q + j) * 64, (4 * q + j + 1) * 64)
                        m = mmul(bank[4 * q][t, j * 64:(j + 1) * 64], mats[q]["TT"][t, j, t], Xs[t, hc],
                                 start=True, stop=True)
                    m.then_inc(S("U"), 1)
                if ck == 0:
                    out_v(1)
                for q in (0, 1):
                    pe.wait_ge(S("Uc"), e0 + q + 1)
                    pe.wait_ge(S("Sup0"), max(e0 + q - 1, 0))
                    for k in (0, 1):
                        hc = slice((2 * q + k) * P, (2 * q + k + 1) * P)
                        o = bank[4 * q + 1][:, k * P:(k + 1) * P]
                        mmul(o, Kt[t, hc], Vt[t, hc], start=True, stop=False)
                        m = mmul(o, Bt[t, hc], Us[t, hc], start=False, stop=True)
                    m.then_inc(S("SN"), 1)
                if ck == 0:
                    for q in (0, 1):
                        out_state(q, 0)
            for q in (0, 1):
                out_u(q)
                out_state(q, 1).then_inc(S("O"), 1)

        SMP = [lambda ht: smp_w[:, ht, :], lambda ht: nkk[:, ht, SEQ:T], lambda ht: bvec[:, ht, SEQ:T],
               lambda ht: z[:, 20 + ht, SEQ:T], lambda ht: z[:, 16 + ht, SEQ:T],
               lambda ht: z[:, ht, SEQ:T]]

        def sample_loads(sp):
            sp.wait_ge(S("Oc"), 16)
            sp.dma_start(smp_S[:, :, :], A["state_rwkv"][0].rearrange("b h (w v) k -> (b h w) v k", w=2))\
                .then_inc(S("post_in"), 16)
            sp.wait_ge(S("decm"), 16)
            sp.dma_start(g2_w[:, 0, :], A["rwkv_g2"][0][0:P, :]).then_inc(S("post_in"), 16)
            sp.dma_start(g2_w[0:32, 1, :], A["rwkv_g2"][0][P:P + 32, :]).then_inc(S("post_in"), 16)
            sp.wait_ge(S("smp_a"), 8)
            sp.dma_start(smp_d.rearrange("i b n -> b i n"), smp_n[:, :, :]).then_inc(S("smp_in"), 16)
            sp.wait_ge(S("smp_in"), 16)
            for w in (0, 1):
                sp.dma_start(smp_v[w::2, 0:5, :], smp_d[0:5].rearrange("i b (h d) -> (b h) i d", h=HEADS))\
                    .then_inc(S("smp_in"), 16)
            sp.dma_start(smp_v[:, 5, 0:32], smp_d[5].rearrange("b (h d) -> (b h) d", d=32))\
                .then_inc(S("smp_in"), 16)
            sp.wait_ge(S("smp_a"), 2)
            for hp in (0, 1):
                r = slice(64 * hp, 64 * hp + 64)
                sp.dma_start(O["state_rwkv_prompt"][0, 0, hp::2].rearrange("h v k -> v h k"),
                             st_out[r, :, r]).then_inc(S("rwkv_out"), 16)
            sp.wait_ge(S("smp_v"), 1)
            sp.dma_start(smp_od.rearrange("b (h d) -> (b h) d", d=32), smp_o[:, 1, :])\
                .then_inc(S("smp_in"), 16)
            sp.dma_start(O["state_rwkv_sample"][0].rearrange("b h (w v) k -> (b h w) v k", w=2),
                         smp_S[:, :, :]).then_inc(S("rwkv_out"), 16)
            sp.wait_ge(S("smp_in"), 80)
            sp.dma_start(smp_on[:, :], smp_od).then_inc(S("smp_in"), 16)
            sp.wait_ge(S("smp_t"), 7)
            sp.dma_start(ya_in[:, :, :], y_save).then_inc(S("ya_in"), 16)
            sp.wait_ge(S("yb"), 12)
            sp.dma_start(x[:, :, :], x_save).then_inc(S("x_back"), 16)

        def post_scalar(act):
            act.wait_ge(S("Oc"), 16)
            nc.scalar.activation(smp_w[:, :, :], sg[:, :, SEQ:T], ACT.Exp, scale=-DECAY)\
                .then_inc(S("smp_a"), 1)
            act.wait_ge(S("smp_t"), 1)
            nc.scalar.activation(st_out[:, :, :], bank[6][:, :].rearrange("p (k n) -> p k n", k=4),
                                 ACT.Copy).then_inc(S("smp_a"), 1)
            for i in range(6):
                act.wait_ge(S("smp_t"), i + 2)
                nc.scalar.activation(smp_n[:, i, :], bank[i][0:NS, :], ACT.Copy).then_inc(S("smp_a"), 1)
            nc.scalar.activation(z[:, 5, :], z[:, 5, :], ACT.Sigmoid).then_inc(S("smp_a"), 1)
            nc.scalar.activation(z[0:32, 6, :], z[0:32, 6, :], ACT.Sigmoid).then_inc(S("smp_a"), 1)
            for m in range(13):
                if m < 12:
                    ht, t = m // 3, m % 3
                    act.wait_ge(S("gn_c"), m + 1)
                    act.wait_ge(S("gn_v"), max(m - 2, 0))
                    nc.scalar.activation(gn_sq[:, m % 3, :], nkk[:, ht, tslice(t)], ACT.Square)\
                        .then_inc(S("gn_q"), 1)
                if m > 0:
                    ht, t = (m - 1) // 3, (m - 1) % 3
                    act.wait_ge(S("gn_v"), m)
                    nc.scalar.activation(sg[:, ht, tslice(t)], bank[2 + (m - 1) % 2][:, 0:344], ACT.Ln,
                                         bias=eps_t[:, 2:3]).then_inc(S("gn_l"), 1)
            act.wait_ge(S("gn_l"), 12)
            nc.scalar.activation(sg[:, :, :], sg[:, :, :], ACT.Exp, scale=-0.5).then_inc(S("gn_l"), 1)
            act.wait_ge(S("ya_in"), 16)
            act.wait_ge(S("rwkv_out"), 80)
            nc.scalar.activation(y_hi[:, 0:4, :], ya_in[:, :, :], ACT.Copy).then_inc(S("yb_hi"), 1)
            for m in range(12):
                ht, t = m // 3, m % 3
                act.wait_ge(S("yb"), m + 1)
                nc.scalar.activation(y_hi[:, 4 + ht, tslice(t)], nkk[:, ht, tslice(t)], ACT.Copy)\
                    .then_inc(S("yb_hi"), 1)

        def post_tensor(pe):
            pe.wait_ge(S("Sup1"), 32)
            pe.wait_ge(S("Oc"), 16)
            for ht in range(4):
                m = nc.tensor.transpose(bank[6][:, ht * P:(ht + 1) * P], st_T[:, 16 % 3, ht, :], ident)
            m.then_inc(S("smp_t"), 1)
            pe.wait_ge(S("smp_a"), 1)
            for i in range(6):
                for ht in range(4):
                    m = nc.tensor.transpose(bank[i][0:NS, ht * P:(ht + 1) * P], SMP[i](ht), ident)
                m.then_inc(S("smp_t"), 1)
            pe.wait_ge(S("smp_in"), 96)
            pe.wait_ge(S("smp_a"), 8)
            for ht in range(4):
                m = nc.tensor.transpose(bank[7][:, ht * NS:(ht + 1) * NS],
                                        smp_on[:, ht * P:(ht + 1) * P], ident[0:NS, 0:NS])
            m.then_inc(S("smp_t"), 1)
            blk = cst[:, C_BLK, :]
            pe.wait_ge(S("smp_v"), 2)
            for m in range(13):
                if m < 12:
                    ht, t = m // 3, m % 3
                    pe.wait_ge(S("gn_c"), max(m - 1, 0))
                    nc.tensor.matmul(bank[m % 2][:, 0:344], blk, nkk[:, ht, tslice(t)],
                                     start=True, stop=True).then_inc(S("gn_m"), 1)
                if m > 0:
                    ht, t = (m - 1) // 3, (m - 1) % 3
                    pe.wait_ge(S("gn_q"), m)
                    pe.wait_ge(S("gn_l"), max(m - 2, 0))
                    nc.tensor.matmul(bank[2 + (m - 1) % 2][:, 0:344], blk, gn_sq[:, (m - 1) % 3, :],
                                     start=True, stop=True).then_inc(S("gn_v"), 1)
            pe.wait_ge(S("smp_a"), 10)
            pe.wait_ge(S("post_in"), 48)
            pe.wait_ge(S("smp_a"), 2)
            for m in range(12):
                ht, t = m // 3, m % 3
                pe.wait_ge(S("bo0"), ht + 1)
                pe.wait_ge(S("bo2"), max(m - 1, 0))
                nc.tensor.matmul(bank[4 + m % 2][:, 0:344], blk, cum[:, ht, tslice(t)],
                                 start=True, stop=True).then_inc(S("bo1"), 1)
                pe.wait_ge(S("yb"), max(m - 1, 0))
                nc.tensor.matmul(bank[6 + m % 2][:, 0:344], g2_w[:, 0, ht * P:(ht + 1) * P],
                                 z[:, 5, tslice(t)], start=True, stop=False)
                nc.tensor.matmul(bank[6 + m % 2][:, 0:344], g2_w[0:32, 1, ht * P:(ht + 1) * P],
                                 z[0:32, 6, tslice(t)], start=False, stop=True).then_inc(S("g2"), 1)

        def post_vector(dve):
            TT, STT = nc.vector.tensor_tensor, nc.vector.scalar_tensor_tensor
            for ht in range(4):
                STT(out=cum[:, ht, :], in0=z[:, 16 + ht, :], scalar=v_col("rwkv_r_k", ht),
                    in1=z[:, 20 + ht, :], op0=ALU.mult, op1=ALU.mult).then_inc(S("bo0"), 1)
            dve.wait_ge(S("post_in"), 48)
            dve.wait_ge(S("smp_in"), 64)
            full = [P, 32, HN]
            over_v = lambda i: smp_v[:, i:i + 1, :].to_broadcast(full)
            over_k = lambda a: a.unsqueeze(2).to_broadcast(full)
            link(TT(smp_t[:, :, :], smp_S[:, :, :], over_v(1), ALU.mult))
            link(nc.vector.tensor_reduce(smp_o[:, 0, :], smp_t[:, :, :], AX.X, ALU.add), False)
            link(TT(smp_S[:, :, :], smp_S[:, :, :], over_v(0), ALU.mult))
            link(TT(smp_t[:, :, :], over_k(smp_o[:, 0, :]), over_v(2), ALU.mult))
            link(TT(smp_S[:, :, :], smp_S[:, :, :], smp_t[:, :, :], ALU.add))
            link(TT(smp_t[:, :, :], over_k(smp_v[:, 5, 0:32]), over_v(3), ALU.mult))
            link(TT(smp_S[:, :, :], smp_S[:, :, :], smp_t[:, :, :], ALU.add))
            link(TT(smp_t[:, :, :], smp_S[:, :, :], over_v(4), ALU.mult))
            nc.vector.tensor_reduce(smp_o[:, 1, :], smp_t[:, :, :], AX.X, ALU.add)\
                .then_inc(S("smp_v"), 1)
            dve.wait_ge(S("smp_t"), 8)
            nc.vector.tensor_copy(nkk[:, :, SEQ:T], bank[7][:, 0:4 * NS].rearrange(
                "p (k t) -> p k t", k=4)).then_inc(S("smp_v"), 1)
            dve.wait_ge(S("smp_v"), 2)
            for m in range(12):
                ht, t = m // 3, m % 3
                dve.wait_ge(S("gn_m"), m + 1)
                TT(nkk[:, ht, tslice(t)], nkk[:, ht, tslice(t)], bank[m % 2][:, 0:344], ALU.subtract)\
                    .then_inc(S("gn_c"), 1)
            dve.wait_ge(S("gn_l"), 13)
            for ht in range(4):
                link(STT(out=nkk[:, ht, :], in0=nkk[:, ht, :], scalar=v_col("rwkv_gn_g", ht),
                         in1=sg[:, ht, :], op0=ALU.mult, op1=ALU.mult))
            dve.wait_ge(S("yb_hi"), 1)
            TT(y_lo[:, 0:4, :], ya_in[:, :, :], y_hi[:, 0:4, :].bitcast(F), ALU.subtract)\
                .then_inc(S("ya_lo"), 1)
            for m in range(12):
                ht, t = m // 3, m % 3
                o = nkk[:, ht, tslice(t)]
                dve.wait_ge(S("bo1"), m + 1)
                STT(out=cum[:, ht, tslice(t)], in0=bank[4 + m % 2][:, 0:344], scalar=float(HN),
                    in1=z[:, ht, tslice(t)], op0=ALU.mult, op1=ALU.mult).then_inc(S("bo2"), 1)
                dve.wait_ge(S("bo2"), m + 1)
                link(STT(out=o, in0=o, scalar=v_col("rwkv_gn_b", ht), in1=cum[:, ht, tslice(t)],
                         op0=ALU.add, op1=ALU.add))
                dve.wait_ge(S("g2"), m + 1)
                TT(o, o, bank[6 + m % 2][:, 0:344], ALU.mult).then_inc(S("yb"), 1)
                dve.wait_ge(S("yb_hi"), m + 2)
                TT(y_lo[:, 4 + ht, tslice(t)], o, y_hi[:, 4 + ht, tslice(t)].bitcast(F), ALU.subtract)\
                    .then_inc(S("yb_lo"), 1)

        def mem_loads(sp):
            sp.wait_ge(S("yb_lo"), 12)
            sp.dma_start(mem_n[:, :, :], A["mem_prompt"][0].rearrange("(m p) d -> p m d", p=P))\
                .then_inc(S("mem_in"), 16)

        def mem_scalar_a(act):
            act.wait_ge(S("mem_in"), 16)
            for m in (0, 1):
                act.wait_ge(S("msq"), m)
                nc.scalar.activation(mem_sq[:, :], mem_n[:, m, :], ACT.Square,
                                     accum_out=mem_st[:, m, 0:1]).then_inc(S("msq"), 1)
            act.wait_ge(S("msq"), 2)
            nc.scalar.activation(mem_st[:, :, 1:2], mem_st[:, :, 0:1], ACT.Sqrt, scale=1.0 / D,
                                 bias=eps_t[:, 0:1]).then_inc(S("msq"), 1)

        def mem_vector_a(dve):
            dve.wait_ge(S("msq"), 3)
            link(nc.vector.reciprocal(mem_st[:, :, 2:3], mem_st[:, :, 1:2]))
            for m in (0, 1):
                nc.vector.tensor_scalar(mem_n[:, m, :], mem_n[:, m, :], mem_st[:, m, 2:3], None,
                                        ALU.mult).then_inc(S("mnorm"), 1)

        def mem_tensor_a(pe):
            pe.wait_ge(S("mnorm"), 2)
            for j in (0, 1):
                pe.wait_ge(evac[j], memk["mm0"][j])
            for k in range(KD):
                for m in (0, 1):
                    i = nc.tensor.transpose(bank[k // 2][:, (k % 2) * 256 + m * P:(k % 2) * 256 + (m + 1) * P],
                                            mem_n[:, m, k * P:(k + 1) * P], ident)
                if k % 2:
                    i.then_inc(S("memT"), 1)

        def mem_scalar_b(act):
            for k in range(KD):
                act.wait_ge(S("memT"), k // 2 + 1)
                if k % 2:
                    act.wait_ge(S("mem_lo"), k)
                nc.scalar.activation(mem_hi[:, k, :], bank[k // 2][:, (k % 2) * 256:(k % 2) * 256 + 256],
                                     ACT.Copy, scale=v_col("mem_norm", k)).then_inc(S("mem_hi"), 1)

        def mem_vector_b(dve):
            for k in range(KD):
                dve.wait_ge(S("mem_hi"), k + 1)
                nc.vector.scalar_tensor_tensor(
                    out=mem_lo[:, k, :], in0=bank[k // 2][:, (k % 2) * 256:(k % 2) * 256 + 256],
                    scalar=v_col("mem_norm", k), in1=mem_hi[:, k, :].bitcast(F),
                    op0=ALU.mult, op1=ALU.subtract).then_inc(S("mem_lo"), 1)

        def plain_evac(eng, is_act, ph, dst):
            def one(i, s, st, t, count):
                if (s == 0) != is_act:
                    return
                t0, tn = ph["toks"][t]
                eng.wait_ge(mm[st], count)
                o = dst[:, ds(2 * i + s, 1), t0:t0 + tn]
                src = bank[3 * st + t][:, 0:tn].rearrange("p (a n) -> p a n", a=1)
                if is_act:
                    nc.scalar.activation(o, src, ACT.Copy).then_inc(evac[st], 1)
                else:
                    nc.vector.tensor_copy(o, src).then_inc(evac[st], 1)
            each_tile(eng, ph, one)

        def nat_tensor(pe):
            for j in (0, 1):
                pe.wait_ge(evac[j], memv["mm1"][j])
            for m in (0, 1):
                pe.wait_ge(S("nat_a"), 2 * m)
                pe.wait_ge(S("nat_b"), 2 * m)
                for g, src in ((0, kT), (2, vT)):
                    for k in range(KD):
                        i = nc.tensor.transpose(bank[g + k // 4][:, (k % 4) * P:(k % 4 + 1) * P],
                                                src[:, k, m * P:(m + 1) * P], ident)
                        if k % 4 == 3:
                            i.then_inc(S("nat"), 1)

        def nat_scalar(act):
            for m in (0, 1):
                for b in (0, 1):
                    act.wait_ge(S("nat"), 4 * m + b + 1)
                    nc.scalar.activation(mk_n[:, m, b * 512:b * 512 + 512], bank[b][:, :], ACT.Copy)\
                        .then_inc(S("nat_a"), 1)

        def nat_vector(dve):
            for m in (0, 1):
                for b in (0, 1):
                    dve.wait_ge(S("nat"), 4 * m + 2 + b + 1)
                    nc.vector.tensor_copy(v_n[:, m, b * 512:b * 512 + 512], bank[2 + b][:, :])\
                        .then_inc(S("nat_b"), 1)

        def nat_out(sp):
            sp.wait_ge(S("nat_a"), 4)
            sp.dma_start(O["mem_k_prompt"][0, 0].rearrange("(m p) h d -> p m (h d)", p=P), mk_n[:, :, :])\
                .then_inc(S("out3"), 16)
            sp.wait_ge(S("nat_b"), 4)
            sp.dma_start(O["mem_v_prompt"][0, 0].rearrange("(m p) h d -> p m (h d)", p=P), v_n[:, :, :])\
                .then_inc(S("out3"), 16)

        SC = float(XD) ** -0.5
        cache_in = [S("cache_in0"), S("cache_in1")]

        def cache_loads(sp, name, n):
            if n < 2:
                sp.wait_ge(S("out3"), 32) if name == "k" else sp.wait_ge(S("s_dot"), 8 * (7 + n))
            else:
                sp.wait_ge(S("s_dot") if name == "k" else S("o_smp"), (8 if name == "k" else 1) * (n - 1))
            sp.dma_start(cache[n % 2][:, :, :],
                         A[f"cache_mem_{name}"][0, n].rearrange("(m p) h d -> p m (h d)", p=P))\
                .then_inc(cache_in[n % 2], 16)

        def att_scores_pe(pe, n):
            c = slice(n * P, (n + 1) * P)
            pe.wait_ge(S("exp"), 4 * n)
            for h in range(XH):
                for d in (0, 1):
                    m = nc.tensor.matmul(bank[h // 2][:, (h % 2) * 256:(h % 2) * 256 + 256],
                                         qT[:, 2 * h + d, c], kT[:, 2 * h + d, :],
                                         start=d == 0, stop=d == 1)
                if h % 2:
                    m.then_inc(S("score"), 1)

        def att_query_pe(pe, n):
            pe.wait_ge(S("s_dot"), 8 * n)
            for k in range(KD):
                m = nc.tensor.matmul(bank[6 + k // 4][:, (k % 4) * P:(k % 4 + 1) * P],
                                     qT[:, k, SEQ + n:SEQ + n + 1].to_broadcast([P, P]), ident,
                                     start=True, stop=True)
            m.then_inc(S("q_bc"), 1)

        def att_out_pe(pe, n):
            b = n % 2
            pe.wait_ge(S("pnorm"), n + 1)
            pe.wait_ge(S("pT"), 2 * n)
            for h in range(XH):
                for m in (0, 1):
                    i = nc.tensor.transpose(bank[2 + h // 2][:, (h % 2) * 256 + m * P:(h % 2) * 256 + (m + 1) * P],
                                            prob[b][:, h, m * P:(m + 1) * P], ident)
                if h % 2:
                    i.then_inc(S("pTt"), 1)
            pe.wait_ge(S("o_lo"), 2 * n)
            for g in (0, 1):
                pe.wait_ge(S("pT"), 2 * n + g + 1)
                for h in (2 * g, 2 * g + 1):
                    for d in (0, 1):
                        for m in (0, 1):
                            i = nc.tensor.matmul(bank[4 + g][:, ((h % 2) * 2 + d) * P:((h % 2) * 2 + d + 1) * P],
                                                 v_n[:, m, h * XD + d * P:h * XD + (d + 1) * P],
                                                 probT[b][:, 2 * h + m, :], start=m == 0, stop=m == 1)
                i.then_inc(S("pv"), 1)

        def att_tensor(pe):
            for j in (0, 1):
                pe.wait_ge(evac[j], xaq["mm1"][j])
            for n in range(9):
                if n < 8:
                    att_scores_pe(pe, n)
                if n < 4:
                    att_query_pe(pe, 2 * n)
                if n == 4:
                    pe.wait_ge(S("s_dot"), 64)
                    for m in (0, 1):
                        i = nc.tensor.transpose(bank[6][0:32, m * P:(m + 1) * P], s_smp[:, :, m], ident)
                    i.then_inc(S("srow"), 1)
                if n:
                    att_out_pe(pe, n - 1)
                if n < 4:
                    att_query_pe(pe, 2 * n + 1)
                if n == 4:
                    pe.wait_ge(S("srow_v"), 2)
                    for m in (0, 1):
                        i = nc.tensor.transpose(bank[7][:, m * 32:(m + 1) * 32],
                                                p_smp[:, m * P:(m + 1) * P], ident[0:32, 0:32])
                    i.then_inc(S("srow"), 1)
                for b in (2 * n - 10, 2 * n - 9) if n > 4 else ():
                    pe.wait_ge(S("srow_v"), 4)
                    pe.wait_ge(cache_in[b % 2], 64 + 16 * (b // 2 + 1))
                    for h in range(XH):
                        for m in (0, 1):
                            i = nc.tensor.matmul(
                                bank[6 + h // 2][0:NS, (h % 2) * XD:(h % 2 + 1) * XD],
                                pT_smp[m].rearrange("p b x -> p (b x)")[
                                    :, 32 * b + 8 * h:32 * b + 8 * h + NS], cache[b % 2][:, m, h * XD:(h + 1) * XD],
                                start=b == 0 and m == 0 and h % 2 == 0, stop=b == NS - 1 and m == 1,
                                skip_group_check=True)
                    i.then_inc(S("o_smp"), 1)
            pe.wait_ge(S("o_rows"), 2)
            pe.wait_ge(S("o_hi"), 16)
            pe.wait_ge(S("exp"), 32)
            for k in range(KD):
                i = nc.tensor.transpose(bank[0][:, k * NS:(k + 1) * NS], o_rows[:, k * P:(k + 1) * P],
                                        ident[0:NS, 0:NS])
            i.then_inc(S("srow"), 1)

        def att_scalar(act):
            for n in range(9):
                if n < 8:
                    b = n % 2
                    act.wait_ge(S("nmax"), n + 1)
                    act.wait_ge(S("pTt"), 2 * max(n - 1, 0))
                    act.wait_ge(S("pnorm"), max(n - 1, 0))
                    for h in range(XH):
                        nc.scalar.activation(prob[b][:, h, :], bank[h // 2][:, (h % 2) * 256:(h % 2) * 256 + 256],
                                             ACT.Exp, scale=SC, bias=att[:, b, 0, h:h + 1],
                                             accum_out=att[:, b, 1, h:h + 1]).then_inc(S("exp"), 1)
                if n == 4:
                    act.wait_ge(S("srow_v"), 1)
                    nc.scalar.activation(p_smp[:, :], bank[6][0:32, 0:NMEM], ACT.Exp, scale=SC,
                                         bias=s_row[:, 0:1], accum_out=s_row[:, 1:2])\
                        .then_inc(S("srow_e"), 1)
                if n:
                    m = n - 1
                    c = slice(m * P, (m + 1) * P)
                    for g in (0, 1):
                        act.wait_ge(S("pTt"), 2 * m + g + 1)
                        act.wait_ge(S("pv"), 2 * max(m - 1, 0))
                        nc.scalar.activation(probT[m % 2][:, 4 * g:4 * g + 4, :],
                                             bank[2 + g][:, :].rearrange("p (k t) -> p k t", k=4),
                                             ACT.Copy).then_inc(S("pT"), 1)
                    for g in (0, 1):
                        act.wait_ge(S("pv"), 2 * m + g + 1)
                        nc.scalar.activation(o_hi[:, 4 * g:4 * g + 4, c],
                                             bank[4 + g][:, :].rearrange("p (k t) -> p k t", k=4),
                                             ACT.Copy).then_inc(S("o_hi"), 1)
            act.wait_ge(S("o_smp"), 8)
            nc.scalar.activation(o_rows[:, 0:512], bank[6][0:NS, :], ACT.Copy).then_inc(S("o_rows"), 1)
            act.wait_ge(S("srow"), 3)
            nc.scalar.activation(o_hi[:, :, SEQ:T], bank[0][:, 0:64].rearrange("p (k b) -> p k b", k=KD),
                                 ACT.Copy).then_inc(S("o_hi"), 1)

        def att_vector(dve):
            def dots(n):
                b = n % 2
                dve.wait_ge(S("q_bc"), n + 1)
                dve.wait_ge(cache_in[b], 16 * (n // 2 + 1))
                for m in (0, 1):
                    for h in range(XH):
                        dve.wait_ge(S("s_dot"), 8 * n + 4 * m + h)
                        nc.vector.scalar_tensor_tensor(
                            out=s_junk[:, :], in0=cache[b][:, m, h * XD:(h + 1) * XD], scalar=1.0,
                            in1=bank[6 + h // 2][:, (h % 2) * 256:(h % 2) * 256 + 256],
                            op0=ALU.mult, op1=ALU.mult,
                            accum_out=s_smp[:, n * XH + h, m:m + 1]).then_inc(S("s_dot"), 1)

            for j in (0, 1):
                dve.wait_ge(evac[j], xaq["mm1"][j])
            for n in range(9):
                if n < 8:
                    b = n % 2
                    for g in (0, 1):
                        dve.wait_ge(S("score"), 2 * n + g + 1)
                        dve.wait_ge(S("exp"), 4 * max(n - 1, 0))
                        link(nc.vector.tensor_reduce(
                            att[:, b, 3, 2 * g:2 * g + 2],
                            bank[g][:, :].rearrange("p (h m) -> p h m", h=2), AX.X, ALU.max))
                    nc.vector.tensor_scalar(att[:, b, 0, :], att[:, b, 3, :], -SC, None, ALU.mult)\
                        .then_inc(S("nmax"), 1)
                    if n < 4:
                        dots(2 * n)
                    dve.wait_ge(S("exp"), 4 * n + 4)
                    link(nc.vector.reciprocal(att[:, b, 2, :], att[:, b, 1, :]))
                    nc.vector.tensor_tensor(prob[b][:, :, :], prob[b][:, :, :],
                                            att[:, b, 2, :].unsqueeze(2).to_broadcast([P, XH, NMEM]),
                                            ALU.mult).then_inc(S("pnorm"), 1)
                    if n < 4:
                        dots(2 * n + 1)
                    if n == 4:
                        dve.wait_ge(S("srow"), 1)
                        link(nc.vector.tensor_reduce(s_row[:, 2:3], bank[6][0:32, 0:NMEM], AX.X, ALU.max))
                        nc.vector.tensor_scalar(s_row[:, 0:1], s_row[:, 2:3], -SC, None, ALU.mult)\
                            .then_inc(S("srow_v"), 1)
                        dve.wait_ge(S("srow_e"), 1)
                        link(nc.vector.reciprocal(s_row[:, 3:4], s_row[:, 1:2]))
                        nc.vector.tensor_scalar(p_smp[:, :], p_smp[:, :], s_row[:, 3:4], None, ALU.mult)\
                            .then_inc(S("srow_v"), 1)
                    if n == 5:
                        dve.wait_ge(S("srow"), 2)
                        link(nc.vector.memset(pT_smp[0][:, :, :], 0.0), False)
                        link(nc.vector.memset(pT_smp[1][:, :, :], 0.0))
                        for m in (0, 1):
                            nc.vector.tensor_copy(
                                pT_smp[m][:, :, 0:32:8],
                                bank[7][:, m * 32:m * 32 + 32].rearrange("p (b h) -> p b h", b=NS))\
                                .then_inc(S("srow_v"), 1)
                if n:
                    m = n - 1
                    c = slice(m * P, (m + 1) * P)
                    for g in (0, 1):
                        dve.wait_ge(S("o_hi"), 2 * m + g + 1)
                        nc.vector.tensor_tensor(o_lo[:, 4 * g:4 * g + 4, c],
                                                bank[4 + g][:, :].rearrange("p (k t) -> p k t", k=4),
                                                o_hi[:, 4 * g:4 * g + 4, c].bitcast(F), ALU.subtract)\
                            .then_inc(S("o_lo"), 1)
            dve.wait_ge(S("o_smp"), 8)
            nc.vector.tensor_copy(o_rows[:, 512:D], bank[7][0:NS, :]).then_inc(S("o_rows"), 1)
            dve.wait_ge(S("o_hi"), 17)
            nc.vector.tensor_tensor(o_lo[:, :, SEQ:T], bank[0][:, 0:64].rearrange("p (k b) -> p k b", k=KD),
                                    o_hi[:, :, SEQ:T].bitcast(F), ALU.subtract).then_inc(S("o_lo"), 1)

        def final_tensor(pe):
            pe.wait_ge(S("y_norm"), 3 * KD)
            for n in range(9):
                tn, b = (P if n < 8 else NS), 2 * (n % 3)
                pe.wait_ge(S("y_a"), max(n - 2, 0))
                pe.wait_ge(S("y_b"), max(n - 2, 0))
                for k in range(KD):
                    m = nc.tensor.transpose(bank[b + k // 4][0:tn, (k % 4) * P:(k % 4 + 1) * P],
                                            x[:, k, n * P:n * P + tn], ident)
                    if k % 4 == 3:
                        m.then_inc(S("yt"), 1)

        def final_evac(eng, half):
            for n in range(9):
                tn, b = (P if n < 8 else NS), 2 * (n % 3) + half
                eng.wait_ge(S("yt"), 2 * n + half + 1)
                o = y_nat[0:tn, n, 512 * half:512 * half + 512]
                if half == 0:
                    nc.scalar.activation(o, bank[b][0:tn, :], ACT.Copy).then_inc(S("y_a"), 1)
                else:
                    nc.vector.tensor_copy(o, bank[b][0:tn, :]).then_inc(S("y_b"), 1)

        def final_out(sp):
            for n in range(9):
                sp.wait_ge(S("y_a"), n + 1)
                sp.wait_ge(S("y_b"), n + 1)
                if n < 8:
                    sp.dma_start(O["y_prompt"][0, n * P:(n + 1) * P, :], y_nat[:, n, :])\
                        .then_inc(S("out4"), 16)
                else:
                    sp.dma_start(O["y_sample"][:, 0, :], y_nat[0:NS, n, :]).then_inc(S("out4"), 16)
            sp.wait_ge(S("out4"), 144)
            sp.wait_ge(S("out3"), 32)
            sp.wait_ge(S("rwkv_out"), 80)



        smp_d = nc.dram_tensor("smp_d", (6, NS, BW), F, kind="Internal").ap()
        smp_od = nc.dram_tensor("smp_od", (NS, BW), F, kind="Internal").ap()
        x_save = nc.dram_tensor("x_save", (P, KD, T), F, kind="Internal").ap()
        y_save = nc.dram_tensor("y_save", (P, 4, T), F, kind="Internal").ap()

        block = ctx.enter_context(nc.Block())

        @block.sync
        def _(sp):
            sp.dma_start(cst[:], A["constants"]).then_inc(S("cst_in"), 16)
            sp.dma_start(xnat_s[0:NS, :], A["x_sample"][:, 0, :]).then_inc(S("xs_in"), 16)
            for n in range(8):
                sp.dma_start(xnat[:, n, :], A["x_prompt"][0, n * P:(n + 1) * P, :])\
                    .then_inc(S("x_in0") if n < 1 else S("x_in1") if n < 4 else S("x_in2"), 16)
            for a, b in ffn1:
                load_weights(sp, a)
                load_weights(sp, b)
            for j in (0, 1):
                sp.wait_ge(evac[j], ffn1[-1][1]["mm1"][j])
            sp.dma_start(x_save, x[:, :, :]).then_inc(S("x_out"), 16)
            for ph in win:
                load_weights(sp, ph)
            gmlp_loads(sp)
            sp.wait_ge(S("vn"), 9)
            sp.dma_start(O["chunk_v_sample"][0, :, 0, :], vn[0:NS, 2, :]).then_inc(S("out"), 16)
            sp.wait_ge(S("gmix"), 9)
            sp.dma_start(y_save, z[:, 8:12, :]).then_inc(S("y_out"), 16)
            win_done(sp)
            sp.dma_start(shift_in[:, :], A["state_shift"][0, :, 0, :]).then_inc(S("prep_in"), 16)
            sp.dma_start(lora_w[0:64, :], A["rwkv_w2"][0]).then_inc(S("prep_in"), 16)
            sp.dma_start(lora_w[64:128, :], A["rwkv_a2"][0]).then_inc(S("prep_in"), 16)
            sp.wait_ge(S("sho_ev"), 4)
            sp.dma_start(O["state_shift_prompt"][0, :, 0, :], shift_out[0:1, :]).then_inc(S("rwkv_out"), 16)
            sp.dma_start(O["state_shift_sample"][0, :, 0, :], shift_out[1:NS + 1, :])\
                .then_inc(S("rwkv_out"), 16)
            sp.wait_ge(S("y_out"), 16)
            sp.wait_ge(S("out"), 16)
            sp.wait_ge(S("rwkv_out"), 32)
            sample_loads(sp)
            load_weights(sp, wout)
            mem_loads(sp)
            for ph in (memk, memv):
                load_weights(sp, ph)
            load_weights(sp, xaq)
            for n in range(8):
                cache_loads(sp, "k", n)
            for n in range(8):
                cache_loads(sp, "v", n)
            load_weights(sp, xao)
            for a, b in ffn2:
                load_weights(sp, a)
                load_weights(sp, b)
            final_out(sp)

        @block.gpsimd
        def _(g):
            nc.gpsimd.memset(eps_t[:, 0:1], 1e-6).then_inc(S("const"), 1)
            nc.gpsimd.memset(eps_t[:, 1:2], 1e-5).then_inc(S("const"), 1)
            nc.gpsimd.memset(eps_t[:, 2:3], 64e-5).then_inc(S("const"), 1)
            nc.gpsimd.memset(eps_t[:, 3:4], LOG_SHIFT / 2).then_inc(S("const"), 1)
            g.wait_ge(S("vz"), 1)
            for name, k in VROWS:
                r0, src = VAT[name], A[name]
                src = src[0] if name != "final_norm" else src
                if name == "rwkv_mu":
                    g.dma_start(vnat[r0:r0 + k - 1, :],
                                src[0:(k - 1) * P].rearrange("(k p) -> k p", p=P)).then_inc(S("v_in"), 16)
                    g.dma_start(vnat[r0 + k - 1:r0 + k, 0:NB - (k - 1) * P],
                                src[(k - 1) * P:NB].rearrange("(k p) -> k p", k=1)).then_inc(S("v_in"), 16)
                elif name == "rwkv_r_k":
                    g.dma_start(vnat[r0:r0 + k, :], src.rearrange("(k a) p -> k (a p)", a=2))\
                        .then_inc(S("v_in"), 16)
                else:
                    g.dma_start(vnat[r0:r0 + k, :], src.rearrange("(k p) -> k p", p=P))\
                        .then_inc(S("v_in"), 16)
            g.wait_ge(S("cst_in"), 16)
            for a, b in ffn1:
                split_weights(g, a)
                split_weights(g, b)
            for ph in win:
                split_weights(g, ph)
            for n in range(8):
                chunk_pool(g, n)
            for ph in (wout, memk, memv, xaq, xao, *(p for ab in ffn2 for p in ab)):
                split_weights(g, ph)

        NVDMA = 16 * (len(VROWS) + 1)

        @block.tensor
        def _(pe):
            pe.wait_ge(S("cst_in"), 16)
            for n in range(8):
                pe.wait_ge(*((S("x_in0"), 16) if n < 1 else (S("x_in1"), 48) if n < 4 else (S("x_in2"), 64)))
                b = 2 * (n % 4)
                if n >= 4:
                    pe.wait_ge(S("xt_a"), n - 3)
                    pe.wait_ge(S("xt_b"), n - 3)
                for k in range(KD):
                    m = nc.tensor.transpose(bank[b + k // 4][:, (k % 4) * P:(k % 4 + 1) * P],
                                            xnat[:, n, k * P:(k + 1) * P], ident)
                    if k % 4 == 3:
                        m.then_inc(S("xt"), 1)
            pe.wait_ge(S("xs_in"), 16)
            pe.wait_ge(S("xt_a"), 5)
            for k in range(KD):
                m = nc.tensor.transpose(bank[0][:, k * NS:(k + 1) * NS],
                                        xnat_s[0:NS, k * P:(k + 1) * P], ident[0:NS, 0:NS])
            m.then_inc(S("xt"), 1)
            pe.wait_ge(S("v_in"), NVDMA)
            pe.wait_ge(S("xt_b"), 5)
            nc.tensor.transpose(bank[1][:, 0:NVEC], vnat[0:NVEC, :], ident[0:NVEC, 0:NVEC])\
                .then_inc(S("vt"), 1)
            norm_tensor(pe, 0)
            for a, b in ffn1:
                if a["f0"] == 0:
                    pe.wait_ge(S("n_lo"), 3 * KD)
                multiply(pe, a)
                multiply(pe, b, lambda h, b=b: pe.wait_ge(
                    S("hid_lo"), 3 * (b["f1"] - b["kt"] + (min(4, b["kt"]) if h == 0 else b["kt"]))))
            pe.wait_ge(evac[0], ffn1[-1][1]["mm1"][0])
            norm_tensor(pe, 1)
            pe.wait_ge(S("n_lo"), 48)
            for ph in win:
                multiply(pe, ph)
            gmlp_tensor(pe)
            prep_tensor(pe)
            for n in range(8):
                chunk_tensor(pe, n)
            post_tensor(pe)
            pe.wait_ge(S("ya_lo"), 1)
            multiply(pe, wout, lambda h: pe.wait_ge(S("yb_lo"), 12))
            mem_tensor_a(pe)
            pe.wait_ge(S("mem_lo"), KD)
            multiply(pe, memk)
            norm_tensor(pe, 2)
            multiply(pe, memv)
            nat_tensor(pe)
            pe.wait_ge(S("n_lo"), 72)
            pe.wait_ge(S("nat_a"), 4)
            pe.wait_ge(S("nat_b"), 4)
            multiply(pe, xaq)
            att_tensor(pe)
            pe.wait_ge(S("o_lo"), 17)
            multiply(pe, xao)
            norm_tensor(pe, 3)
            for a, b in ffn2:
                if a is ffn2[0][0]:
                    pe.wait_ge(S("n_lo"), 96)
                multiply(pe, a)
                multiply(pe, b, lambda h, b=b: pe.wait_ge(
                    S("hid_lo"), 3 * (b["f1"] - b["kt"] + (min(4, b["kt"]) if h == 0 else b["kt"]))))
            norm_tensor(pe, 4)
            final_tensor(pe)


        @block.scalar
        def _(act):
            for n in range(8):
                b = 2 * (n % 4)
                act.wait_ge(S("xt"), 2 * n + 1)
                nc.scalar.activation(x[:, 0:4, n * P:(n + 1) * P],
                                     bank[b][:, :].rearrange("p (k n) -> p k n", k=4), ACT.Copy)\
                    .then_inc(S("xt_a"), 1)
            act.wait_ge(S("xt"), 17)
            nc.scalar.activation(x[:, :, SEQ:T],
                                 bank[0][:, 0:KD * NS].rearrange("p (k n) -> p k n", k=KD), ACT.Copy)\
                .then_inc(S("xt_a"), 1)

            def ready0(e):
                e.wait_ge(S("xt_a"), 9)
                e.wait_ge(S("xt_b"), 8)
                e.wait_ge(S("vt"), 1)
            norm_scalar(act, 0, ready0)
            prev = None
            for a, b in ffn1:
                gu_scalar(act, a, prev)
                prev = b

            def ready1(e):
                for j in (0, 1):
                    e.wait_ge(evac[j], ffn1[-1][1]["mm1"][j])
            norm_scalar(act, 1, ready1)
            z_evac(act, True)
            gmlp_scalar(act)
            prep_scalar(act)
            for n in range(8):
                chunk_scalar(act, n)
            post_scalar(act)

            def after(ph):
                def wait(e):
                    for j in (0, 1):
                        e.wait_ge(evac[j], ph["mm1"][j])
                return wait
            mem_scalar_a(act)
            mem_scalar_b(act)
            plain_evac(act, True, memk, kT)
            norm_scalar(act, 2, after(wout))
            plain_evac(act, True, memv, vT)
            nat_scalar(act)
            nat_out(act)
            plain_evac(act, True, xaq, qT)
            att_scalar(act)
            norm_scalar(act, 3, after(xao))
            prev = None
            for a, b in ffn2:
                gu_scalar(act, a, prev)
                prev = b
            norm_scalar(act, 4, after(ffn2[-1][1]))
            final_evac(act, 0)

        @block.vector
        def _(dve):
            nc.vector.memset(vnat[:, :], 0.0).then_inc(S("vz"), 1)
            for n in range(8):
                b = 2 * (n % 4) + 1
                dve.wait_ge(S("xt"), 2 * n + 2)
                nc.vector.tensor_copy(x[:, 4:8, n * P:(n + 1) * P],
                                      bank[b][:, :].rearrange("p (k n) -> p k n", k=4))\
                    .then_inc(S("xt_b"), 1)
            dve.wait_ge(S("vt"), 1)
            link(nc.vector.tensor_copy(vec[:, :], bank[1][:, 0:NVEC]))
            dve.wait_ge(S("xt_a"), 9)
            norm_vector(dve, 0, "ln_ffn1")
            for a, b in ffn1:
                gu_vector(dve, a)
                add_to_x(dve, b, 0.5)
            for j in (0, 1):
                dve.wait_ge(evac[j], ffn1[-1][1]["mm1"][j])
            norm_vector(dve, 1, "ln_mix")
            z_evac(dve, False)
            gmlp_vector(dve)
            prep_vector(dve)
            dve.wait_ge(mm[0], WIN_END[0])
            dve.wait_ge(mm[1], WIN_END[1])
            nc.vector.memset(st_T[:, 0, :, :], 0.0).then_inc(S("st0"), 1)
            nc.vector.memset(Us[:, :], 0.0).then_inc(S("st0"), 1)
            dve.wait_ge(S("st0"), 2)
            for n in range(8):
                chunk_vector(dve, n)
            post_vector(dve)
            dve.wait_ge(S("x_back"), 16)
            add_to_x(dve, wout, 1.0)
            mem_vector_a(dve)
            mem_vector_b(dve)
            plain_evac(dve, False, memk, kT)
            norm_vector(dve, 2, "ln_xattn")
            plain_evac(dve, False, memv, vT)
            nat_vector(dve)
            plain_evac(dve, False, xaq, qT)
            att_vector(dve)
            add_to_x(dve, xao, 1.0)
            norm_vector(dve, 3, "ln_ffn2")
            for a, b in ffn2:
                gu_vector(dve, a)
                add_to_x(dve, b, 0.5)
            for j in (0, 1):
                dve.wait_ge(evac[j], ffn2[-1][1]["mm1"][j])
            norm_vector(dve, 4, "final_norm")
            final_evac(dve, 1)


_IN = ["x_prompt", "x_sample", "state_rwkv", "state_shift", "cache_mem_k", "cache_mem_v", "mem_prompt",
       "ln_ffn1", "ffn1_gate", "ffn1_up", "ffn1_down", "ln_mix", "w_in", "w_out", "sgu_w", "sgu_b",
       "sgu_ln_g", "sgu_ln_b", "rwkv_mu", "rwkv_w0", "rwkv_w2", "rwkv_a0", "rwkv_a2", "rwkv_g2",
       "rwkv_k_k", "rwkv_k_a", "rwkv_r_k", "rwkv_gn_g", "rwkv_gn_b", "ln_xattn", "mem_norm", "xa_q",
       "xa_k", "xa_v", "xa_o", "ln_ffn2", "ffn2_gate", "ffn2_up", "ffn2_down", "final_norm"]
_OUT = [("y_prompt", (1, SEQ, D)), ("y_sample", (NS, 1, D)),
        ("state_rwkv_prompt", (1, 1, HEADS, HN, HN)), ("state_shift_prompt", (1, 1, 1, NB)),
        ("mem_k_prompt", (1, 1, NMEM, XH, XD)), ("mem_v_prompt", (1, 1, NMEM, XH, XD)),
        ("state_rwkv_sample", (1, NS, HEADS, HN, HN)), ("state_shift_sample", (1, NS, 1, NB)),
        ("chunk_v_sample", (1, NS, 1, AW))]


def kernel(**inputs):
    import concourse.bacc as bacc
    from concourse.bass_utils import run_bass_kernel_spmd

    nc = bacc.Bacc("TRN2", target_bir_lowering=False, num_devices=1)
    arrays = {f"in_{n}": np.ascontiguousarray(inputs[n]) for n in _IN}
    arrays["in_constants"] = constants()
    A = {k[3:]: nc.dram_tensor(k, a.shape, mybir.dt.from_np(a.dtype), kind="ExternalInput").ap()
         for k, a in arrays.items()}
    O = {n: nc.dram_tensor(f"out_{n}", s, mybir.dt.float32, kind="ExternalOutput").ap() for n, s in _OUT}
    program(nc, A, O)
    r = run_bass_kernel_spmd(nc, [arrays], core_ids=[0])
    return tuple(r.results[0][f"out_{n}"] for n, _ in _OUT)
```

```python
import numpy as np
import concourse.bass as bass
from concourse import mybir
from contextlib import ExitStack

P = 128
D, SEQ, NS = 1024, 1024, 8
T = SEQ + NS
KD = D // P
TOK = [(0, 344), (344, 344), (688, 344)]
DFF = 2816
FT = DFF // P
GROUPS = [8, 8, 6]
AW = BW = 512
HEADS, HN = 8, 64
NB = 3 * BW + 64 + 64 + 160
INP = 2 * AW + NB
NBT = -(-NB // P)
CH = 64
NMEM, XH, XD = 256, 4, 256
DECAY = float(np.exp(-0.5))

LOG_SHIFT = 20 * float(np.log(2.0))

VROWS = [("ln_ffn1", 8), ("ln_mix", 8), ("ln_xattn", 8), ("mem_norm", 8), ("ln_ffn2", 8),
         ("final_norm", 8), ("rwkv_w0", 4), ("rwkv_a0", 4), ("rwkv_k_k", 4), ("rwkv_k_a", 4),
         ("rwkv_r_k", 4), ("rwkv_gn_g", 4), ("rwkv_gn_b", 4), ("rwkv_mu", NBT)]
VAT, _n = {}, 0
for _name, _k in VROWS:
    VAT[_name] = _n
    _n += _k
NVEC = _n

C_ID, C_ONE, C_BLK, C_STR, C_INC, C_TRI, C_LVL = 0, 1, 2, 3, 4, 5, 6
NCST = 12
LEVELS = 6


def constants():
    s, t = np.arange(P)[:, None], np.arange(P)[None, :]
    same = s // CH == t // CH
    tabs = [s == t, s == s + 0 * t, same / HN, same & (s < t), same & (s <= t), s <= t]
    tabs += [(s >> (l + 1) == t >> (l + 1)) & (s >> l < t >> l) for l in range(LEVELS)]
    return np.stack([np.asarray(m, np.float32) for m in tabs], 1)


def program(nc, A, O):
    F, R = mybir.dt.float32, mybir.dt.float32r
    ALU, ACT, AX = mybir.AluOpType, mybir.ActivationFunctionType, mybir.AxisListType
    ds = bass.ds
    ctx = ExitStack()
    with ctx:
        base = [-(-int(nc.sbuf_base) // 32) * 32]

        def take(nbytes):
            at = base[0]
            base[0] += -(-nbytes // 32) * 32
            return at

        def at(name, shape, off, dt=F):
            return nc.alloc_sbuf_tensor_at(name, shape, dt, offset=off)

        ROW = T * 4
        arena_z = take(24 * ROW)
        arena_h = take(16 * ROW)
        arena_w = take(3 * 4 * 4 * P * 4)
        arena_c = take(NCST * P * 4)
        arena_v = take(NVEC * 4)
        arena_g = take(3 * 344 * 4)
        arena_t = take(3 * 344 * 4)
        arena_m = take(8192)
        cap = int(nc.sbuf_usable_end) if not callable(nc.sbuf_usable_end) else int(nc.sbuf_usable_end())
        assert base[0] <= cap, (base[0], cap)

        x = at("x", [P, KD, T], arena_z)
        z = at("z", [P, 24, T], arena_z)
        xnat = at("xnat", [P, 8, D], arena_z + 8 * ROW)
        xnat_s = at("xnat_s", [P, D], arena_z + 16 * ROW)
        hid_hi = at("hid_hi", [P, 8, T], arena_z + 8 * ROW, R)
        hid_lo = at("hid_lo", [P, 8, T], arena_z + 16 * ROW, R)
        h_hi = at("h_hi", [P, KD, T], arena_h, R)
        h_lo = at("h_lo", [P, KD, T], arena_h + 8 * ROW, R)
        raw = at("raw", [P, 4, 4, P], arena_w)
        w_hi = at("w_hi", [P, 4, 4, P], arena_w + 8192, R)
        w_lo = at("w_lo", [P, 4, 4, P], arena_w + 16384, R)
        cst = at("cst", [P, NCST, P], arena_c)
        vec = at("vec", [P, NVEC], arena_v)
        vnat = at("vnat", [P, P], arena_g)
        gate_s = at("gate_s", [P, 3, 344], arena_g)
        tmp = at("tmp", [P, 3, 344], arena_t)
        rstd = at("rstd", [P, 3, 344], arena_m)
        bank = [ctx.enter_context(nc.psum_tensor(f"bank{i}", [P, 512], F)) for i in range(8)]
        ident = cst[:, C_ID, :]

        mem_hi = at("mem_hi", [P, KD, NMEM], arena_z + 8 * ROW, R)
        mem_lo = at("mem_lo", [P, KD, NMEM], arena_z + 8 * ROW + 8192, R)
        qT = at("qT", [P, KD, T], arena_z + 8 * ROW)
        kT = at("kT", [P, KD, NMEM], arena_z + 16 * ROW)
        v_n = at("v_n", [P, 2, D], arena_z + 16 * ROW + 8192)
        vT = at("vT", [P, KD, NMEM], arena_z + 16 * ROW + 16384)
        mk_n = at("mk_n", [P, 2, D], arena_z + 16 * ROW + 24576)
        mem_n = at("mem_n", [P, 2, D], arena_m)
        mem_sq = at("mem_sq", [P, D], arena_c + C_BLK * 512)
        cache = [at("cache0", [P, 2, D], arena_z + 16 * ROW + 16384),
                 at("cache1", [P, 2, D], arena_z + 16 * ROW + 24576)]
        prob = [at("prob0", [P, XH, NMEM], arena_g), at("prob1", [P, XH, NMEM], arena_m)]
        probT = [at("probT0", [P, XH * 2, P], arena_t), at("probT1", [P, XH * 2, P], arena_m + 4096)]
        att = at("att", [P, 2, 4, XH], arena_c + C_LVL * 512)
        mem_st = at("mem_st", [P, 2, 4], arena_c + C_BLK * 512 + 4096)
        s_smp = at("s_smp", [P, NS * XH, 2], arena_c + C_LVL * 512 + 256)
        s_row = at("s_row", [NS * XH, 4], arena_c + C_LVL * 512 + 512)
        p_smp = at("p_smp", [NS * XH, NMEM], arena_c + C_LVL * 512 + 544)
        pT_smp = [at("pT_smp0", [P, NS, 33], arena_c + C_BLK * 512),
                  at("pT_smp1", [P, NS, 33], arena_c + C_LVL * 512 + 2016)]
        s_junk = at("s_junk", [P, XD], arena_c + C_STR * 512)
        o_rows = at("o_rows", [NS, D], arena_z + 16 * ROW + 16384)
        o_hi = at("o_hi", [P, KD, T], arena_h, R)
        o_lo = at("o_lo", [P, KD, T], arena_h + 8 * ROW, R)
        y_nat = at("y_nat", [P, 9, D], arena_z + 8 * ROW)
        h2_hi = at("h2_hi", [P, KD, T], arena_z + 8 * ROW, R)
        h2_lo = at("h2_lo", [P, KD, T], arena_z + 16 * ROW, R)
        hid2_hi = at("hid2_hi", [P, 8, T], arena_h, R)
        hid2_lo = at("hid2_lo", [P, 8, T], arena_h + 8 * ROW, R)
        fin_g = at("fin_g", [P, D], arena_c + C_BLK * 512)
        fin_st = at("fin_st", [P, 9, 4], arena_c + C_BLK * 512 + 4096)
        fin_sq = at("fin_sq", [P, 2, 512], arena_g)

        gw_nat = at("gw_nat", [P, 8, P], arena_z + 7 * ROW)
        gwT = at("gwT", [P, 8, P], arena_t)
        ln_gb = at("ln_gb", [P, 2, AW], arena_g)
        g_bias = at("g_bias", [P, 4, P], arena_m + 4160)
        g_w00 = at("g_w00", [P, 4], arena_m + 6208)
        g_stat = at("g_stat", [P, 2, 8], arena_m + 6240)
        vn = at("vn", [P, 3, AW], arena_h)
        g_mix = at("g_mix", [P, 2, AW], arena_h + 2 * ROW)
        shift_out = at("shift_out", [NS + 1, NB], arena_h + 4 * ROW)
        shift_in = at("shift_in", [NS, NB], arena_h + 6 * ROW)
        shiftT = at("shiftT", [P, NBT, NS], arena_h + 8 * ROW - 512)
        diff = at("diff", [P, 8, T], arena_z + 8 * ROW)
        diff_p = at("diff_p", [P, 7, T], arena_h + 9 * ROW)
        lora_w = at("lora_w", [P, BW], arena_g)
        nkk = at("nkk", [P, 4, T], arena_h)
        bvec = at("bvec", [P, 4, T], arena_h + 4 * ROW)
        sg = at("sg", [P, 4, T], arena_h + 8 * ROW)
        cum = at("cum", [P, 4, T], arena_h + 12 * ROW)
        scan_mask = at("scan_mask", [P, T], arena_z + 7 * ROW)
        mats = [{n: at(f"{n}{q}", [P, 4, P], arena_z + 8 * ROW + (8 * q + j) * 2048)
                 for j, n in enumerate(("MT", "QKT", "TT", "Ti", "Y", "LoT"), 2)}
                for q in (0, 1)]
        LQ = [at(f"LQ{q}", [P, 2, 4, P], arena_z + 8 * ROW + 8 * q * 2048) for q in (0, 1)]
        for q in (0, 1):
            mats[q]["LT"], mats[q]["QBT"] = LQ[q][:, 0], LQ[q][:, 1]
        AR = [at("AR0", [P, 2, 4, P], arena_g),
              at("AR1", [P, 2, 4, P], arena_w + 14336)]
        BK = at("BK", [P, 2, 4, P], arena_t)
        dec = at("dec", [P, 4, P], arena_z + 7 * ROW)
        ext = at("ext", [P, 4, P], arena_z + 7 * ROW + 2048)
        Bt = at("Bt", [P, BW], arena_z + 4 * ROW)
        Kt = at("Kt", [P, BW], arena_z + 4 * ROW + 2048)
        Vt = at("Vt", [P, BW], arena_m)
        vstage = at("vstage", [P, 4, P], arena_w + 18432)
        Xs = at("Xs", [P, BW], arena_m + 2048)
        Us = at("Us", [P, BW], arena_m + 4096)
        smp_n = at("smp_n", [NS, 6, BW], arena_z + 8 * ROW)
        smp_S = at("smp_S", [P, 32, HN], arena_z + 8 * ROW + 12288)
        smp_t = at("smp_t", [P, 32, HN], arena_z + 8 * ROW + 20480)
        smp_v = at("smp_v", [P, 6, HN], arena_z + 8 * ROW + 28672)
        smp_o = at("smp_o", [P, 2, 32], arena_z + 8 * ROW + 30208)
        gn_sq = at("gn_sq", [P, 3, 344], arena_t)
        smp_on = at("smp_on", [NS, BW], arena_z + 8 * ROW + 30464)
        smp_w = at("smp_w", [P, 4, NS], arena_z + 8 * ROW + 32512)
        st_out = at("st_out", [P, 4, P], arena_w + 12288)
        g2_w = at("g2_w", [P, 2, BW], arena_z + 7 * ROW)
        ya_in = at("ya_in", [P, 4, T], arena_h + 4 * ROW)
        y_hi = at("y_hi", [P, KD, T], arena_z + 8 * ROW, R)
        y_lo = at("y_lo", [P, KD, T], arena_z + 16 * ROW, R)
        st_T = at("st_T", [P, 3, 4, P], arena_w)
        decm = at("decm", [P, 2, 4, P], arena_w + 6144)

        links = [0]

        def link(ins, wait=True):
            links[0] += 1
            ins.then_inc(S("link"), 1)
            if wait:
                nc.vector.wait_ge(S("link"), links[0])

        def v_col(name, k):
            return vec[:, VAT[name] + k:VAT[name] + k + 1]

        sems = {}

        def S(name):
            if name not in sems:
                sems[name] = ctx.enter_context(nc.semaphore(name))
            return sems[name]

        raw_in = [S(f"raw_in{i}") for i in range(4)]
        hi_done = [S(f"hi_done{i}") for i in range(4)]
        split_done = [S(f"split_done{i}") for i in range(4)]
        w_used = [S(f"w_used{i}") for i in range(2)]
        mm = [S("mm0"), S("mm1")]
        evac = [S("evac0"), S("evac1")]

        phases = []
        total = {"unit": 0, "mm": [0, 0], "f": 0}

        def phase(name, units, kt, src, hi, lo, toks=TOK, width=P):
            ph = dict(name=name, units=units, kt=kt, src=src, hi=hi, lo=lo, toks=toks, width=width,
                      u0=total["unit"], mm0=list(total["mm"]), f0=total["f"])
            total["unit"] += units
            for u in range(units):
                total["mm"][(ph["u0"] + u) % 2] += len(toks)
            ph["mm1"] = list(total["mm"])
            phases.append(ph)
            return ph

        def kview(w):
            return w.rearrange("(k p) c -> p k c", p=P)

        def ffn(n):
            wg, wu, wd = (kview(A[f"ffn{n}_{m}"][0]) for m in ("gate", "up", "down"))
            out, f = [], 0
            hi, lo, gh, gl = (h_hi, h_lo, hid_hi, hid_lo) if n == 1 else (h2_hi, h2_lo, hid2_hi, hid2_lo)
            for g in GROUPS:
                gu = phase(f"gu{n}_{f}", 2 * g, 8,
                           lambda s, i, f=f: ((wg, wu)[s], (i + f) * P), hi, lo)
                total["f"] += g
                dn = phase(f"dn{n}_{f}", 8, g,
                           lambda s, i, f=f, g=g: (wd[:, f:f + g, :], (2 * i + s) * P), gh, gl)
                dn["f1"] = total["f"]
                gu["hid"] = gh, gl
                out.append((gu, dn))
                f += g
            return out

        w_in = kview(A["w_in"][0])
        ffn1 = ffn(1)
        win_a = phase("win_a", 16, 8, lambda s, i: (w_in, (2 * i + s) * P), h_hi, h_lo)
        win_b = phase("win_b", 6, 8, lambda s, i: (w_in, (2 * i + s + 16) * P), h_hi, h_lo)
        win_c = phase("win_c", 1, 8, lambda s, i: (w_in, 22 * P), h_hi, h_lo, width=NB - 14 * P)
        win = [win_a, win_b, win_c]
        win_a["peel"] = True
        wo = kview(A["w_out"][0])
        wout = phase("wout", 8, 8, lambda s, i: (wo, (2 * i + s) * P), y_hi, y_lo)
        xk, xv, xq, xo = (kview(A[n][0]) for n in ("xa_k", "xa_v", "xa_q", "xa_o"))
        MTOK = [(0, NMEM)]
        memk = phase("memk", 8, 8, lambda s, i: (xk, (2 * i + s) * P), mem_hi, mem_lo, toks=MTOK)
        memv = phase("memv", 8, 8, lambda s, i: (xv, (2 * i + s) * P), mem_hi, mem_lo, toks=MTOK)
        xaq = phase("xaq", 8, 8, lambda s, i: (xq, (2 * i + s) * P), h_hi, h_lo)
        xao = phase("xao", 8, 8, lambda s, i: (xo, (2 * i + s) * P), o_hi, o_lo)
        ffn2 = ffn(2)
        ffn2[0][0]["peel"] = True

        def pairs(eng, ph, step):
            first = 0
            if ph["u0"] == 0 or "peel" in ph:
                step(0)
                first = 1
            if ph["units"] // 2 > first:
                with eng.Fori(first, ph["units"] // 2) as i:
                    step(i)

        def unit_steps(eng, ph, body):
            def run(i, s):
                for_u = ph["u0"] + s
                body(i, s, [((2 * for_u + h) % 4, (2 * for_u + h) // 4 + i) for h in (0, 1)])
            pairs(eng, ph, lambda i: [run(i, s) for s in (0, 1)])
            if ph["units"] % 2:
                i = ph["units"] // 2
                run(i, 0)

        def split_k(kt):
            return [(0, min(4, kt)), (4, kt - 4)]

        def load_weights(sp, ph):
            def body(i, s, turns):
                w, col = ph["src"](s, i)
                for (slot, turn), (k0, nk) in zip(turns, split_k(ph["kt"])):
                    sp.wait_ge(split_done[slot], turn)
                    sp.dma_start(raw[:, slot, 0:nk, 0:ph["width"]],
                                 w[:, k0:k0 + nk, ds(col, ph["width"])]).then_inc(raw_in[slot], 16)
            unit_steps(sp, ph, body)

        def split_weights(g, ph, high=True, low=True):
            def body(i, s, turns):
                st = (ph["u0"] + s) % 2
                for h, ((slot, turn), (k0, nk)) in enumerate(zip(turns, split_k(ph["kt"]))):
                    part = (slice(None), slot, slice(0, nk), slice(0, ph["width"]))
                    if high:
                        if h == 0:
                            g.wait_ge(w_used[st], turn)
                        else:
                            g.wait_ge(mm[st], i * len(ph["toks"]) + ph["mm0"][st])
                        g.wait_ge(raw_in[slot], turn * 16 + 16)
                    if high and not low:
                        nc.scalar.activation(w_hi[part], raw[part], ACT.Copy).then_inc(hi_done[slot], 1)
                        continue
                    if high:
                        nc.gpsimd.tensor_tensor(w_hi[part], raw[part],
                                                cst[:, C_ONE:C_ONE + 1, 0:ph["width"]].to_broadcast(
                                                    [P, nk, ph["width"]]), ALU.mult)\
                            .then_inc(hi_done[slot], 1)
                    g.wait_ge(hi_done[slot], turn + 1)
                    nc.gpsimd.tensor_tensor(w_lo[part], raw[part], w_hi[part].bitcast(F),
                                            ALU.subtract).then_inc(split_done[slot], 1)
            unit_steps(g, ph, body)

        def multiply(pe, ph, piece_ready=None, tile_ready=None, after_first=None):
            nt, width, kt = len(ph["toks"]), ph["width"], ph["kt"]

            def body(i, s, turns):
                st = (ph["u0"] + s) % 2
                pieces = list(zip((0, 1), turns, split_k(kt)))

                def product(h, slot, k0, nk, t):
                    t0, tn = ph["toks"][t]
                    out = bank[3 * st + t][0:width, 0:tn]
                    for k in range(nk):
                        a, b = w_hi[:, slot, k, 0:width], w_lo[:, slot, k, 0:width]
                        hi, lo = ph["hi"][:, k0 + k, t0:t0 + tn], ph["lo"][:, k0 + k, t0:t0 + tn]
                        first, last = k0 + k == 0, k0 + k == kt - 1
                        nc.tensor.matmul(out, b, hi, start=first, stop=False)
                        nc.tensor.matmul(out, a, lo, start=False, stop=False)
                        m = nc.tensor.matmul(out, a, hi, start=False, stop=last)
                    if h == 1:
                        m.then_inc(mm[st], 1)
                    elif t == nt - 1:
                        m.then_inc(w_used[slot // 2], 1)

                pe.wait_ge(evac[st], i * nt + ph["mm0"][st])
                if tile_ready and isinstance(i, int) and s == 0:
                    for h, (slot, turn), _ in pieces:
                        pe.wait_ge(split_done[slot], turn + 1)
                    for t in range(nt):
                        tile_ready(t)
                        for h, (slot, turn), (k0, nk) in pieces:
                            product(h, slot, k0, nk, t)
                    after_first()
                    return
                for h, (slot, turn), (k0, nk) in pieces:
                    if piece_ready and s == 0:
                        piece_ready(h)
                    pe.wait_ge(split_done[slot], turn + 1)
                    for t in range(nt):
                        product(h, slot, k0, nk, t)
                if after_first and isinstance(i, int) and s == 0:
                    after_first()
            unit_steps(pe, ph, body)

        def each_tile(eng, ph, fn):
            nt = len(ph["toks"])

            def body(i, s, turns):
                st = (ph["u0"] + s) % 2
                for t in range(nt):
                    fn(i, s, st, t, i * nt + ph["mm0"][st] + t + 1)
            unit_steps(eng, ph, body)

        def tslice(t):
            return slice(TOK[t][0], TOK[t][0] + TOK[t][1])

        def gu_scalar(act, ph, prev_down):
            st = ph["u0"] % 2
            if prev_down:
                for j in (0, 1):
                    act.wait_ge(mm[j], prev_down["mm1"][j])
            hi = ph["hid"][0]

            def step(i):
                for t in range(3):
                    act.wait_ge(evac[st], i * 3 + ph["mm0"][st] + t + 1)
                    nc.scalar.activation(gate_s[:, t, :], gate_s[:, t, :], ACT.Silu)\
                        .then_inc(S("silu"), 1)
                for t in range(3):
                    act.wait_ge(S("prod"), i * 3 + 3 * ph["f0"] + t + 1)
                    nc.scalar.activation(hi[:, ds(i, 1), tslice(t)],
                                         tmp[:, t:t + 1, :], ACT.Copy).then_inc(S("hid_hi"), 1)
            pairs(act, ph, step)

        def gu_vector(dve, ph):
            sg, su = ph["u0"] % 2, (ph["u0"] + 1) % 2
            hi, lo = ph["hid"]

            def step(i):
                done = i * 3 + 3 * ph["f0"]

                def gate(t):
                    dve.wait_ge(mm[sg], i * 3 + ph["mm0"][sg] + t + 1)
                    dve.wait_ge(S("prod"), done)
                    nc.vector.tensor_tensor(gate_s[:, t, :], bank[3 * sg + t][:, 0:344],
                                            rstd[:, t, :], ALU.mult).then_inc(evac[sg], 1)

                def up(t):
                    dve.wait_ge(mm[su], i * 3 + ph["mm0"][su] + t + 1)
                    dve.wait_ge(S("hid_lo"), done)
                    nc.vector.tensor_tensor(tmp[:, t, :], bank[3 * su + t][:, 0:344],
                                            rstd[:, t, :], ALU.mult).then_inc(evac[su], 1)

                def prod(t):
                    dve.wait_ge(evac[su], i * 3 + ph["mm0"][su] + t + 1)
                    dve.wait_ge(S("silu"), done + t + 1)
                    nc.vector.tensor_tensor(tmp[:, t, :], tmp[:, t, :], gate_s[:, t, :], ALU.mult)\
                        .then_inc(S("prod"), 1)

                def low(t):
                    dve.wait_ge(S("hid_hi"), done + t + 1)
                    nc.vector.tensor_tensor(lo[:, ds(i, 1), tslice(t)], tmp[:, t:t + 1, :],
                                            hi[:, ds(i, 1), tslice(t)].bitcast(F),
                                            ALU.subtract).then_inc(S("hid_lo"), 1)
                for t in range(3):
                    gate(t)
                up(0)
                prod(0)
                up(1)
                prod(1)
                low(0)
                up(2)
                prod(2)
                low(1)
                low(2)
            pairs(dve, ph, step)

        def add_to_x(dve, ph, scale):
            for j in (0, 1):
                dve.wait_ge(evac[j], ph["mm0"][j])

            def one(i, s, st, t, count):
                dve.wait_ge(mm[st], count)
                xs = x[:, ds(2 * i + s, 1), tslice(t)]
                nc.vector.scalar_tensor_tensor(
                    out=xs, in0=bank[3 * st + t][:, 0:344].rearrange("p (a n) -> p a n", a=1),
                    scalar=scale, in1=xs, op0=ALU.mult, op1=ALU.add).then_inc(evac[st], 1)
            each_tile(dve, ph, one)

        def split_scalar(act, e, gain, hi, k, t, c):
            nc.scalar.activation(hi[:, k, tslice(t)], x[:, k, tslice(t)], ACT.Copy,
                                 scale=v_col(gain, k)).then_inc(S("x_hi"), 1)
            act.wait_ge(S("x_acc"), max(24 * e + c - 2, 0))
            nc.scalar.activation(gate_s[:, c % 3, :], x[:, k, tslice(t)], ACT.Square)\
                .then_inc(S("x_sq"), 1)

        def split_vector(dve, e, gain, hi, lo, k, t, c):
            dve.wait_ge(S("x_hi"), 24 * e + c + 1)
            nc.vector.scalar_tensor_tensor(out=lo[:, k, tslice(t)], in0=x[:, k, tslice(t)],
                                           scalar=v_col(gain, k), in1=hi[:, k, tslice(t)].bitcast(F),
                                           op0=ALU.mult, op1=ALU.subtract).then_inc(S("x_lo"), 1)
            dve.wait_ge(S("x_sq"), 24 * e + c + 1)
            if k == 0:
                nc.vector.tensor_copy(tmp[:, t, :], gate_s[:, c % 3, :]).then_inc(S("x_acc"), 1)
            else:
                dve.wait_ge(S("x_acc"), 24 * e + c)
                nc.vector.tensor_tensor(tmp[:, t, :], tmp[:, t, :], gate_s[:, c % 3, :], ALU.add)\
                    .then_inc(S("x_acc"), 1)

        def residual_scalar(act, e, gain, ph, hi):
            for u in range(8):
                for t in range(3):
                    st = (ph["u0"] + u) % 2
                    act.wait_ge(evac[st], ph["mm0"][st] + 3 * (u // 2) + t + 1)
                    split_scalar(act, e, gain, hi, u, t, 3 * u + t)

        def residual_vector(dve, e, gain, ph, hi, lo, scale):
            for j in (0, 1):
                dve.wait_ge(evac[j], ph["mm0"][j])
            for c in range(25):
                if c < 24:
                    u, t = c // 3, c % 3
                    st = (ph["u0"] + u) % 2
                    dve.wait_ge(mm[st], ph["mm0"][st] + 3 * (u // 2) + t + 1)
                    xs = x[:, u, tslice(t)]
                    nc.vector.scalar_tensor_tensor(out=xs, in0=bank[3 * st + t][:, 0:344], scalar=scale,
                                                   in1=xs, op0=ALU.mult, op1=ALU.add)\
                        .then_inc(evac[st], 1)
                if c > 0:
                    split_vector(dve, e, gain, hi, lo, (c - 1) // 3, (c - 1) % 3, c - 1)

        def rms_tensor(pe, e):
            for t in range(3):
                pe.wait_ge(S("x_acc"), 24 * (e + 1))
                if t == 2:
                    pe.wait_ge(S("rms"), 3 * e + 1)
                nc.tensor.matmul(bank[6 + t % 2][:, 0:344], cst[:, C_ONE, :], tmp[:, t, :],
                                 start=True, stop=True).then_inc(S("x_sum"), 1)

        def rms_scalar(act, e):
            act.wait_ge(S("const"), 4)
            for t in range(3):
                act.wait_ge(S("x_sum"), 3 * e + t + 1)
                nc.scalar.activation(rstd[:, t, :], bank[6 + t % 2][:, 0:344], ACT.Sqrt,
                                     bias=eps_col, scale=1.0 / D).then_inc(S("rms"), 1)

        def rms_vector(dve, e):
            for t in range(3):
                dve.wait_ge(S("rms"), 3 * e + t + 1)
                link(nc.vector.reciprocal(rstd[:, t, :], rstd[:, t, :]), t == 2)

        eps_t = at("eps_t", [P, 8], take(32))
        eps_col = eps_t[:, 0:1]


        ZB = [8 + u for u in range(8, 16)] + list(range(0, 7))
        WIN_END = win_c["mm1"]

        def z_evac(dve):
            for ph, z0 in zip(win, (8, 0, 6)):
                if ph is win_b:
                    dve.wait_ge(S("x_out"), 16)
                w = ph["width"]

                def one(i, s, st, t, count, z0=z0, w=w):
                    dve.wait_ge(mm[st], count)
                    nc.vector.tensor_tensor(
                        z[0:w, ds(2 * i + s + z0, 1), tslice(t)],
                        bank[3 * st + t][0:w, 0:344].rearrange("p (a n) -> p a n", a=1),
                        rstd[0:w, t:t + 1, :], ALU.mult).then_inc(evac[st], 1)
                each_tile(dve, ph, one)

        def win_done(eng):
            for j in (0, 1):
                eng.wait_ge(evac[j], WIN_END[j])

        def gmlp_loads(sp):
            sp.wait_ge(S("x_out"), 16)
            sp.dma_start(gw_nat[:, :, :], A["sgu_w"][0].rearrange("g t s -> t g s"))\
                .then_inc(S("ln_in"), 16)
            sp.wait_ge(S("x_acc"), 48)
            for j, n in enumerate(("sgu_ln_g", "sgu_ln_b")):
                sp.dma_start(ln_gb[:, j, :], A[n][0].partition_broadcast(P)).then_inc(S("ln_in"), 16)
            for hp in (0, 1):
                rows = slice(64 * hp, 64 * hp + 64)
                sp.dma_start(g_bias[rows, :, :], A["sgu_b"][0][hp::2, :].partition_broadcast(64))\
                    .then_inc(S("ln_in"), 16)
                sp.dma_start(g_w00[rows, :], A["sgu_w"][0][hp::2, 0, 0].partition_broadcast(64),
                             allow_slow_non_contiguous=True)\
                    .then_inc(S("ln_in"), 16)

        def gmlp_tensor(pe):
            pe.wait_ge(S("ln_in"), 112)
            pe.wait_ge(S("rms"), 6)
            for g in range(8):
                m = nc.tensor.transpose(bank[6 + g // 4][:, (g % 4) * P:(g % 4 + 1) * P],
                                        gw_nat[:, g, :], ident)
                if g % 4 == 3:
                    m.then_inc(S("gwt"), 1)
            win_done(pe)
            shift_tensor(pe)
            pe.wait_ge(S("gelu"), 1)

            def mixing(n):
                pe.wait_ge(S("shTc"), 2)
                pe.wait_ge(S("vn"), n + 1)
                pe.wait_ge(S("gwT"), 2)
                pe.wait_ge(S("gmix"), max(n - 1, 0))
                for g in range(8):
                    m = nc.tensor.matmul(
                        bank[2 + n % 2][64 * (g % 2):64 * (g % 2) + 64, (g // 2) * P:(g // 2 + 1) * P],
                        vn[:, n % 2, 64 * g:64 * g + 64], gwT[:, g, :], start=True, stop=True)
                m.then_inc(S("mixed"), 1)
            for n in range(9):
                tn = P if n < 8 else NS
                pe.wait_ge(S("vn0"), max(n - 1, 0))
                for j in range(4):
                    m = nc.tensor.transpose(bank[n % 2][0:tn, j * P:(j + 1) * P],
                                            z[:, 12 + j, n * P:n * P + tn], ident)
                m.then_inc(S("vtok"), 1)
                if n > 0:
                    mixing(n - 1)
            pe.wait_ge(S("vn"), 9)
            pe.wait_ge(S("gmix"), 7)
            for j in range(4):
                m = nc.tensor.transpose(bank[2][:, j * NS:(j + 1) * NS],
                                        vn[0:NS, 2, j * P:(j + 1) * P], ident[0:NS, 0:NS])
            m.then_inc(S("mixed"), 1)

        def gmlp_scalar(act):
            win_done(act)
            nc.scalar.activation(z[:, 12:16, :], z[:, 12:16, :], ACT.Gelu_apprx_tanh).then_inc(S("gelu"), 1)
            nc.scalar.activation(z[:, 8:12, :], z[:, 8:12, :], ACT.Gelu_apprx_tanh).then_inc(S("gelu"), 1)
            shift_scalar(act)
            for n in range(9):
                tn = P if n < 8 else NS
                act.wait_ge(S("gvar"), n + 1)
                nc.scalar.activation(g_stat[0:tn, n % 2, 6:7], g_stat[0:tn, n % 2, 7:8], ACT.Sqrt,
                                     bias=eps_t[0:tn, 1:2]).then_inc(S("gelu"), 1)

        def gmlp_vector(dve):
            dve.wait_ge(S("ln_in"), 112)
            for b in (0, 1):
                dve.wait_ge(S("gwt"), b + 1)
                nc.vector.tensor_tensor(gwT[:, 4 * b:4 * b + 4, :],
                                        bank[6 + b][:, :].rearrange("p (g t) -> p g t", g=4),
                                        cst[:, C_TRI:C_TRI + 1, :].to_broadcast([P, 4, P]), ALU.mult)\
                    .then_inc(S("gwT"), 1)
            shift_vector(dve)
            dve.wait_ge(S("gelu"), 2)

            def mixed(n):
                dve.wait_ge(S("mixed"), n + 1)
                b = n % 2
                if n < 8:
                    link(nc.vector.tensor_tensor(
                        g_mix[:, b, :], bank[2 + b][:, :], g_bias[:, :, :].rearrange("p k t -> p (k t)"),
                        ALU.add))
                    us = z[:, 8:12, n * P:(n + 1) * P]
                    nc.vector.tensor_tensor(us, g_mix[:, b, :].rearrange("p (k t) -> p k t", k=4), us,
                                            ALU.mult).then_inc(S("gmix"), 1)
                else:
                    gm = g_mix[:, b, 0:4 * NS].rearrange("p (k t) -> p k t", k=4)
                    link(nc.vector.tensor_tensor(
                        gm, bank[2][:, 0:4 * NS].rearrange("p (k t) -> p k t", k=4),
                        g_w00[:, :].unsqueeze(2).to_broadcast([P, 4, NS]), ALU.mult))
                    link(nc.vector.tensor_tensor(
                        gm, gm, g_bias[:, :, 0:1].to_broadcast([P, 4, NS]), ALU.add))
                    us = z[:, 8:12, SEQ:T]
                    nc.vector.tensor_tensor(us, gm, us, ALU.mult).then_inc(S("gmix"), 1)
            for n in range(9):
                tn, b = (P if n < 8 else NS), n % 2
                v = vn[0:tn, b if n < 8 else 2, :]
                dve.wait_ge(S("vtok"), n + 1)
                link(nc.vector.bn_stats(g_stat[0:tn, b, 0:6], bank[b][0:tn, :]))
                link(nc.vector.bn_aggr(g_stat[0:tn, b, 6:8], g_stat[0:tn, b, 0:6]))
                nc.vector.tensor_copy(g_stat[0:tn, b, 0:1], g_stat[0:tn, b, 6:7]).then_inc(S("gvar"), 1)
                dve.wait_ge(S("gelu"), 2 + n + 1)
                link(nc.vector.reciprocal(g_stat[0:tn, b, 1:2], g_stat[0:tn, b, 6:7]))
                if 2 <= n < 8:
                    dve.wait_ge(S("mixed"), n - 1)
                nc.vector.tensor_scalar(v, bank[b][0:tn, :], g_stat[0:tn, b, 0:1], g_stat[0:tn, b, 1:2],
                                        ALU.subtract, ALU.mult).then_inc(S("vn0"), 1)
                dve.wait_ge(S("vn0"), n + 1)
                link(nc.vector.tensor_tensor(v, v, ln_gb[0:tn, 0, :], ALU.mult))
                nc.vector.tensor_tensor(v, v, ln_gb[0:tn, 1, :], ALU.add).then_inc(S("vn"), 1)
                if n > 0:
                    mixed(n - 1)
            mixed(8)

        def pw(j):
            return P if j < NBT - 1 else NB - (NBT - 1) * P

        def shift_tensor(pe):
            pe.wait_ge(S("gwT"), 2)
            for j in range(NBT):
                m = nc.tensor.transpose(bank[4 + j // 4][0:NS + 1, (j % 4) * P:(j % 4) * P + pw(j)],
                                        z[0:pw(j), ZB[j], SEQ - 1:T], ident[0:pw(j), 0:pw(j)])
                if j % 4 == 3 or j == NBT - 1:
                    m.then_inc(S("sho"), 1)
            pe.wait_ge(S("prep_in"), 16)
            for j in range(NBT):
                m = nc.tensor.transpose(bank[3][0:pw(j), j * NS:(j + 1) * NS],
                                        shift_in[:, j * P:j * P + pw(j)], ident[0:NS, 0:NS])
            m.then_inc(S("sho"), 1)

        def prep_tensor(pe):
            pe.wait_ge(S("gmix"), 9)
            pe.wait_ge(S("vn0"), 9)
            pe.wait_ge(S("prep_in"), 48)
            pe.wait_ge(S("sho_ev"), 5)
            def lora(which):
                for m in range(12 * which, 12 * which + 12):
                    ht, t = m % 12 // 3, m % 3
                    rows = slice(64 * which, 64 * which + 64)
                    if which:
                        pe.wait_ge(S("kmax"), 12)
                    pe.wait_ge(S("lora_ev"), max(m - 7, 0))
                    nc.tensor.matmul(bank[m % 8][:, 0:344], lora_w[rows, ht * P:(ht + 1) * P],
                                     z[rows, 4, tslice(t)], start=True, stop=True)\
                        .then_inc(S("lora"), 1)
            lora(0)
            for m in range(12):
                ht, t = m // 3, m % 3
                pe.wait_ge(S("ksq"), ht + 1)
                pe.wait_ge(S("lora_ev"), min(12, m + 9))
                pe.wait_ge(S("kmax"), max(m - 7, 0))
                nc.tensor.matmul(bank[m % 8][:, 0:344], cst[:, C_BLK, :], diff[:, 4 + ht, tslice(t)],
                                 start=True, stop=True).then_inc(S("ksum"), 1)
            lora(1)

        def shift_scalar(act):
            for b in range(4):
                act.wait_ge(S("sho"), b + 1)
                wd = 512 if b < 3 else NB - 3 * 512
                nc.scalar.activation(shift_out[:, b * 512:b * 512 + wd], bank[4 + b][0:NS + 1, 0:wd],
                                     ACT.Copy).then_inc(S("sho_ev"), 1)

        def prep_scalar(act):
            act.wait_ge(S("mix_p"), 3)
            nc.scalar.activation(z[0:64, 4, :], z[0:64, 4, :], ACT.Tanh).then_inc(S("sho_ev"), 1)
            for ht in range(4):
                act.wait_ge(S("kk0"), ht + 1)
                nc.scalar.activation(diff[:, 4 + ht, :], nkk[:, ht, :], ACT.Square).then_inc(S("ksq"), 1)
            act.wait_ge(S("mix_p"), 15)
            for m in range(24):
                which, ht, t = m // 12, m % 12 // 3, m % 3
                if m == 12:
                    act.wait_ge(S("mix_p"), 21)
                    nc.scalar.activation(z[:, 5, :], z[:, 5, :], ACT.Sigmoid).then_inc(S("sgd"), 1)
                    nc.scalar.activation(z[0:32, 6, :], z[0:32, 6, :], ACT.Sigmoid).then_inc(S("sgd"), 1)
                    act.wait_ge(S("rwkv_out"), 32)
                    act.wait_ge(S("shifted"), 8)
                act.wait_ge(S("lora"), m + 1)
                dst, b = ((sg, "rwkv_w0"), (bvec, "rwkv_a0"))[which]
                nc.scalar.activation(dst[:, ht, tslice(t)], bank[m % 8][:, 0:344], ACT.Sigmoid,
                                     bias=v_col(b, ht)).then_inc(S("lora_ev"), 1)
            act.wait_ge(S("kmax"), 12)
            nc.scalar.activation(diff[:, 4:8, :], diff[:, 4:8, :], ACT.Ln, scale=float(2 ** 20))\
                .then_inc(S("kln"), 1)
            act.wait_ge(S("kln"), 1)
            nc.scalar.activation(diff[:, 4:8, :], diff[:, 4:8, :], ACT.Exp, scale=-0.5,
                                 bias=eps_t[:, 3:4]).then_inc(S("kln"), 1)

        def shift_vector(dve):
            dve.wait_ge(S("sho"), 5)
            nc.vector.tensor_copy(shiftT[:, 0:NBT - 1, :],
                                  bank[3][:, 0:(NBT - 1) * NS].rearrange("p (k t) -> p k t", t=NS))\
                .then_inc(S("shTc"), 1)
            nc.vector.tensor_copy(shiftT[0:32, NBT - 1, :], bank[3][0:32, (NBT - 1) * NS:NBT * NS])\
                .then_inc(S("shTc"), 1)
            dve.wait_ge(S("shTc"), 2)
            for rows, i, n in ((P, 0, 6), (32, 6, 1)):
                d, zz = diff_p[0:rows, i:i + n, :], z[0:rows, i:i + n, :]
                nc.vector.tensor_scalar(d[:, :, 0:1], zz[:, :, 0:1], -1.0, None, ALU.mult)\
                    .then_inc(S("shTc"), 1)
                nc.vector.tensor_tensor(d[:, :, SEQ:T], shiftT[0:rows, 8 + i:8 + i + n, :],
                                        zz[:, :, SEQ:T], ALU.subtract).then_inc(S("shTc"), 1)

        def shift_pool(g):
            TT = nc.gpsimd.tensor_tensor
            g.wait_ge(S("shTc"), 6)
            g.wait_ge(S("sho"), 4)
            for n, i in enumerate((4, 0, 1, 2, 3, 5, 6)):
                rows = P if i < 6 else 32
                d, zz = diff_p[0:rows, i, :], z[0:rows, i, :]
                TT(d[:, 1:SEQ], zz[:, 0:SEQ - 1], zz[:, 1:SEQ], ALU.subtract).then_inc(S("mix_p"), 1)
                g.wait_ge(S("mix_p"), 3 * n + 1)
                TT(d, d, v_col("rwkv_mu", 8 + i)[0:rows].to_broadcast([rows, T]), ALU.mult)\
                    .then_inc(S("mix_p"), 1)
                g.wait_ge(S("mix_p"), 3 * n + 2)
                TT(zz, zz, d, ALU.add).then_inc(S("mix_p"), 1)

        def prep_vector(dve):
            done = 0
            for j0 in (4, 0):
                z0, d0 = ZB[j0], j0
                d, zz = diff[:, d0:d0 + 4, :], z[:, z0:z0 + 4, :]
                if j0 == 0:
                    dve.wait_ge(S("y_out"), 16)
                link(nc.vector.tensor_tensor(d[:, :, 1:SEQ], zz[:, :, 0:SEQ - 1], zz[:, :, 1:SEQ],
                                             ALU.subtract), False)
                link(nc.vector.tensor_scalar(d[:, :, 0:1], zz[:, :, 0:1], -1.0, None, ALU.mult), False)
                link(nc.vector.tensor_tensor(d[:, :, SEQ:T], shiftT[:, j0:j0 + 4, :],
                                             zz[:, :, SEQ:T], ALU.subtract))
                for j in range(4):
                    nc.vector.scalar_tensor_tensor(
                        out=z[:, z0 + j, :], in0=diff[:, d0 + j, :],
                        scalar=v_col("rwkv_mu", j0 + j), in1=z[:, z0 + j, :],
                        op0=ALU.mult, op1=ALU.add).then_inc(S("shifted"), 1)
                    done += 1
                if j0 == 4:
                    dve.wait_ge(S("shifted"), done)
                    dve.wait_ge(S("out"), 16)
                    for ht in range(4):
                        nc.vector.tensor_scalar(nkk[:, ht, :], z[:, 20 + ht, :],
                                                v_col("rwkv_k_k", ht), None,
                                                ALU.mult).then_inc(S("kk0"), 1)
            dve.wait_ge(S("shifted"), done)
            dve.wait_ge(S("gwt"), 2)
            link(nc.vector.memset(scan_mask[:, :], 1.0))
            link(nc.vector.memset(scan_mask[:, 0:SEQ:CH], 0.0), False)
            link(nc.vector.memset(scan_mask[:, SEQ:T], 0.0))
            dve.wait_ge(S("lora_ev"), 12)
            dve.wait_ge(S("mix_p"), 21)
            for ht in range(4):
                link(nc.vector.tensor_tensor_scan(cum[:, ht, :], scan_mask[:, :], sg[:, ht, :], 0.0,
                                                  ALU.mult, ALU.add), False)
                for m in range(3 * ht, 3 * ht + 3):
                    t = m % 3
                    dve.wait_ge(S("ksum"), m + 1)
                    nc.vector.tensor_scalar(diff[:, 4 + ht, tslice(t)], bank[m % 8][:, 0:344],
                                            float(HN), 1e-24, ALU.mult, ALU.max)\
                        .then_inc(S("kmax"), 1)
            dve.wait_ge(S("lora_ev"), 24)
            for ht in range(4):
                link(nc.vector.tensor_scalar(diff[:, ht, :], bvec[:, ht, :], 1.0,
                                             v_col("rwkv_k_a", ht), ALU.subtract, ALU.mult))
                link(nc.vector.scalar_tensor_tensor(out=z[:, 20 + ht, :], in0=diff[:, ht, :],
                                                    scalar=1.0, in1=z[:, 20 + ht, :], op0=ALU.add,
                                                    op1=ALU.mult), False)
            dve.wait_ge(S("kln"), 2)
            link(nc.vector.scalar_tensor_tensor(out=nkk[:, :, :], in0=nkk[:, :, :], scalar=-1.0,
                                                in1=diff[:, 4:8, :], op0=ALU.mult, op1=ALU.mult))
            link(nc.vector.scalar_tensor_tensor(out=bvec[:, :, :], in0=nkk[:, :, :], scalar=-1.0,
                                                in1=bvec[:, :, :], op0=ALU.mult, op1=ALU.mult))

        NLV = LEVELS - 1

        def part(name, g):
            return mats[g // 2][name][:, 2 * (g % 2):2 * (g % 2) + 2, :]

        def pair(b):
            return bank[b][:, 0:256].rearrange("p (j t) -> p j t", j=2)

        def scale_scalar(act, n):
            c = slice(n * P, (n + 1) * P)
            act.wait_ge(S("ediff"), n + 1)
            nc.scalar.activation(ext[:, :, :], ext[:, :, :], ACT.Exp, scale=-DECAY)\
                .then_inc(S("exps"), 1)
            act.wait_ge(S("decm"), 2 * n)
            act.wait_ge(S("stR"), n)
            nc.scalar.activation(dec[:, :, :], cum[:, :, c], ACT.Exp, scale=-DECAY).then_inc(S("exps"), 1)
            act.wait_ge(S("tok"), 3 * n)
            nc.scalar.activation(vstage[:, :, :], z[:, 0:4, c], ACT.Copy).then_inc(S("vst"), 1)
            act.wait_ge(S("stA"), n + 1)
            nc.scalar.activation(ext[:, :, :], cum[:, :, c], ACT.Exp, scale=DECAY).then_inc(S("exps"), 1)

        def chunk_scalar(act, n):
            c = slice(n * P, (n + 1) * P)
            if n == 0:
                scale_scalar(act, 0)
            act.wait_ge(S("tok"), 3 * n + 3)
            act.wait_ge(S("SN"), 4 * n)
            act.wait_ge(S("O"), 2 * n)
            nc.scalar.activation(Vt[:, :], bank[6][:, :], ACT.Copy).then_inc(S("tokc"), 1)
            for q in (0, 1):
                for b in (0, 1):
                    act.wait_ge(S("pair"), 8 * n + 4 * q + b + 1)
                    if b == 0:
                        act.wait_ge(S("LoT"), max(2 * NLV * n + q - 1, 0))
                        act.wait_ge(S("TT0"), 4 * n)
                    nc.scalar.activation(
                        LQ[q][:, :, b::2, :],
                        bank[4 * q + b][:, :].rearrange("p (j a t) -> p a j t", j=2, a=2),
                        ACT.Copy).then_inc(S("LTc"), 1)
            for lv in range(NLV):
                for g in range(4):
                    act.wait_ge(S("pY"), 4 * (NLV * n + lv) + g + 1)
                    nc.scalar.activation(part("Y", g), pair(2 * g + 1 - lv % 2), ACT.Copy)\
                        .then_inc(S("Yc"), 1)
            if n < 7:
                scale_scalar(act, n + 1)
            for ck in (0, 1):
                r, e0 = slice(64 * ck, 64 * ck + 64), 4 * n + 2 * ck
                for q in (0, 1):
                    cols = slice(q * 256, q * 256 + 256)
                    act.wait_ge(S("X"), e0 + q + 1)
                    nc.scalar.activation(Xs[r, cols], bank[4 * q + 3][r, 0:256], ACT.Copy)\
                        .then_inc(S("Xc"), 1)
                for q in (0, 1):
                    cols = slice(q * 256, q * 256 + 256)
                    act.wait_ge(S("U"), e0 + q + 1)
                    act.wait_ge(S("O"), 2 * n)
                    nc.scalar.activation(Us[r, cols], bank[4 * q][r, 0:256], ACT.Copy)\
                        .then_inc(S("Uc"), 1)
            for q in (0, 1):
                act.wait_ge(S("O"), 2 * n + q + 1)
                nc.scalar.activation(
                    nkk[:, 2 * q:2 * q + 2, c],
                    bank[4 * q + 2][:, 0:256].rearrange("p (k t) -> p k t", k=2),
                    ACT.Copy).then_inc(S("Oc"), 1)

        def chunk_pool(g, n):
            for ck in (0, 1):
                g.wait_ge(S("exps"), 3 * n + 2)
                g.wait_ge(S("Sup1"), 4 * n)
                end = 64 * ck + 63
                nc.gpsimd.tensor_tensor(decm[:, ck], dec[:, :, end:end + 1].to_broadcast([P, 4, P]),
                                        cst[:, C_BLK:C_BLK + 1, :].to_broadcast([P, 4, P]),
                                        ALU.mult).then_inc(S("decm"), 1)
            for lv in range(1, NLV + 1):
                for q in (0, 1):
                    if lv == 1:
                        g.wait_ge(S("LTc"), 4 * n + 2 * q + 2)
                    if lv == 2:
                        nc.gpsimd.tensor_tensor(mats[q]["QBT"], mats[q]["QBT"],
                                                cst[:, C_INC:C_INC + 1, :].to_broadcast([P, 4, P]),
                                                ALU.mult).then_inc(S("QBm"), 1)
                    if NLV * n + lv > 1:
                        g.wait_ge(S("pY"), 4 * (NLV * n + lv - 2) + 2 * q + 2)
                    nc.gpsimd.tensor_tensor(mats[q]["LoT"][:, :, :], mats[q]["LT"][:, :, :],
                                            cst[:, C_LVL + lv:C_LVL + lv + 1, :].to_broadcast([P, 4, P]),
                                            ALU.mult).then_inc(S("LoT"), 1)

        def scale_vector(dve, n):
            c = slice(n * P, (n + 1) * P)
            TT = nc.vector.tensor_tensor
            dve.wait_ge(S("stB"), 2 * n)
            TT(ext[:, :, :], cum[:, :, c], sg[:, :, c], ALU.subtract).then_inc(S("ediff"), 1)
            dve.wait_ge(S("exps"), 3 * n + 1)
            dve.wait_ge(S("pair"), 8 * n)
            dve.wait_ge(S("tok"), 3 * n)
            dve.wait_ge(S("O"), max(2 * n - 2, 0))
            TT(AR[n % 2][:, 0, :, :], nkk[:, :, c], ext[:, :, :], ALU.mult).then_inc(S("stA"), 1)
            dve.wait_ge(S("exps"), 3 * n + 2)
            TT(AR[n % 2][:, 1, :, :], z[:, 16:20, c], dec[:, :, :], ALU.mult).then_inc(S("stR"), 1)
            dve.wait_ge(S("exps"), 3 * n + 3)
            TT(BK[:, 0, :, :], bvec[:, :, c], ext[:, :, :], ALU.mult).then_inc(S("stB"), 1)
            TT(BK[:, 1, :, :], z[:, 20:24, c], ext[:, :, :], ALU.mult).then_inc(S("stB"), 1)

        def chunk_vector(dve, n):
            TT = nc.vector.tensor_tensor
            if n == 0:
                scale_vector(dve, 0)
            for j, dst in enumerate((Bt, Kt)):
                dve.wait_ge(S("tok"), 3 * n + j + 1)
                dve.wait_ge(S("SN"), 4 * n)
                nc.vector.tensor_copy(dst[:, :], bank[4 + j][:, :]).then_inc(S("tokc"), 1)

            def pv(b, a):
                return bank[b][:, :].rearrange("p (j a t) -> p j a t", j=2, a=2)[:, :, a, :]
            for q in (0, 1):
                m = mats[q]
                msk = lambda k: cst[:, k:k + 1, :].to_broadcast([P, 2, P])
                for b in (0, 1):
                    hs = slice(b, 4, 2)
                    dve.wait_ge(S("LTc"), 4 * n + 2 * q + b + 1)
                    if b == 0:
                        dve.wait_ge(S("U"), 4 * n)
                        dve.wait_ge(S("X"), 4 * n)
                        dve.wait_ge(S("TTa"), 4 * NLV * n)
                    TT(m["TT"][:, hs, :], m["LT"][:, hs, :], msk(C_LVL), ALU.mult)\
                        .then_inc(S("TT0"), 1)
                    dve.wait_ge(S("TT0"), 4 * n + 2 * q + b + 1)
                    TT(m["TT"][:, hs, :], m["TT"][:, hs, :], msk(C_ID), ALU.add).then_inc(S("TT1"), 1)
                for b in (0, 1):
                    hs = slice(b, 4, 2)
                    dve.wait_ge(S("pair"), 8 * n + 4 * q + 2 + b + 1)
                    TT(m["MT"][:, hs, :], pv(4 * q + 2 + b, 0), msk(C_STR), ALU.mult)\
                        .then_inc(S("pKr"), 1)
                    TT(m["QKT"][:, hs, :], pv(4 * q + 2 + b, 1), msk(C_INC), ALU.mult)\
                        .then_inc(S("pKr"), 1)
            for lv in range(NLV):
                for g in range(4):
                    dve.wait_ge(S("Tt"), 4 * (NLV * n + lv) + g + 1)
                    nc.vector.tensor_copy(part("Ti", g), pair(2 * g + lv % 2)).then_inc(S("Tc"), 1)
                for g in range(4):
                    dve.wait_ge(S("pD"), 4 * (NLV * n + lv) + g + 1)
                    TT(part("TT", g), part("TT", g), pair(2 * g + lv % 2), ALU.add)\
                        .then_inc(S("TTa"), 1)
            if n < 7:
                scale_vector(dve, n + 1)
            else:
                for ht in range(4):
                    nc.vector.scalar_tensor_tensor(
                        out=cum[:, ht, :], in0=z[:, 16 + ht, :], scalar=v_col("rwkv_r_k", ht),
                        in1=z[:, 20 + ht, :], op0=ALU.mult, op1=ALU.mult).then_inc(S("bo2"), 1)
            for ck in (0, 1):
                e0 = 4 * n + 2 * ck
                for q in (0, 1):
                    hs = slice(2 * q, 2 * q + 2)
                    dve.wait_ge(S("SN"), e0 + q + 1)
                    dve.wait_ge(S("Sup1"), max(e0 + q - 1, 0))
                    dve.wait_ge(S("O"), 2 * n)
                    TT(st_T[:, (2 * n + ck + 1) % 3, hs, :], st_T[:, (2 * n + ck) % 3, hs, :],
                       bank[4 * q + 1][:, 0:256].rearrange("p (k v) -> p k v", k=2), ALU.add)\
                        .then_inc(S("Sup0"), 1)
                for q in (0, 1):
                    hs = slice(2 * q, 2 * q + 2)
                    new = st_T[:, (2 * n + ck + 1) % 3, hs, :]
                    dve.wait_ge(S("Sup0"), e0 + q + 1)
                    dve.wait_ge(S("decm"), 2 * n + ck + 1)
                    nc.vector.scalar_tensor_tensor(out=new, in0=new, scalar=float(HN),
                                                   in1=decm[:, ck, hs, :], op0=ALU.mult,
                                                   op1=ALU.mult).then_inc(S("Sup1"), 1)

        def chunk_tensor(pe, n):
            mmul = nc.tensor.matmul
            heads = lambda q: [(j, (4 * q + j) // 2, (4 * q + j) % 2) for j in range(4)]
            pe.wait_ge(S("stB"), 2 * n + 2)
            pe.wait_ge(S("Oc"), 2 * n)
            pe.wait_ge(S("Sup0"), 4 * n)
            for j, src in enumerate((BK[:, 0], BK[:, 1], vstage[:, :, :])):
                if j == 2:
                    pe.wait_ge(S("vst"), n + 1)
                for ht in range(4):
                    m = nc.tensor.transpose(bank[4 + j][:, ht * P:(ht + 1) * P], src[:, ht, :], ident)
                m.then_inc(S("tok"), 1)
            for q in (0, 1):
                if q == 1:
                    pe.wait_ge(S("tokc"), 3 * n + 3)
                for side in (0, 1):
                    for j, ht, hp in sorted(heads(q), key=lambda x: x[2]):
                        r = slice(64 * hp, 64 * hp + 64)
                        m = mmul(bank[4 * q + 2 * side + hp][:, (j // 2) * 256:(j // 2) * 256 + 256],
                                 BK[r, side, ht, :], AR[n % 2][r, :, ht, :], start=True, stop=True)
                        if j >= 2:
                            m.then_inc(S("pair"), 1)
            for lv in range(NLV):
                for g in range(4):
                    q = g // 2
                    if lv == 0:
                        pe.wait_ge(S("TT1"), 4 * n + 2 * q + 2)
                        pe.wait_ge(S("pKr"), 8 * n + 4 * q + 4)
                        pe.wait_ge(S("LTc"), 4 * n + 2 * q + 2)
                    else:
                        pe.wait_ge(S("TTa"), 4 * (NLV * n + lv - 1) + g + 1)
                    for j in (0, 1):
                        m = nc.tensor.transpose(bank[2 * g + lv % 2][:, j * P:(j + 1) * P],
                                                part("TT", g)[:, j, :], ident)
                    m.then_inc(S("Tt"), 1)
                for g in range(4):
                    pe.wait_ge(S("LoT"), 2 * (NLV * n + lv) + g // 2 + 1)
                    pe.wait_ge(S("Tc"), 4 * (NLV * n + lv) + g + 1)
                    for j in (0, 1):
                        m = mmul(bank[2 * g + 1 - lv % 2][:, j * P:(j + 1) * P],
                                 part("LoT", g)[:, j, :], part("Ti", g)[:, j, :], start=True, stop=True)
                    m.then_inc(S("pY"), 1)
                for g in range(4):
                    pe.wait_ge(S("Yc"), 4 * (NLV * n + lv) + g + 1)
                    for j in (0, 1):
                        m = mmul(bank[2 * g + lv % 2][:, j * P:(j + 1) * P],
                                 part("Y", g)[:, j, :], part("TT", g)[:, j, :], start=True, stop=True)
                    m.then_inc(S("pD"), 1)
            pe.wait_ge(S("TTa"), 4 * NLV * (n + 1))

            def out_v(q):
                pe.wait_ge(S("Oc"), max(2 * n + q - 1, 0))
                for j, ht, hp in heads(q):
                    hc = slice((4 * q + j) * 64, (4 * q + j + 1) * 64)
                    mmul(bank[4 * q + 2][64 * hp:64 * hp + 64, (j // 2) * P:(j // 2 + 1) * P],
                         Vt[:, hc], mats[q]["QKT"][:, j, :], start=j < 2, stop=False,
                         skip_group_check=True)

            def out_u(q):
                pe.wait_ge(S("QBm"), 2 * n + q + 1)
                for j, ht, hp in heads(q):
                    hc = slice((4 * q + j) * 64, (4 * q + j + 1) * 64)
                    mmul(bank[4 * q + 2][64 * hp:64 * hp + 64, (j // 2) * P:(j // 2 + 1) * P],
                         Us[:, hc], mats[q]["QBT"][:, j, :], start=False, stop=False,
                         skip_group_check=True)

            def out_state(q, ck):
                for k in (0, 1):
                    m = mmul(bank[4 * q + 2][:, k * P + 64 * ck:k * P + 64 * ck + 64],
                             st_T[:, (2 * n + ck) % 3, 2 * q + k, :],
                             AR[n % 2][:, 1, 2 * q + k, 64 * ck:64 * ck + 64],
                             start=False, stop=ck == 1, skip_group_check=True)
                return m
            for ck in (0, 1):
                t, e0 = slice(64 * ck, 64 * ck + 64), 4 * n + 2 * ck
                for q in (0, 1):
                    pe.wait_ge(S("Sup1"), max(e0 + q - 1, 0))
                    pe.wait_ge(S("Xc"), max(e0 - 1 + q, 0))
                    if n == 0 and ck == 0:
                        pe.wait_ge(S("st0"), 2)
                    for k in (0, 1):
                        ht = 2 * q + k
                        mmul(bank[4 * q + 3][t, k * P:(k + 1) * P], AR[n % 2][:, 0, ht, t],
                             st_T[:, (2 * n + ck) % 3, ht, :], start=True, stop=False)
                        for hp in (0, 1):
                            j = 2 * k + hp
                            hc = slice((2 * ht + hp) * 64, (2 * ht + hp + 1) * 64)
                            m = mmul(bank[4 * q + 3][t, j * 64:(j + 1) * 64], mats[q]["MT"][:, j, t],
                                     Vt[:, hc], start=False, stop=hp == 1)
                    m.then_inc(S("X"), 1)
                if ck == 0:
                    out_v(0)
                for q in (0, 1):
                    pe.wait_ge(S("Xc"), e0 + q + 1)
                    pe.wait_ge(S("Uc"), max(e0 + q - 1, 0))
                    for j, ht, hp in heads(q):
                        hc = slice((4 * q + j) * 64, (4 * q + j + 1) * 64)
                        m = mmul(bank[4 * q][t, j * 64:(j + 1) * 64], mats[q]["TT"][t, j, t], Xs[t, hc],
                                 start=True, stop=True)
                    m.then_inc(S("U"), 1)
                if ck == 0:
                    out_v(1)
                for q in (0, 1):
                    pe.wait_ge(S("Uc"), e0 + q + 1)
                    pe.wait_ge(S("Sup0"), max(e0 + q - 1, 0))
                    for k in (0, 1):
                        hc = slice((2 * q + k) * P, (2 * q + k + 1) * P)
                        o = bank[4 * q + 1][:, k * P:(k + 1) * P]
                        mmul(o, Kt[t, hc], Vt[t, hc], start=True, stop=False)
                        m = mmul(o, Bt[t, hc], Us[t, hc], start=False, stop=True)
                    m.then_inc(S("SN"), 1)
                if ck == 0:
                    for q in (0, 1):
                        out_state(q, 0)
            for q in (0, 1):
                out_u(q)
                out_state(q, 1).then_inc(S("O"), 1)

        SMP = [lambda ht: smp_w[:, ht, :], lambda ht: nkk[:, ht, SEQ:T], lambda ht: bvec[:, ht, SEQ:T],
               lambda ht: z[:, 20 + ht, SEQ:T], lambda ht: z[:, 16 + ht, SEQ:T],
               lambda ht: z[:, ht, SEQ:T]]

        def sample_loads(sp):
            sp.wait_ge(S("Oc"), 16)
            sp.dma_start(smp_S[:, :, :], A["state_rwkv"][0].rearrange("b h (w v) k -> (b h w) v k", w=2))\
                .then_inc(S("post_in"), 16)
            sp.wait_ge(S("decm"), 16)
            sp.dma_start(g2_w[:, 0, :], A["rwkv_g2"][0][0:P, :]).then_inc(S("post_in"), 16)
            sp.dma_start(g2_w[0:32, 1, :], A["rwkv_g2"][0][P:P + 32, :]).then_inc(S("post_in"), 16)
            sp.wait_ge(S("smp_a"), 8)
            sp.dma_start(smp_d.rearrange("i b n -> b i n"), smp_n[:, :, :]).then_inc(S("smp_in"), 16)
            sp.wait_ge(S("smp_in"), 16)
            for w in (0, 1):
                sp.dma_start(smp_v[w::2, 0:5, :], smp_d[0:5].rearrange("i b (h d) -> (b h) i d", h=HEADS))\
                    .then_inc(S("smp_in"), 16)
            sp.dma_start(smp_v[:, 5, 0:32], smp_d[5].rearrange("b (h d) -> (b h) d", d=32))\
                .then_inc(S("smp_in"), 16)
            sp.wait_ge(S("smp_a"), 2)
            for hp in (0, 1):
                r = slice(64 * hp, 64 * hp + 64)
                sp.dma_start(O["state_rwkv_prompt"][0, 0, hp::2].rearrange("h v k -> v h k"),
                             st_out[r, :, r]).then_inc(S("rwkv_out"), 16)
            sp.wait_ge(S("smp_v"), 1)
            sp.dma_start(smp_od.rearrange("b (h d) -> (b h) d", d=32), smp_o[:, 1, :])\
                .then_inc(S("smp_in"), 16)
            sp.dma_start(O["state_rwkv_sample"][0].rearrange("b h (w v) k -> (b h w) v k", w=2),
                         smp_S[:, :, :]).then_inc(S("rwkv_out"), 16)
            sp.wait_ge(S("smp_in"), 80)
            sp.dma_start(smp_on[:, :], smp_od).then_inc(S("smp_in"), 16)

        def post_scalar(act):
            act.wait_ge(S("Oc"), 16)
            act.dma_start(mem_n[:, :, :], A["mem_prompt"][0].rearrange("(m p) d -> p m d", p=P))\
                .then_inc(S("mem_in"), 16)
            nc.scalar.activation(smp_w[:, :, :], sg[:, :, SEQ:T], ACT.Exp, scale=-DECAY)\
                .then_inc(S("smp_a"), 1)
            act.wait_ge(S("smp_t"), 1)
            nc.scalar.activation(st_out[:, :, :], bank[6][:, :].rearrange("p (k n) -> p k n", k=4),
                                 ACT.Copy).then_inc(S("smp_a"), 1)
            for i in range(6):
                act.wait_ge(S("smp_t"), i + 2)
                nc.scalar.activation(smp_n[:, i, :], bank[i][0:NS, :], ACT.Copy).then_inc(S("smp_a"), 1)
            for m in range(13):
                if m < 12:
                    ht, t = m % 4, m // 4
                    act.wait_ge(S("gn_c"), m + 1)
                    act.wait_ge(S("gn_v"), max(m - 2, 0))
                    nc.scalar.activation(gn_sq[:, m % 3, :], nkk[:, ht, tslice(t)], ACT.Square)\
                        .then_inc(S("gn_q"), 1)
                if m > 0:
                    ht, t = (m - 1) % 4, (m - 1) // 4
                    act.wait_ge(S("gn_v"), m)
                    nc.scalar.activation(sg[:, ht, tslice(t)], bank[2 + (m - 1) % 2][:, 0:344], ACT.Ln,
                                         bias=eps_t[:, 2:3]).then_inc(S("gn_l"), 1)
            act.wait_ge(S("gn_l"), 12)
            nc.scalar.activation(sg[:, :, :], sg[:, :, :], ACT.Exp, scale=-0.5).then_inc(S("gn_l"), 1)
            act.dma_start(ya_in[:, :, :], y_save).then_inc(S("ya_in"), 16)
            act.wait_ge(S("ya_in"), 16)
            act.wait_ge(S("rwkv_out"), 80)
            nc.scalar.activation(y_hi[:, 0:4, :], ya_in[:, :, :], ACT.Copy).then_inc(S("yb_hi"), 1)
            for m in range(12):
                ht, t = m % 4, m // 4
                act.wait_ge(S("yb"), m + 1)
                nc.scalar.activation(y_hi[:, 4 + ht, tslice(t)], nkk[:, ht, tslice(t)], ACT.Copy)\
                    .then_inc(S("yb_hi"), 1)
            act.dma_start(x[:, :, :], x_save).then_inc(S("x_back"), 16)

        def post_tensor(pe):
            pe.wait_ge(S("Sup1"), 32)
            pe.wait_ge(S("Oc"), 16)
            for ht in range(4):
                m = nc.tensor.transpose(bank[6][:, ht * P:(ht + 1) * P], st_T[:, 16 % 3, ht, :], ident)
            m.then_inc(S("smp_t"), 1)
            pe.wait_ge(S("smp_a"), 1)
            for i in range(6):
                for ht in range(4):
                    m = nc.tensor.transpose(bank[i][0:NS, ht * P:(ht + 1) * P], SMP[i](ht), ident)
                m.then_inc(S("smp_t"), 1)
            blk = cst[:, C_BLK, :]
            pe.wait_ge(S("smp_a"), 8)
            for m in range(13):
                if m == 8:
                    pe.wait_ge(S("smp_in"), 96)
                    pe.wait_ge(S("smp_a"), 8)
                    for ht in range(4):
                        tr = nc.tensor.transpose(bank[7][:, ht * NS:(ht + 1) * NS],
                                                smp_on[:, ht * P:(ht + 1) * P], ident[0:NS, 0:NS])
                    tr.then_inc(S("smp_t"), 1)
                    pe.wait_ge(S("smp_v"), 2)
                if m < 12:
                    ht, t = m % 4, m // 4
                    pe.wait_ge(S("gn_c"), max(m - 1, 0))
                    nc.tensor.matmul(bank[m % 2][:, 0:344], blk, nkk[:, ht, tslice(t)],
                                     start=True, stop=True).then_inc(S("gn_m"), 1)
                if m > 0:
                    ht, t = (m - 1) % 4, (m - 1) // 4
                    pe.wait_ge(S("gn_q"), m)
                    pe.wait_ge(S("gn_l"), max(m - 2, 0))
                    nc.tensor.matmul(bank[2 + (m - 1) % 2][:, 0:344], blk, gn_sq[:, (m - 1) % 3, :],
                                     start=True, stop=True).then_inc(S("gn_v"), 1)
            pe.wait_ge(S("sgd"), 2)
            pe.wait_ge(S("post_in"), 48)
            pe.wait_ge(S("smp_a"), 2)
            for m in range(12):
                ht, t = m % 4, m // 4
                pe.wait_ge(S("bo2"), 4)
                pe.wait_ge(S("bo2"), 4 + max(m - 1, 0))
                nc.tensor.matmul(bank[4 + m % 2][:, 0:344], blk, cum[:, ht, tslice(t)],
                                 start=True, stop=True).then_inc(S("bo1"), 1)
                pe.wait_ge(S("yb"), max(m - 1, 0))
                nc.tensor.matmul(bank[6 + m % 2][:, 0:344], g2_w[:, 0, ht * P:(ht + 1) * P],
                                 z[:, 5, tslice(t)], start=True, stop=False)
                nc.tensor.matmul(bank[6 + m % 2][:, 0:344], g2_w[0:32, 1, ht * P:(ht + 1) * P],
                                 z[0:32, 6, tslice(t)], start=False, stop=True).then_inc(S("g2"), 1)

        def sample_vector(dve):
            TT = nc.vector.tensor_tensor
            dve.wait_ge(S("post_in"), 48)
            dve.wait_ge(S("smp_in"), 64)
            full = [P, 32, HN]
            over_v = lambda i: smp_v[:, i:i + 1, :].to_broadcast(full)
            over_k = lambda a: a.unsqueeze(2).to_broadcast(full)
            link(TT(smp_t[:, :, :], smp_S[:, :, :], over_v(1), ALU.mult))
            link(nc.vector.tensor_reduce(smp_o[:, 0, :], smp_t[:, :, :], AX.X, ALU.add), False)
            link(TT(smp_S[:, :, :], smp_S[:, :, :], over_v(0), ALU.mult))
            link(TT(smp_t[:, :, :], over_k(smp_o[:, 0, :]), over_v(2), ALU.mult))
            link(TT(smp_S[:, :, :], smp_S[:, :, :], smp_t[:, :, :], ALU.add))
            link(TT(smp_t[:, :, :], over_k(smp_v[:, 5, 0:32]), over_v(3), ALU.mult))
            link(TT(smp_S[:, :, :], smp_S[:, :, :], smp_t[:, :, :], ALU.add))
            link(TT(smp_t[:, :, :], smp_S[:, :, :], over_v(4), ALU.mult))
            nc.vector.tensor_reduce(smp_o[:, 1, :], smp_t[:, :, :], AX.X, ALU.add)\
                .then_inc(S("smp_v"), 1)
            dve.wait_ge(S("smp_t"), 8)
            nc.vector.tensor_copy(nkk[:, :, SEQ:T], bank[7][:, 0:4 * NS].rearrange(
                "p (k t) -> p k t", k=4)).then_inc(S("smp_v"), 1)
            dve.wait_ge(S("smp_v"), 2)

        def post_vector(dve):
            TT, STT = nc.vector.tensor_tensor, nc.vector.scalar_tensor_tensor
            for m in range(12):
                ht, t = m % 4, m // 4
                if m == 8:
                    sample_vector(dve)
                dve.wait_ge(S("gn_m"), m + 1)
                TT(nkk[:, ht, tslice(t)], nkk[:, ht, tslice(t)], bank[m % 2][:, 0:344], ALU.subtract)\
                    .then_inc(S("gn_c"), 1)
            dve.wait_ge(S("gn_l"), 13)
            for ht in range(4):
                link(STT(out=nkk[:, ht, :], in0=nkk[:, ht, :], scalar=v_col("rwkv_gn_g", ht),
                         in1=sg[:, ht, :], op0=ALU.mult, op1=ALU.mult))
            for m in range(12):
                ht, t = m % 4, m // 4
                o = nkk[:, ht, tslice(t)]
                dve.wait_ge(S("bo1"), m + 1)
                STT(out=cum[:, ht, tslice(t)], in0=bank[4 + m % 2][:, 0:344], scalar=float(HN),
                    in1=z[:, ht, tslice(t)], op0=ALU.mult, op1=ALU.mult).then_inc(S("bo2"), 1)
                dve.wait_ge(S("bo2"), 4 + m + 1)
                link(STT(out=o, in0=o, scalar=v_col("rwkv_gn_b", ht), in1=cum[:, ht, tslice(t)],
                         op0=ALU.add, op1=ALU.add))
                dve.wait_ge(S("g2"), m + 1)
                TT(o, o, bank[6 + m % 2][:, 0:344], ALU.mult).then_inc(S("yb"), 1)

        def post_pool(g):
            g.wait_ge(S("yb"), 1)
            g.wait_ge(S("yb_hi"), 1)
            nc.gpsimd.tensor_tensor(y_lo[:, 0:4, :], ya_in[:, :, :], y_hi[:, 0:4, :].bitcast(F),
                                    ALU.subtract).then_inc(S("yb_lo"), 1)
            for m in range(12):
                ht, t = m % 4, m // 4
                g.wait_ge(S("yb_hi"), m + 2)
                nc.gpsimd.tensor_tensor(y_lo[:, 4 + ht, tslice(t)], nkk[:, ht, tslice(t)],
                                        y_hi[:, 4 + ht, tslice(t)].bitcast(F), ALU.subtract)\
                    .then_inc(S("yb_lo"), 1)

        def mem_scalar_a(act):
            act.wait_ge(S("mem_in"), 16)
            for m in (0, 1):
                act.wait_ge(S("msq"), m)
                nc.scalar.activation(mem_sq[:, :], mem_n[:, m, :], ACT.Square,
                                     accum_out=mem_st[:, m, 0:1]).then_inc(S("msq"), 1)
            act.wait_ge(S("msq"), 2)
            nc.scalar.activation(mem_st[:, :, 1:2], mem_st[:, :, 0:1], ACT.Sqrt, scale=1.0 / D,
                                 bias=eps_t[:, 0:1]).then_inc(S("msq"), 1)

        def mem_vector_a(dve):
            dve.wait_ge(S("msq"), 3)
            link(nc.vector.reciprocal(mem_st[:, :, 2:3], mem_st[:, :, 1:2]))
            for m in (0, 1):
                nc.vector.tensor_scalar(mem_n[:, m, :], mem_n[:, m, :], mem_st[:, m, 2:3], None,
                                        ALU.mult).then_inc(S("mnorm"), 1)

        def mem_tensor_a(pe):
            pe.wait_ge(S("mnorm"), 2)
            for j in (0, 1):
                pe.wait_ge(evac[j], memk["mm0"][j])
            for k in range(KD):
                for m in (0, 1):
                    i = nc.tensor.transpose(bank[k // 2][:, (k % 2) * 256 + m * P:(k % 2) * 256 + (m + 1) * P],
                                            mem_n[:, m, k * P:(k + 1) * P], ident)
                if k % 2:
                    i.then_inc(S("memT"), 1)

        def mem_scalar_b(act):
            for k in range(KD):
                act.wait_ge(S("memT"), k // 2 + 1)
                if k % 2:
                    act.wait_ge(S("mem_lo"), k)
                nc.scalar.activation(mem_hi[:, k, :], bank[k // 2][:, (k % 2) * 256:(k % 2) * 256 + 256],
                                     ACT.Copy, scale=v_col("mem_norm", k)).then_inc(S("mem_hi"), 1)

        def mem_vector_b(dve):
            for k in range(KD):
                dve.wait_ge(S("mem_hi"), k + 1)
                nc.vector.scalar_tensor_tensor(
                    out=mem_lo[:, k, :], in0=bank[k // 2][:, (k % 2) * 256:(k % 2) * 256 + 256],
                    scalar=v_col("mem_norm", k), in1=mem_hi[:, k, :].bitcast(F),
                    op0=ALU.mult, op1=ALU.subtract).then_inc(S("mem_lo"), 1)

        def plain_evac(dve, ph, dst, normed=False):
            def one(i, s, st, t, count):
                t0, tn = ph["toks"][t]
                dve.wait_ge(mm[st], count)
                o = dst[:, ds(2 * i + s, 1), t0:t0 + tn]
                src = bank[3 * st + t][:, 0:tn].rearrange("p (a n) -> p a n", a=1)
                if normed:
                    nc.vector.tensor_tensor(o, src, rstd[:, t:t + 1, :], ALU.mult).then_inc(evac[st], 1)
                else:
                    nc.vector.tensor_copy(o, src).then_inc(evac[st], 1)
            each_tile(dve, ph, one)

        def nat_tensor(pe):
            for j in (0, 1):
                pe.wait_ge(evac[j], memv["mm1"][j])
            for m in (0, 1):
                pe.wait_ge(S("nat_a"), 2 * m)
                pe.wait_ge(S("nat_b"), 2 * m)
                for g, src in ((0, kT), (2, vT)):
                    for k in range(KD):
                        i = nc.tensor.transpose(bank[g + k // 4][:, (k % 4) * P:(k % 4 + 1) * P],
                                                src[:, k, m * P:(m + 1) * P], ident)
                        if k % 4 == 3:
                            i.then_inc(S("nat"), 1)

        def nat_scalar(act):
            for m in (0, 1):
                for b in (0, 1):
                    act.wait_ge(S("nat"), 4 * m + b + 1)
                    nc.scalar.activation(mk_n[:, m, b * 512:b * 512 + 512], bank[b][:, :], ACT.Copy)\
                        .then_inc(S("nat_a"), 1)

        def nat_vector(dve):
            for m in (0, 1):
                for b in (0, 1):
                    dve.wait_ge(S("nat"), 4 * m + 2 + b + 1)
                    nc.vector.tensor_copy(v_n[:, m, b * 512:b * 512 + 512], bank[2 + b][:, :])\
                        .then_inc(S("nat_b"), 1)

        def nat_out(sp):
            sp.wait_ge(S("nat_a"), 4)
            sp.dma_start(O["mem_k_prompt"][0, 0].rearrange("(m p) h d -> p m (h d)", p=P), mk_n[:, :, :])\
                .then_inc(S("out3"), 16)
            sp.wait_ge(S("nat_b"), 4)
            sp.dma_start(O["mem_v_prompt"][0, 0].rearrange("(m p) h d -> p m (h d)", p=P), v_n[:, :, :])\
                .then_inc(S("out3"), 16)

        SC = float(XD) ** -0.5
        cache_in = [S("cache_in0"), S("cache_in1")]

        def cache_loads(sp, name, n):
            if n < 2:
                sp.wait_ge(S("out3"), 32) if name == "k" else sp.wait_ge(S("s_dot"), 8 * (7 + n))
            else:
                sp.wait_ge(S("s_dot") if name == "k" else S("o_smp"), (8 if name == "k" else 1) * (n - 1))
            sp.dma_start(cache[n % 2][:, :, :],
                         A[f"cache_mem_{name}"][0, n].rearrange("(m p) h d -> p m (h d)", p=P))\
                .then_inc(cache_in[n % 2], 16)

        def att_scores_pe(pe, n):
            c = slice(n * P, (n + 1) * P)
            pe.wait_ge(S("exp"), 4 * n)
            for h in range(XH):
                for d in (0, 1):
                    m = nc.tensor.matmul(bank[h // 2][:, (h % 2) * 256:(h % 2) * 256 + 256],
                                         qT[:, 2 * h + d, c], kT[:, 2 * h + d, :],
                                         start=d == 0, stop=d == 1)
                if h % 2:
                    m.then_inc(S("score"), 1)

        def att_query_pe(pe, n):
            pe.wait_ge(S("s_dot"), 8 * n)
            for k in range(KD):
                m = nc.tensor.matmul(bank[6 + k // 4][:, (k % 4) * P:(k % 4 + 1) * P],
                                     qT[:, k, SEQ + n:SEQ + n + 1].to_broadcast([P, P]), ident,
                                     start=True, stop=True)
            m.then_inc(S("q_bc"), 1)

        def att_out_pe(pe, n):
            b = n % 2
            pe.wait_ge(S("pnorm"), n + 1)
            pe.wait_ge(S("pT"), 2 * n)
            for h in range(XH):
                for m in (0, 1):
                    i = nc.tensor.transpose(bank[2 + h // 2][:, (h % 2) * 256 + m * P:(h % 2) * 256 + (m + 1) * P],
                                            prob[b][:, h, m * P:(m + 1) * P], ident)
                if h % 2:
                    i.then_inc(S("pTt"), 1)
            pe.wait_ge(S("o_lo"), 2 * n)
            for g in (0, 1):
                pe.wait_ge(S("pT"), 2 * n + g + 1)
                for h in (2 * g, 2 * g + 1):
                    for d in (0, 1):
                        for m in (0, 1):
                            i = nc.tensor.matmul(bank[4 + g][:, ((h % 2) * 2 + d) * P:((h % 2) * 2 + d + 1) * P],
                                                 v_n[:, m, h * XD + d * P:h * XD + (d + 1) * P],
                                                 probT[b][:, 2 * h + m, :], start=m == 0, stop=m == 1)
                i.then_inc(S("pv"), 1)

        def att_tensor(pe):
            for j in (0, 1):
                pe.wait_ge(evac[j], xaq["mm1"][j])
            for n in range(9):
                if n < 8:
                    att_scores_pe(pe, n)
                if n < 4:
                    att_query_pe(pe, 2 * n)
                if n == 4:
                    pe.wait_ge(S("s_dot"), 64)
                    for m in (0, 1):
                        i = nc.tensor.transpose(bank[6][0:32, m * P:(m + 1) * P], s_smp[:, :, m], ident)
                    i.then_inc(S("srow"), 1)
                if n:
                    att_out_pe(pe, n - 1)
                if n < 4:
                    att_query_pe(pe, 2 * n + 1)
                if n == 4:
                    pe.wait_ge(S("srow_v"), 2)
                    for m in (0, 1):
                        i = nc.tensor.transpose(bank[7][:, m * 32:(m + 1) * 32],
                                                p_smp[:, m * P:(m + 1) * P], ident[0:32, 0:32])
                    i.then_inc(S("srow"), 1)
                for b in (2 * n - 10, 2 * n - 9) if n > 4 else ():
                    pe.wait_ge(S("srow_v"), 4)
                    pe.wait_ge(cache_in[b % 2], 64 + 16 * (b // 2 + 1))
                    for h in range(XH):
                        for m in (0, 1):
                            i = nc.tensor.matmul(
                                bank[6 + h // 2][0:NS, (h % 2) * XD:(h % 2 + 1) * XD],
                                pT_smp[m].rearrange("p b x -> p (b x)")[
                                    :, 32 * b + 8 * h:32 * b + 8 * h + NS], cache[b % 2][:, m, h * XD:(h + 1) * XD],
                                start=b == 0 and m == 0 and h % 2 == 0, stop=b == NS - 1 and m == 1,
                                skip_group_check=True)
                    i.then_inc(S("o_smp"), 1)
            pe.wait_ge(S("o_rows"), 2)
            pe.wait_ge(S("o_hi"), 16)
            pe.wait_ge(S("exp"), 32)
            for k in range(KD):
                i = nc.tensor.transpose(bank[0][:, k * NS:(k + 1) * NS], o_rows[:, k * P:(k + 1) * P],
                                        ident[0:NS, 0:NS])
            i.then_inc(S("srow"), 1)

        def att_scalar(act):
            for n in range(9):
                if n < 8:
                    b = n % 2
                    act.wait_ge(S("nmax"), n + 1)
                    act.wait_ge(S("pTt"), 2 * max(n - 1, 0))
                    act.wait_ge(S("pnorm"), max(n - 1, 0))
                    for h in range(XH):
                        nc.scalar.activation(prob[b][:, h, :], bank[h // 2][:, (h % 2) * 256:(h % 2) * 256 + 256],
                                             ACT.Exp, scale=SC, bias=att[:, b, 0, h:h + 1],
                                             accum_out=att[:, b, 1, h:h + 1]).then_inc(S("exp"), 1)
                if n == 4:
                    act.wait_ge(S("srow_v"), 1)
                    nc.scalar.activation(p_smp[:, :], bank[6][0:32, 0:NMEM], ACT.Exp, scale=SC,
                                         bias=s_row[:, 0:1], accum_out=s_row[:, 1:2])\
                        .then_inc(S("srow_e"), 1)
                if n:
                    m = n - 1
                    c = slice(m * P, (m + 1) * P)
                    for g in (0, 1):
                        act.wait_ge(S("pTt"), 2 * m + g + 1)
                        act.wait_ge(S("pv"), 2 * max(m - 1, 0))
                        nc.scalar.activation(probT[m % 2][:, 4 * g:4 * g + 4, :],
                                             bank[2 + g][:, :].rearrange("p (k t) -> p k t", k=4),
                                             ACT.Copy).then_inc(S("pT"), 1)
                    for g in (0, 1):
                        act.wait_ge(S("pv"), 2 * m + g + 1)
                        nc.scalar.activation(o_hi[:, 4 * g:4 * g + 4, c],
                                             bank[4 + g][:, :].rearrange("p (k t) -> p k t", k=4),
                                             ACT.Copy).then_inc(S("o_hi"), 1)
            act.wait_ge(S("o_smp"), 8)
            nc.scalar.activation(o_rows[:, 0:512], bank[6][0:NS, :], ACT.Copy).then_inc(S("o_rows"), 1)
            act.wait_ge(S("srow"), 3)
            nc.scalar.activation(o_hi[:, :, SEQ:T], bank[0][:, 0:64].rearrange("p (k b) -> p k b", k=KD),
                                 ACT.Copy).then_inc(S("o_hi"), 1)

        def att_vector(dve):
            def dots(n):
                b = n % 2
                dve.wait_ge(S("q_bc"), n + 1)
                dve.wait_ge(cache_in[b], 16 * (n // 2 + 1))
                for m in (0, 1):
                    for h in range(XH):
                        dve.wait_ge(S("s_dot"), 8 * n + 4 * m + h)
                        nc.vector.scalar_tensor_tensor(
                            out=s_junk[:, :], in0=cache[b][:, m, h * XD:(h + 1) * XD], scalar=1.0,
                            in1=bank[6 + h // 2][:, (h % 2) * 256:(h % 2) * 256 + 256],
                            op0=ALU.mult, op1=ALU.mult,
                            accum_out=s_smp[:, n * XH + h, m:m + 1]).then_inc(S("s_dot"), 1)

            for j in (0, 1):
                dve.wait_ge(evac[j], xaq["mm1"][j])
            for n in range(9):
                if n < 8:
                    b = n % 2
                    for g in (0, 1):
                        dve.wait_ge(S("score"), 2 * n + g + 1)
                        dve.wait_ge(S("exp"), 4 * max(n - 1, 0))
                        link(nc.vector.tensor_reduce(
                            att[:, b, 3, 2 * g:2 * g + 2],
                            bank[g][:, :].rearrange("p (h m) -> p h m", h=2), AX.X, ALU.max))
                    nc.vector.tensor_scalar(att[:, b, 0, :], att[:, b, 3, :], -SC, None, ALU.mult)\
                        .then_inc(S("nmax"), 1)
                    if n < 4:
                        dots(2 * n)
                    dve.wait_ge(S("exp"), 4 * n + 4)
                    link(nc.vector.reciprocal(att[:, b, 2, :], att[:, b, 1, :]))
                    nc.vector.tensor_tensor(prob[b][:, :, :], prob[b][:, :, :],
                                            att[:, b, 2, :].unsqueeze(2).to_broadcast([P, XH, NMEM]),
                                            ALU.mult).then_inc(S("pnorm"), 1)
                    if n < 4:
                        dots(2 * n + 1)
                    if n == 4:
                        dve.wait_ge(S("srow"), 1)
                        link(nc.vector.tensor_reduce(s_row[:, 2:3], bank[6][0:32, 0:NMEM], AX.X, ALU.max))
                        nc.vector.tensor_scalar(s_row[:, 0:1], s_row[:, 2:3], -SC, None, ALU.mult)\
                            .then_inc(S("srow_v"), 1)
                        dve.wait_ge(S("srow_e"), 1)
                        link(nc.vector.reciprocal(s_row[:, 3:4], s_row[:, 1:2]))
                        nc.vector.tensor_scalar(p_smp[:, :], p_smp[:, :], s_row[:, 3:4], None, ALU.mult)\
                            .then_inc(S("srow_v"), 1)
                    if n == 5:
                        dve.wait_ge(S("srow"), 2)
                        link(nc.vector.memset(pT_smp[0][:, :, :], 0.0), False)
                        link(nc.vector.memset(pT_smp[1][:, :, :], 0.0))
                        for m in (0, 1):
                            nc.vector.tensor_copy(
                                pT_smp[m][:, :, 0:32:8],
                                bank[7][:, m * 32:m * 32 + 32].rearrange("p (b h) -> p b h", b=NS))\
                                .then_inc(S("srow_v"), 1)
                if n:
                    m = n - 1
                    c = slice(m * P, (m + 1) * P)
                    for g in (0, 1):
                        dve.wait_ge(S("o_hi"), 2 * m + g + 1)
                        nc.vector.tensor_tensor(o_lo[:, 4 * g:4 * g + 4, c],
                                                bank[4 + g][:, :].rearrange("p (k t) -> p k t", k=4),
                                                o_hi[:, 4 * g:4 * g + 4, c].bitcast(F), ALU.subtract)\
                            .then_inc(S("o_lo"), 1)
            dve.wait_ge(S("o_smp"), 8)
            nc.vector.tensor_copy(o_rows[:, 512:D], bank[7][0:NS, :]).then_inc(S("o_rows"), 1)
            dve.wait_ge(S("o_hi"), 17)
            nc.vector.tensor_tensor(o_lo[:, :, SEQ:T], bank[0][:, 0:64].rearrange("p (k b) -> p k b", k=KD),
                                    o_hi[:, :, SEQ:T].bitcast(F), ALU.subtract).then_inc(S("o_lo"), 1)

        def blk_rows(n):
            return P if n < 8 else NS

        def final_tensor(pe):
            for j in (0, 1):
                pe.wait_ge(evac[j], ffn2[-1][1]["mm1"][j])
            for n in range(9):
                pe.wait_ge(S("y_out2"), 2 * max(n - 2, 0))
                for k in range(KD):
                    m = nc.tensor.transpose(
                        bank[2 * (n % 3) + k // 4][0:blk_rows(n), (k % 4) * P:(k % 4 + 1) * P],
                        x[:, k, n * P:n * P + blk_rows(n)], ident)
                    if k % 4 == 3:
                        m.then_inc(S("yt"), 1)

        def final_scalar(act):
            for n in range(9):
                r = slice(0, blk_rows(n))
                for h in (0, 1):
                    act.wait_ge(S("yt"), 2 * n + h + 1)
                    act.wait_ge(S("y_sq"), 3 * n if h == 0 else max(3 * n - 1, 0))
                    nc.scalar.activation(fin_sq[r, h, :], bank[2 * (n % 3) + h][r, :], ACT.Square,
                                         accum_out=fin_st[r, n, h:h + 1]).then_inc(S("y_sq"), 1)
                act.wait_ge(S("y_ms"), n + 1)
                nc.scalar.activation(fin_st[r, n, 3:4], fin_st[r, n, 2:3], ACT.Sqrt,
                                     bias=eps_t[r, 0:1], scale=1.0 / D).then_inc(S("y_sq"), 1)

        def final_vector(dve):
            dve.wait_ge(S("fin_in"), 16)
            for n in range(9):
                r = slice(0, blk_rows(n))
                dve.wait_ge(S("y_sq"), 3 * n + 2)
                nc.vector.tensor_tensor(fin_st[r, n, 2:3], fin_st[r, n, 0:1], fin_st[r, n, 1:2],
                                        ALU.add).then_inc(S("y_ms"), 1)
                dve.wait_ge(S("y_sq"), 3 * n + 3)
                link(nc.vector.reciprocal(fin_st[r, n, 2:3], fin_st[r, n, 3:4]))
                for h in (0, 1):
                    nc.vector.scalar_tensor_tensor(
                        out=y_nat[r, n, 512 * h:512 * h + 512], in0=bank[2 * (n % 3) + h][r, :],
                        scalar=fin_st[r, n, 2:3], in1=fin_g[r, 512 * h:512 * h + 512],
                        op0=ALU.mult, op1=ALU.mult).then_inc(S("y_out2"), 1)

        def final_out(sp):
            for n in range(9):
                sp.wait_ge(S("y_out2"), 2 * n + 2)
                if n < 8:
                    sp.dma_start(O["y_prompt"][0, n * P:(n + 1) * P, :], y_nat[:, n, :])\
                        .then_inc(S("out4"), 16)
                else:
                    sp.dma_start(O["y_sample"][:, 0, :], y_nat[0:NS, n, :]).then_inc(S("out4"), 16)
            sp.wait_ge(S("out4"), 144)
            sp.wait_ge(S("out3"), 32)
            sp.wait_ge(S("rwkv_out"), 80)

        smp_d = nc.dram_tensor("smp_d", (6, NS, BW), F, kind="Internal").ap()
        smp_od = nc.dram_tensor("smp_od", (NS, BW), F, kind="Internal").ap()
        x_save = nc.dram_tensor("x_save", (P, KD, T), F, kind="Internal").ap()
        y_save = nc.dram_tensor("y_save", (P, 4, T), F, kind="Internal").ap()

        block = ctx.enter_context(nc.Block())

        @block.sync
        def _(sp):
            sp.dma_start(cst[:], A["constants"]).then_inc(S("cst_in"), 16)
            sp.dma_start(xnat_s[0:NS, :], A["x_sample"][:, 0, :]).then_inc(S("x_in1"), 16)
            for n in range(8):
                sp.dma_start(xnat[:, n, :], A["x_prompt"][0, n * P:(n + 1) * P, :])\
                    .then_inc(S("x_in0") if n < 1 else S("x_in1") if n < 4 else S("x_in2"), 16)
            for a, b in ffn1:
                load_weights(sp, a)
                load_weights(sp, b)
            for ph in win:
                load_weights(sp, ph)
            gmlp_loads(sp)
            win_done(sp)
            sp.dma_start(shift_in[:, :], A["state_shift"][0, :, 0, :]).then_inc(S("prep_in"), 16)
            sp.wait_ge(S("sho_ev"), 4)
            sp.dma_start(O["state_shift_prompt"][0, :, 0, :], shift_out[0:1, :]).then_inc(S("rwkv_out"), 16)
            sp.dma_start(O["state_shift_sample"][0, :, 0, :], shift_out[1:NS + 1, :])\
                .then_inc(S("rwkv_out"), 16)
            sp.wait_ge(S("vn"), 9)
            sp.dma_start(O["chunk_v_sample"][0, :, 0, :], vn[0:NS, 2, :]).then_inc(S("out"), 16)
            sp.wait_ge(S("gmix"), 9)
            sp.dma_start(lora_w[0:64, :], A["rwkv_w2"][0]).then_inc(S("prep_in"), 16)
            sp.dma_start(lora_w[64:128, :], A["rwkv_a2"][0]).then_inc(S("prep_in"), 16)
            sp.dma_start(y_save, z[:, 8:12, :]).then_inc(S("y_out"), 16)
            sp.wait_ge(S("y_out"), 16)
            sp.wait_ge(S("out"), 16)
            sp.wait_ge(S("rwkv_out"), 32)
            sample_loads(sp)
            load_weights(sp, wout)
            for ph in (memk, memv):
                load_weights(sp, ph)
            load_weights(sp, xaq)
            for n in range(8):
                cache_loads(sp, "k", n)
            for n in range(8):
                cache_loads(sp, "v", n)
            load_weights(sp, xao)
            sp.wait_ge(S("o_lo"), 17)
            sp.dma_start(fin_g[:, :], A["final_norm"].partition_broadcast(P)).then_inc(S("fin_in"), 16)
            for a, b in ffn2:
                load_weights(sp, a)
                load_weights(sp, b)
            final_out(sp)

        @block.gpsimd
        def _(g):
            nc.gpsimd.memset(eps_t[:, 0:1], 1e-6).then_inc(S("const"), 1)
            nc.gpsimd.memset(eps_t[:, 1:2], 1e-5).then_inc(S("const"), 1)
            nc.gpsimd.memset(eps_t[:, 2:3], 64e-5).then_inc(S("const"), 1)
            nc.gpsimd.memset(eps_t[:, 3:4], LOG_SHIFT / 2).then_inc(S("const"), 1)
            g.wait_ge(S("vz"), 1)
            for name, k in VROWS:
                r0, src = VAT[name], A[name]
                src = src[0] if name != "final_norm" else src
                if name == "rwkv_mu":
                    g.dma_start(vnat[r0:r0 + k - 1, :],
                                src[0:(k - 1) * P].rearrange("(k p) -> k p", p=P)).then_inc(S("v_in"), 16)
                    g.dma_start(vnat[r0 + k - 1:r0 + k, 0:NB - (k - 1) * P],
                                src[(k - 1) * P:NB].rearrange("(k p) -> k p", k=1)).then_inc(S("v_in"), 16)
                elif name == "rwkv_r_k":
                    g.dma_start(vnat[r0:r0 + k, :], src.rearrange("(k a) p -> k (a p)", a=2))\
                        .then_inc(S("v_in"), 16)
                else:
                    g.dma_start(vnat[r0:r0 + k, :], src.rearrange("(k p) -> k p", p=P))\
                        .then_inc(S("v_in"), 16)
            g.wait_ge(S("cst_in"), 16)
            for a, b in ffn1:
                split_weights(g, a)
                split_weights(g, b)
            for ph in win:
                split_weights(g, ph)
            shift_pool(g)
            for n in range(8):
                chunk_pool(g, n)
            post_pool(g)
            for ph in (wout, memk, memv, xaq, xao, *(p for ab in ffn2 for p in ab)):
                split_weights(g, ph, high=ph not in (memk, memv))

        NVDMA = 16 * (len(VROWS) + 1)

        @block.tensor
        def _(pe):
            pe.wait_ge(S("cst_in"), 16)
            for n in range(8):
                pe.wait_ge(*((S("x_in0"), 16) if n < 1 else (S("x_in1"), 64) if n < 4 else (S("x_in2"), 64)))
                b = 2 * (n % 4)
                if n >= 4:
                    pe.wait_ge(S("xt_a"), n - 3)
                    pe.wait_ge(S("xt_b"), n - 3)
                for k in range(KD):
                    m = nc.tensor.transpose(bank[b + k // 4][:, (k % 4) * P:(k % 4 + 1) * P],
                                            xnat[:, n, k * P:(k + 1) * P], ident)
                    if k % 4 == 3:
                        m.then_inc(S("xt"), 1)
                if n == 2:
                    pe.wait_ge(S("v_in"), NVDMA)
                    nc.tensor.transpose(bank[7][:, 0:NVEC], vnat[0:NVEC, :], ident[0:NVEC, 0:NVEC])\
                        .then_inc(S("vt"), 1)
                    pe.wait_ge(S("vz"), 2)
            pe.wait_ge(S("xt_a"), 5)
            for k in range(KD):
                m = nc.tensor.transpose(bank[0][:, k * NS:(k + 1) * NS],
                                        xnat_s[0:NS, k * P:(k + 1) * P], ident[0:NS, 0:NS])
            m.then_inc(S("xt"), 1)
            pe.wait_ge(S("xt_a"), 9)
            pe.wait_ge(S("xt_b"), 8)
            for a, b in ffn1:
                if a["f0"] == 0:
                    multiply(pe, a, tile_ready=lambda t: pe.wait_ge(S("x_lo"), KD * (t + 1)),
                             after_first=lambda: rms_tensor(pe, 0))
                else:
                    multiply(pe, a)
                multiply(pe, b, lambda h, b=b: pe.wait_ge(
                    S("hid_lo"), 3 * (b["f1"] - b["kt"] + (min(4, b["kt"]) if h == 0 else b["kt"]))))
            for ph in win:
                if ph is win_a:
                    multiply(pe, ph, lambda h: pe.wait_ge(S("x_lo"), 24 + 12 * (h + 1)),
                             after_first=lambda: rms_tensor(pe, 1))
                else:
                    multiply(pe, ph)
            gmlp_tensor(pe)
            prep_tensor(pe)
            for n in range(8):
                chunk_tensor(pe, n)
            post_tensor(pe)
            pe.wait_ge(S("yb_lo"), 1)
            multiply(pe, wout, lambda h: pe.wait_ge(S("yb_lo"), 13))
            mem_tensor_a(pe)
            rms_tensor(pe, 2)
            pe.wait_ge(S("mem_lo"), KD)
            multiply(pe, memk)
            multiply(pe, memv)
            nat_tensor(pe)
            pe.wait_ge(S("nat_a"), 4)
            pe.wait_ge(S("nat_b"), 4)
            multiply(pe, xaq)
            att_tensor(pe)
            pe.wait_ge(S("o_lo"), 17)
            multiply(pe, xao)
            for a, b in ffn2:
                if a is ffn2[0][0]:
                    multiply(pe, a, lambda h: pe.wait_ge(S("x_lo"), 72 + 12 * (h + 1)),
                             after_first=lambda: rms_tensor(pe, 3))
                else:
                    multiply(pe, a)
                multiply(pe, b, lambda h, b=b: pe.wait_ge(
                    S("hid_lo"), 3 * (b["f1"] - b["kt"] + (min(4, b["kt"]) if h == 0 else b["kt"]))))
            final_tensor(pe)


        @block.scalar
        def _(act):
            for t in range(3):
                for n in range(3 * t, min(3 * t + 3, 8)):
                    act.wait_ge(S("xt"), 2 * n + 1)
                    nc.scalar.activation(x[:, 0:4, n * P:(n + 1) * P],
                                         bank[2 * (n % 4)][:, :].rearrange("p (k n) -> p k n", k=4),
                                         ACT.Copy).then_inc(S("xt_a"), 1)
                if t == 2:
                    act.wait_ge(S("xt"), 17)
                    nc.scalar.activation(x[:, :, SEQ:T],
                                         bank[0][:, 0:KD * NS].rearrange("p (k n) -> p k n", k=KD),
                                         ACT.Copy).then_inc(S("xt_a"), 1)
                act.wait_ge(S("vz"), 2)
                act.wait_ge(S("xt_a"), 3 * t + 3)
                act.wait_ge(S("xt_b"), min(3 * t + 3, 8))
                for k in range(KD):
                    split_scalar(act, 0, "ln_ffn1", h_hi, k, t, KD * t + k)
            rms_scalar(act, 0)
            prev = None
            for a, b in ffn1:
                gu_scalar(act, a, prev)
                prev = b
            residual_scalar(act, 1, "ln_mix", ffn1[-1][1], h_hi)
            act.dma_start(x_save, x[:, :, :]).then_inc(S("x_out"), 16)
            rms_scalar(act, 1)
            gmlp_scalar(act)
            prep_scalar(act)
            for n in range(8):
                chunk_scalar(act, n)
            post_scalar(act)
            mem_scalar_a(act)
            residual_scalar(act, 2, "ln_xattn", wout, h_hi)
            mem_scalar_b(act)
            rms_scalar(act, 2)
            for ph in (memk, memv):
                split_weights(act, ph, low=False)
            nat_scalar(act)
            nat_out(act)
            att_scalar(act)
            residual_scalar(act, 3, "ln_ffn2", xao, h2_hi)
            rms_scalar(act, 3)
            prev = None
            for a, b in ffn2:
                gu_scalar(act, a, prev)
                prev = b
            final_scalar(act)

        @block.vector
        def _(dve):
            nc.vector.memset(vnat[:, :], 0.0).then_inc(S("vz"), 1)
            for t in range(3):
                for n in range(3 * t, min(3 * t + 3, 8)):
                    dve.wait_ge(S("xt"), 2 * n + 2)
                    nc.vector.tensor_copy(x[:, 4:8, n * P:(n + 1) * P],
                                          bank[2 * (n % 4) + 1][:, :].rearrange("p (k n) -> p k n", k=4))\
                        .then_inc(S("xt_b"), 1)
                if t == 0:
                    dve.wait_ge(S("vt"), 1)
                    nc.vector.tensor_copy(vec[:, :], bank[7][:, 0:NVEC]).then_inc(S("vz"), 1)
                    dve.wait_ge(S("vz"), 2)
                for k in range(KD):
                    split_vector(dve, 0, "ln_ffn1", h_hi, h_lo, k, t, KD * t + k)
            rms_vector(dve, 0)
            for a, b in ffn1:
                gu_vector(dve, a)
                if b is ffn1[-1][1]:
                    residual_vector(dve, 1, "ln_mix", b, h_hi, h_lo, 0.5)
                else:
                    add_to_x(dve, b, 0.5)
            rms_vector(dve, 1)
            z_evac(dve)
            gmlp_vector(dve)
            prep_vector(dve)
            dve.wait_ge(mm[0], WIN_END[0])
            dve.wait_ge(mm[1], WIN_END[1])
            nc.vector.memset(st_T[:, 0, :, :], 0.0).then_inc(S("st0"), 1)
            nc.vector.memset(Us[:, :], 0.0).then_inc(S("st0"), 1)
            dve.wait_ge(S("st0"), 2)
            for n in range(8):
                chunk_vector(dve, n)
            post_vector(dve)
            mem_vector_a(dve)
            dve.wait_ge(S("x_back"), 16)
            residual_vector(dve, 2, "ln_xattn", wout, h_hi, h_lo, 1.0)
            mem_vector_b(dve)
            rms_vector(dve, 2)
            plain_evac(dve, memk, kT)
            plain_evac(dve, memv, vT)
            nat_vector(dve)
            plain_evac(dve, xaq, qT, normed=True)
            att_vector(dve)
            residual_vector(dve, 3, "ln_ffn2", xao, h2_hi, h2_lo, 1.0)
            rms_vector(dve, 3)
            for a, b in ffn2:
                gu_vector(dve, a)
                add_to_x(dve, b, 0.5)
            final_vector(dve)


_IN = ["x_prompt", "x_sample", "state_rwkv", "state_shift", "cache_mem_k", "cache_mem_v", "mem_prompt",
       "ln_ffn1", "ffn1_gate", "ffn1_up", "ffn1_down", "ln_mix", "w_in", "w_out", "sgu_w", "sgu_b",
       "sgu_ln_g", "sgu_ln_b", "rwkv_mu", "rwkv_w0", "rwkv_w2", "rwkv_a0", "rwkv_a2", "rwkv_g2",
       "rwkv_k_k", "rwkv_k_a", "rwkv_r_k", "rwkv_gn_g", "rwkv_gn_b", "ln_xattn", "mem_norm", "xa_q",
       "xa_k", "xa_v", "xa_o", "ln_ffn2", "ffn2_gate", "ffn2_up", "ffn2_down", "final_norm"]
_OUT = [("y_prompt", (1, SEQ, D)), ("y_sample", (NS, 1, D)),
        ("state_rwkv_prompt", (1, 1, HEADS, HN, HN)), ("state_shift_prompt", (1, 1, 1, NB)),
        ("mem_k_prompt", (1, 1, NMEM, XH, XD)), ("mem_v_prompt", (1, 1, NMEM, XH, XD)),
        ("state_rwkv_sample", (1, NS, HEADS, HN, HN)), ("state_shift_sample", (1, NS, 1, NB)),
        ("chunk_v_sample", (1, NS, 1, AW))]


def kernel(**inputs):
    import concourse.bacc as bacc
    from concourse.bass_utils import run_bass_kernel_spmd

    nc = bacc.Bacc("TRN2", target_bir_lowering=False, num_devices=1)
    arrays = {f"in_{n}": np.ascontiguousarray(inputs[n]) for n in _IN}
    arrays["in_constants"] = constants()
    A = {k[3:]: nc.dram_tensor(k, a.shape, mybir.dt.from_np(a.dtype), kind="ExternalInput").ap()
         for k, a in arrays.items()}
    O = {n: nc.dram_tensor(f"out_{n}", s, mybir.dt.float32, kind="ExternalOutput").ap() for n, s in _OUT}
    program(nc, A, O)
    r = run_bass_kernel_spmd(nc, [arrays], core_ids=[0])
    return tuple(r.results[0][f"out_{n}"] for n, _ in _OUT)
```

```python
import numpy as np
import concourse.bass as bass
from concourse import mybir
from contextlib import ExitStack

P = 128
D, SEQ, NS = 1024, 1024, 8
T = SEQ + NS
KD = D // P
TOK = [(0, 344), (344, 344), (688, 344)]
DFF = 2816
FT = DFF // P
GROUPS = [8, 8, 6]
AW = BW = 512
HEADS, HN = 8, 64
NB = 3 * BW + 64 + 64 + 160
INP = 2 * AW + NB
NBT = -(-NB // P)
CH = 64
NMEM, XH, XD = 256, 4, 256
DECAY = float(np.exp(-0.5))

LOG_SHIFT = 20 * float(np.log(2.0))

VROWS = [("ln_ffn1", 8), ("ln_mix", 8), ("ln_xattn", 8), ("mem_norm", 8), ("ln_ffn2", 8),
         ("final_norm", 8), ("rwkv_w0", 4), ("rwkv_a0", 4), ("rwkv_k_k", 4), ("rwkv_k_a", 4),
         ("rwkv_r_k", 4), ("rwkv_gn_g", 4), ("rwkv_gn_b", 4), ("rwkv_mu", NBT)]
VAT, _n = {}, 0
for _name, _k in VROWS:
    VAT[_name] = _n
    _n += _k
NVEC = _n

C_ID, C_ONE, C_BLK, C_STR, C_INC, C_TRI, C_LVL = 0, 1, 2, 3, 4, 5, 6
NCST = 12
LEVELS = 6


def constants():
    s, t = np.arange(P)[:, None], np.arange(P)[None, :]
    same = s // CH == t // CH
    tabs = [s == t, s == s + 0 * t, same / HN, same & (s < t), same & (s <= t), s <= t]
    tabs += [(s >> (l + 1) == t >> (l + 1)) & (s >> l < t >> l) for l in range(LEVELS)]
    return np.stack([np.asarray(m, np.float32) for m in tabs], 1)


def program(nc, A, O):
    F, R = mybir.dt.float32, mybir.dt.float32r
    ALU, ACT, AX = mybir.AluOpType, mybir.ActivationFunctionType, mybir.AxisListType
    ds = bass.ds
    ctx = ExitStack()
    with ctx:
        base = [-(-int(nc.sbuf_base) // 32) * 32]

        def take(nbytes):
            at = base[0]
            base[0] += -(-nbytes // 32) * 32
            return at

        def at(name, shape, off, dt=F):
            return nc.alloc_sbuf_tensor_at(name, shape, dt, offset=off)

        ROW = T * 4
        arena_z = take(24 * ROW)
        arena_h = take(16 * ROW)
        arena_w = take(3 * 4 * 4 * P * 4)
        arena_c = take(NCST * P * 4)
        arena_v = take(NVEC * 4)
        arena_g = take(3 * 344 * 4)
        arena_t = take(3 * 344 * 4)
        arena_m = take(8192)
        cap = int(nc.sbuf_usable_end) if not callable(nc.sbuf_usable_end) else int(nc.sbuf_usable_end())
        assert base[0] <= cap, (base[0], cap)

        x = at("x", [P, KD, T], arena_z)
        z = at("z", [P, 24, T], arena_z)
        xnat = at("xnat", [P, 8, D], arena_z + 8 * ROW)
        xnat_s = at("xnat_s", [P, D], arena_z + 16 * ROW)
        hid_hi = at("hid_hi", [P, 8, T], arena_z + 8 * ROW, R)
        hid_lo = at("hid_lo", [P, 8, T], arena_z + 16 * ROW, R)
        h_hi = at("h_hi", [P, KD, T], arena_h, R)
        h_lo = at("h_lo", [P, KD, T], arena_h + 8 * ROW, R)
        raw = at("raw", [P, 4, 4, P], arena_w)
        w_hi = at("w_hi", [P, 4, 4, P], arena_w + 8192, R)
        w_lo = at("w_lo", [P, 4, 4, P], arena_w + 16384, R)
        cst = at("cst", [P, NCST, P], arena_c)
        vec = at("vec", [P, NVEC], arena_v)
        vnat = at("vnat", [P, P], arena_g)
        gate_s = at("gate_s", [P, 3, 344], arena_g)
        tmp = at("tmp", [P, 3, 344], arena_t)
        rstd = at("rstd", [P, 3, 344], arena_m)
        bank = [ctx.enter_context(nc.psum_tensor(f"bank{i}", [P, 512], F)) for i in range(8)]
        ident = cst[:, C_ID, :]

        mem_hi = at("mem_hi", [P, KD, NMEM], arena_z + 8 * ROW, R)
        mem_lo = at("mem_lo", [P, KD, NMEM], arena_z + 8 * ROW + 8192, R)
        qT = at("qT", [P, KD, T], arena_z + 8 * ROW)
        kT = at("kT", [P, KD, NMEM], arena_z + 16 * ROW)
        v_n = at("v_n", [P, 2, D], arena_z + 16 * ROW + 8192)
        vT = at("vT", [P, KD, NMEM], arena_z + 16 * ROW + 16384)
        mk_n = at("mk_n", [P, 2, D], arena_z + 16 * ROW + 24576)
        mem_n = at("mem_n", [P, 2, D], arena_m)
        mem_sq = at("mem_sq", [P, D], arena_c + C_BLK * 512)
        cache = [at("cache0", [P, 2, D], arena_z + 16 * ROW + 16384),
                 at("cache1", [P, 2, D], arena_z + 16 * ROW + 24576)]
        prob = [at("prob0", [P, XH, NMEM], arena_g), at("prob1", [P, XH, NMEM], arena_m)]
        probT = [at("probT0", [P, XH * 2, P], arena_t), at("probT1", [P, XH * 2, P], arena_m + 4096)]
        att = at("att", [P, 2, 4, XH], arena_c + C_LVL * 512)
        mem_st = at("mem_st", [P, 2, 4], arena_c + C_BLK * 512 + 4096)
        s_smp = at("s_smp", [P, NS * XH, 2], arena_c + C_LVL * 512 + 256)
        s_row = at("s_row", [NS * XH, 4], arena_c + C_LVL * 512 + 512)
        p_smp = at("p_smp", [NS * XH, NMEM], arena_c + C_LVL * 512 + 544)
        pT_smp = [at("pT_smp0", [P, NS, 33], arena_c + C_BLK * 512),
                  at("pT_smp1", [P, NS, 33], arena_c + C_LVL * 512 + 2016)]
        s_junk = at("s_junk", [P, XD], arena_c + C_STR * 512)
        o_rows = at("o_rows", [NS, D], arena_z + 16 * ROW + 16384)
        o_hi = at("o_hi", [P, KD, T], arena_h, R)
        o_lo = at("o_lo", [P, KD, T], arena_h + 8 * ROW, R)
        y_nat = at("y_nat", [P, 9, D], arena_z + 8 * ROW)
        h2_hi = at("h2_hi", [P, KD, T], arena_z + 8 * ROW, R)
        h2_lo = at("h2_lo", [P, KD, T], arena_z + 16 * ROW, R)
        hid2_hi = at("hid2_hi", [P, 8, T], arena_h, R)
        hid2_lo = at("hid2_lo", [P, 8, T], arena_h + 8 * ROW, R)
        fin_g = at("fin_g", [P, D], arena_c + C_BLK * 512)
        fin_st = at("fin_st", [P, 9, 4], arena_c + C_BLK * 512 + 4096)
        fin_sq = at("fin_sq", [P, 2, 512], arena_g)

        gw_nat = at("gw_nat", [P, 8, P], arena_z + 7 * ROW)
        gwT = at("gwT", [P, 8, P], arena_t)
        ln_gb = at("ln_gb", [P, 2, AW], arena_g)
        g_bias = at("g_bias", [P, 4, P], arena_m + 4160)
        g_w00 = at("g_w00", [P, 4], arena_m + 6208)
        g_stat = at("g_stat", [P, 2, 8], arena_m + 6240)
        vn = at("vn", [P, 3, AW], arena_z)
        g_mix = at("g_mix", [P, 2, AW], arena_z + 2 * ROW)
        shift_out = at("shift_out", [NS + 1, NB], arena_h + 4 * ROW)
        shift_in = at("shift_in", [NS, NB], arena_h + 6 * ROW)
        shiftT = at("shiftT", [P, NBT, NS], arena_m + 6400)
        diff = at("diff", [P, 8, T], arena_z + 8 * ROW)
        diff_p = at("diff_p", [P, T], arena_w + 10208)
        lora_w = at("lora_w", [P, 2, BW], arena_g)
        nkk = at("nkk", [P, 4, T], arena_h)
        bvec = at("bvec", [P, 4, T], arena_h + 4 * ROW)
        sg = at("sg", [P, 4, T], arena_h + 8 * ROW)
        cum = at("cum", [P, 4, T], arena_h + 12 * ROW)
        scan_mask = at("scan_mask", [P, T], arena_z + 7 * ROW)
        mats = [{n: at(f"{n}{q}", [P, 4, P], arena_z + 8 * ROW + (8 * q + j) * 2048)
                 for j, n in enumerate(("MT", "QKT", "TT", "Ti", "Y", "LoT"), 2)}
                for q in (0, 1)]
        LQ = [at(f"LQ{q}", [P, 2, 4, P], arena_z + 8 * ROW + 8 * q * 2048) for q in (0, 1)]
        for q in (0, 1):
            mats[q]["LT"], mats[q]["QBT"] = LQ[q][:, 0], LQ[q][:, 1]
        AR = [at("AR0", [P, 2, 4, P], arena_g),
              at("AR1", [P, 2, 4, P], arena_w + 14336)]
        BK = at("BK", [P, 2, 4, P], arena_t)
        dec = at("dec", [P, 4, P], arena_z + 7 * ROW)
        ext = at("ext", [P, 4, P], arena_z + 7 * ROW + 2048)
        Bt = at("Bt", [P, BW], arena_z + 4 * ROW)
        Kt = at("Kt", [P, BW], arena_z + 4 * ROW + 2048)
        Vt = at("Vt", [P, BW], arena_m)
        vstage = at("vstage", [P, 4, P], arena_w + 18432)
        Xs = at("Xs", [P, BW], arena_m + 2048)
        Us = at("Us", [P, BW], arena_m + 4096)
        smp_n = at("smp_n", [NS, 6, BW], arena_z + 8 * ROW)
        smp_S = at("smp_S", [P, 32, HN], arena_z + 8 * ROW + 12288)
        smp_t = at("smp_t", [P, 32, HN], arena_z + 8 * ROW + 20480)
        smp_v = at("smp_v", [P, 6, HN], arena_z + 8 * ROW + 28672)
        smp_o = at("smp_o", [P, 2, 32], arena_z + 8 * ROW + 30208)
        gn_sq = at("gn_sq", [P, 3, 344], arena_t)
        smp_on = at("smp_on", [NS, BW], arena_w + 22528)
        smp_vk = at("smp_vk", [P, 32, HN], arena_w + 14336)
        smp_w = at("smp_w", [P, 4, NS], arena_z + 8 * ROW + 32512)
        st_out = at("st_out", [P, 4, P], arena_w + 12288)
        g2_w = at("g2_w", [P, 2, BW], arena_z + 7 * ROW)
        ya_in = at("ya_in", [P, 4, T], arena_h + 4 * ROW)
        y_hi = at("y_hi", [P, KD, T], arena_z + 8 * ROW, R)
        y_lo = at("y_lo", [P, KD, T], arena_z + 16 * ROW, R)
        st_T = at("st_T", [P, 3, 4, P], arena_w)
        decm = at("decm", [P, 2, 4, P], arena_w + 6144)

        links = [0]

        def link(ins, wait=True):
            links[0] += 1
            ins.then_inc(S("link"), 1)
            if wait:
                nc.vector.wait_ge(S("link"), links[0])

        def v_col(name, k):
            return vec[:, VAT[name] + k:VAT[name] + k + 1]

        sems = {}

        def S(name):
            if name not in sems:
                sems[name] = ctx.enter_context(nc.semaphore(name))
            return sems[name]

        raw_in = [S(f"raw_in{i}") for i in range(4)]
        hi_done = [S(f"hi_done{i}") for i in range(4)]
        split_done = [S(f"split_done{i}") for i in range(4)]
        w_used = [S(f"w_used{i}") for i in range(2)]
        mm = [S("mm0"), S("mm1")]
        evac = [S("evac0"), S("evac1")]

        phases = []
        total = {"unit": 0, "mm": [0, 0], "f": 0}

        def phase(name, units, kt, src, hi, lo, toks=TOK, width=P):
            ph = dict(name=name, units=units, kt=kt, src=src, hi=hi, lo=lo, toks=toks, width=width,
                      u0=total["unit"], mm0=list(total["mm"]), f0=total["f"])
            total["unit"] += units
            for u in range(units):
                total["mm"][(ph["u0"] + u) % 2] += len(toks)
            ph["mm1"] = list(total["mm"])
            phases.append(ph)
            return ph

        def kview(w):
            return w.rearrange("(k p) c -> p k c", p=P)

        def ffn(n):
            wg, wu, wd = (kview(A[f"ffn{n}_{m}"][0]) for m in ("gate", "up", "down"))
            out, f = [], 0
            hi, lo, gh, gl = (h_hi, h_lo, hid_hi, hid_lo) if n == 1 else (h2_hi, h2_lo, hid2_hi, hid2_lo)
            for g in GROUPS:
                gu = phase(f"gu{n}_{f}", 2 * g, 8,
                           lambda s, i, f=f: ((wg, wu)[s], (i + f) * P), hi, lo)
                total["f"] += g
                dn = phase(f"dn{n}_{f}", 8, g,
                           lambda s, i, f=f, g=g: (wd[:, f:f + g, :], (2 * i + s) * P), gh, gl)
                dn["f1"] = total["f"]
                gu["hid"] = gh, gl
                out.append((gu, dn))
                f += g
            return out

        w_in = kview(A["w_in"][0])
        ffn1 = ffn(1)
        win_a = phase("win_a", 8, 8, lambda s, i: (w_in, (2 * i + s) * P), h_hi, h_lo)
        win_b = phase("win_b", 8, 8, lambda s, i: (w_in, (2 * i + s + 8) * P), h_hi, h_lo)
        win_c = phase("win_c", 2, 8, lambda s, i: (w_in, (2 * i + s + 20) * P), h_hi, h_lo)
        win_d = phase("win_d", 1, 8, lambda s, i: (w_in, 22 * P), h_hi, h_lo, width=NB - 14 * P)
        win_e = phase("win_e", 4, 8, lambda s, i: (w_in, (2 * i + s + 16) * P), h_hi, h_lo)
        win = [win_a, win_b, win_c, win_d, win_e]
        WIN_Z = (8, 16, 4, 6, 0)
        win_a["peel"] = True
        wo = kview(A["w_out"][0])
        wout = phase("wout", 8, 8, lambda s, i: (wo, (2 * i + s) * P), y_hi, y_lo)
        xk, xv, xq, xo = (kview(A[n][0]) for n in ("xa_k", "xa_v", "xa_q", "xa_o"))
        MTOK = [(0, NMEM)]
        memk = phase("memk", 8, 8, lambda s, i: (xk, (2 * i + s) * P), mem_hi, mem_lo, toks=MTOK)
        memv = phase("memv", 8, 8, lambda s, i: (xv, (2 * i + s) * P), mem_hi, mem_lo, toks=MTOK)
        xaq = phase("xaq", 8, 8, lambda s, i: (xq, (2 * i + s) * P), h_hi, h_lo)
        xao = phase("xao", 8, 8, lambda s, i: (xo, (2 * i + s) * P), o_hi, o_lo)
        ffn2 = ffn(2)
        ffn2[0][0]["peel"] = True

        def pairs(eng, ph, step, static=False):
            first = 0
            if static:
                for i in range(ph["units"] // 2):
                    step(i)
                return
            if ph["u0"] == 0 or "peel" in ph:
                step(0)
                first = 1
            if ph["units"] // 2 > first:
                with eng.Fori(first, ph["units"] // 2) as i:
                    step(i)

        def unit_steps(eng, ph, body, after=None):
            def run(i, s):
                for_u = ph["u0"] + s
                body(i, s, [((2 * for_u + h) % 4, (2 * for_u + h) // 4 + i) for h in (0, 1)])
                if after:
                    after(2 * i + s)
            pairs(eng, ph, lambda i: [run(i, s) for s in (0, 1)], static=after is not None)
            if ph["units"] % 2:
                i = ph["units"] // 2
                run(i, 0)

        def split_k(kt):
            return [(0, min(4, kt)), (4, kt - 4)]

        def load_weights(sp, ph):
            def body(i, s, turns):
                w, col = ph["src"](s, i)
                for (slot, turn), (k0, nk) in zip(turns, split_k(ph["kt"])):
                    sp.wait_ge(split_done[slot], turn)
                    sp.dma_start(raw[:, slot, 0:nk, 0:ph["width"]],
                                 w[:, k0:k0 + nk, ds(col, ph["width"])]).then_inc(raw_in[slot], 16)
            unit_steps(sp, ph, body)

        def split_weights(g, ph, high=True, low=True):
            def body(i, s, turns):
                st = (ph["u0"] + s) % 2
                for h, ((slot, turn), (k0, nk)) in enumerate(zip(turns, split_k(ph["kt"]))):
                    part = (slice(None), slot, slice(0, nk), slice(0, ph["width"]))
                    if high:
                        if h == 0:
                            g.wait_ge(w_used[st], turn)
                        else:
                            g.wait_ge(mm[st], i * len(ph["toks"]) + ph["mm0"][st])
                        g.wait_ge(raw_in[slot], turn * 16 + 16)
                    if high and not low:
                        nc.scalar.activation(w_hi[part], raw[part], ACT.Copy).then_inc(hi_done[slot], 1)
                        continue
                    if high:
                        nc.gpsimd.tensor_tensor(w_hi[part], raw[part],
                                                cst[:, C_ONE:C_ONE + 1, 0:ph["width"]].to_broadcast(
                                                    [P, nk, ph["width"]]), ALU.mult)\
                            .then_inc(hi_done[slot], 1)
                    g.wait_ge(hi_done[slot], turn + 1)
                    nc.gpsimd.tensor_tensor(w_lo[part], raw[part], w_hi[part].bitcast(F),
                                            ALU.subtract).then_inc(split_done[slot], 1)
            unit_steps(g, ph, body)

        def multiply(pe, ph, piece_ready=None, tile_ready=None, after_first=None,
                     after=None):
            nt, width, kt = len(ph["toks"]), ph["width"], ph["kt"]

            def body(i, s, turns):
                st = (ph["u0"] + s) % 2
                pieces = list(zip((0, 1), turns, split_k(kt)))

                def product(h, slot, k0, nk, t):
                    t0, tn = ph["toks"][t]
                    out = bank[3 * st + t][0:width, 0:tn]
                    for k in range(nk):
                        a, b = w_hi[:, slot, k, 0:width], w_lo[:, slot, k, 0:width]
                        hi, lo = ph["hi"][:, k0 + k, t0:t0 + tn], ph["lo"][:, k0 + k, t0:t0 + tn]
                        first, last = k0 + k == 0, k0 + k == kt - 1
                        nc.tensor.matmul(out, b, hi, start=first, stop=False)
                        nc.tensor.matmul(out, a, lo, start=False, stop=False)
                        m = nc.tensor.matmul(out, a, hi, start=False, stop=last)
                    if h == 1:
                        m.then_inc(mm[st], 1)
                    elif t == nt - 1:
                        m.then_inc(w_used[slot // 2], 1)

                pe.wait_ge(evac[st], i * nt + ph["mm0"][st])
                if tile_ready and isinstance(i, int) and s == 0:
                    for h, (slot, turn), _ in pieces:
                        pe.wait_ge(split_done[slot], turn + 1)
                    for t in range(nt):
                        tile_ready(t)
                        for h, (slot, turn), (k0, nk) in pieces:
                            product(h, slot, k0, nk, t)
                    after_first()
                    return
                for h, (slot, turn), (k0, nk) in pieces:
                    if piece_ready and s == 0:
                        piece_ready(h)
                    pe.wait_ge(split_done[slot], turn + 1)
                    for t in range(nt):
                        product(h, slot, k0, nk, t)
                if after_first and isinstance(i, int) and s == 0:
                    after_first()
            unit_steps(pe, ph, body, after)

        def each_tile(eng, ph, fn, after=None):
            nt = len(ph["toks"])

            def body(i, s, turns):
                st = (ph["u0"] + s) % 2
                for t in range(nt):
                    fn(i, s, st, t, i * nt + ph["mm0"][st] + t + 1)
            unit_steps(eng, ph, body, after)

        def tslice(t):
            return slice(TOK[t][0], TOK[t][0] + TOK[t][1])

        def gu_scalar(act, ph, prev_down):
            st = ph["u0"] % 2
            if prev_down:
                for j in (0, 1):
                    act.wait_ge(mm[j], prev_down["mm1"][j])
            hi = ph["hid"][0]

            def step(i):
                for t in range(3):
                    act.wait_ge(evac[st], i * 3 + ph["mm0"][st] + t + 1)
                    nc.scalar.activation(gate_s[:, t, :], gate_s[:, t, :], ACT.Silu)\
                        .then_inc(S("silu"), 1)
                for t in range(3):
                    act.wait_ge(S("prod"), i * 3 + 3 * ph["f0"] + t + 1)
                    nc.scalar.activation(hi[:, ds(i, 1), tslice(t)],
                                         tmp[:, t:t + 1, :], ACT.Copy).then_inc(S("hid_hi"), 1)
            pairs(act, ph, step)

        def gu_vector(dve, ph):
            sg, su = ph["u0"] % 2, (ph["u0"] + 1) % 2
            hi, lo = ph["hid"]

            def step(i):
                done = i * 3 + 3 * ph["f0"]

                def gate(t):
                    dve.wait_ge(mm[sg], i * 3 + ph["mm0"][sg] + t + 1)
                    dve.wait_ge(S("prod"), done)
                    nc.vector.tensor_tensor(gate_s[:, t, :], bank[3 * sg + t][:, 0:344],
                                            rstd[:, t, :], ALU.mult).then_inc(evac[sg], 1)

                def up(t):
                    dve.wait_ge(mm[su], i * 3 + ph["mm0"][su] + t + 1)
                    dve.wait_ge(S("hid_lo"), done)
                    nc.vector.tensor_tensor(tmp[:, t, :], bank[3 * su + t][:, 0:344],
                                            rstd[:, t, :], ALU.mult).then_inc(evac[su], 1)

                def prod(t):
                    dve.wait_ge(evac[su], i * 3 + ph["mm0"][su] + t + 1)
                    dve.wait_ge(S("silu"), done + t + 1)
                    nc.vector.tensor_tensor(tmp[:, t, :], tmp[:, t, :], gate_s[:, t, :], ALU.mult)\
                        .then_inc(S("prod"), 1)

                def low(t):
                    dve.wait_ge(S("hid_hi"), done + t + 1)
                    nc.vector.tensor_tensor(lo[:, ds(i, 1), tslice(t)], tmp[:, t:t + 1, :],
                                            hi[:, ds(i, 1), tslice(t)].bitcast(F),
                                            ALU.subtract).then_inc(S("hid_lo"), 1)
                for t in range(3):
                    gate(t)
                up(0)
                prod(0)
                up(1)
                prod(1)
                low(0)
                up(2)
                prod(2)
                low(1)
                low(2)
            pairs(dve, ph, step)

        def add_to_x(dve, ph, scale):
            for j in (0, 1):
                dve.wait_ge(evac[j], ph["mm0"][j])

            def one(i, s, st, t, count):
                dve.wait_ge(mm[st], count)
                xs = x[:, ds(2 * i + s, 1), tslice(t)]
                nc.vector.scalar_tensor_tensor(
                    out=xs, in0=bank[3 * st + t][:, 0:344].rearrange("p (a n) -> p a n", a=1),
                    scalar=scale, in1=xs, op0=ALU.mult, op1=ALU.add).then_inc(evac[st], 1)
            each_tile(dve, ph, one)

        def split_scalar(act, e, gain, hi, k, t, c):
            nc.scalar.activation(hi[:, k, tslice(t)], x[:, k, tslice(t)], ACT.Copy,
                                 scale=v_col(gain, k)).then_inc(S("x_hi"), 1)
            act.wait_ge(S("x_acc"), max(24 * e + c - 2, 0))
            nc.scalar.activation(gate_s[:, c % 3, :], x[:, k, tslice(t)], ACT.Square)\
                .then_inc(S("x_sq"), 1)

        def split_vector(dve, e, gain, hi, lo, k, t, c):
            dve.wait_ge(S("x_hi"), 24 * e + c + 1)
            nc.vector.scalar_tensor_tensor(out=lo[:, k, tslice(t)], in0=x[:, k, tslice(t)],
                                           scalar=v_col(gain, k), in1=hi[:, k, tslice(t)].bitcast(F),
                                           op0=ALU.mult, op1=ALU.subtract).then_inc(S("x_lo"), 1)
            dve.wait_ge(S("x_sq"), 24 * e + c + 1)
            if k == 0:
                nc.vector.tensor_copy(tmp[:, t, :], gate_s[:, c % 3, :]).then_inc(S("x_acc"), 1)
            else:
                dve.wait_ge(S("x_acc"), 24 * e + c)
                nc.vector.tensor_tensor(tmp[:, t, :], tmp[:, t, :], gate_s[:, c % 3, :], ALU.add)\
                    .then_inc(S("x_acc"), 1)

        def residual_scalar(act, e, gain, ph, hi):
            for u in range(8):
                for t in range(3):
                    st = (ph["u0"] + u) % 2
                    act.wait_ge(evac[st], ph["mm0"][st] + 3 * (u // 2) + t + 1)
                    split_scalar(act, e, gain, hi, u, t, 3 * u + t)

        def residual_vector(dve, e, gain, ph, hi, lo, scale):
            for j in (0, 1):
                dve.wait_ge(evac[j], ph["mm0"][j])
            for c in range(25):
                if c < 24:
                    u, t = c // 3, c % 3
                    st = (ph["u0"] + u) % 2
                    dve.wait_ge(mm[st], ph["mm0"][st] + 3 * (u // 2) + t + 1)
                    if e == 2:
                        dve.wait_ge(*((S("x_back0"), 16) if u == 0 else
                                      (S("x_back1"), 48) if u < 4 else (S("x_back2"), 64)))
                    xs = x[:, u, tslice(t)]
                    nc.vector.scalar_tensor_tensor(out=xs, in0=bank[3 * st + t][:, 0:344], scalar=scale,
                                                   in1=xs, op0=ALU.mult, op1=ALU.add)\
                        .then_inc(evac[st], 1)
                if c > 0:
                    split_vector(dve, e, gain, hi, lo, (c - 1) // 3, (c - 1) % 3, c - 1)

        def rms_tensor(pe, e):
            for t in range(3):
                pe.wait_ge(S("x_acc"), 24 * (e + 1))
                if t == 2:
                    pe.wait_ge(S("rms"), 3 * e + 1)
                nc.tensor.matmul(bank[6 + t % 2][:, 0:344], cst[:, C_ONE, :], tmp[:, t, :],
                                 start=True, stop=True).then_inc(S("x_sum"), 1)

        def rms_scalar(act, e):
            act.wait_ge(S("const"), 4)
            for t in range(3):
                act.wait_ge(S("x_sum"), 3 * e + t + 1)
                nc.scalar.activation(rstd[:, t, :], bank[6 + t % 2][:, 0:344], ACT.Sqrt,
                                     bias=eps_col, scale=1.0 / D).then_inc(S("rms"), 1)

        def rms_vector(dve, e):
            for t in range(3):
                dve.wait_ge(S("rms"), 3 * e + t + 1)
                link(nc.vector.reciprocal(rstd[:, t, :], rstd[:, t, :]), t == 2)

        eps_t = at("eps_t", [P, 8], take(32))
        eps_col = eps_t[:, 0:1]


        ZB = [8 + u for u in range(8, 16)] + list(range(0, 7))
        WIN_END = win_e["mm1"]

        def gmlp_steps(ph, step):
            first = {"win_b": 0, "win_c": 8}.get(ph["name"])
            return None if first is None else lambda u: step(first + u)

        def z_evac(dve):
            for ph, z0 in zip(win, WIN_Z):
                if ph is win_c:
                    dve.wait_ge(S("x_stored"), 16)
                if ph is win_e:
                    dve.wait_ge(S("vchunk_stored"), 16)
                if ph is win_b:
                    gmlp_vector_start(dve)
                w = ph["width"]

                def one(i, s, st, t, count, z0=z0, w=w):
                    dve.wait_ge(mm[st], count)
                    nc.vector.tensor_tensor(
                        z[0:w, ds(2 * i + s + z0, 1), tslice(t)],
                        bank[3 * st + t][0:w, 0:344].rearrange("p (a n) -> p a n", a=1),
                        rstd[0:w, t:t + 1, :], ALU.mult).then_inc(evac[st], 1)
                each_tile(dve, ph, one, gmlp_steps(ph, lambda n: gmlp_vector(dve, n)))

        def win_done(eng):
            for j in (0, 1):
                eng.wait_ge(evac[j], WIN_END[j])

        def gmlp_loads(sp):
            sp.wait_ge(S("x_stored"), 16)
            sp.dma_start(gw_nat[:, :, :], A["sgu_w"][0].rearrange("g t s -> t g s"))\
                .then_inc(S("ln_in"), 16)
            sp.wait_ge(S("x_acc"), 48)
            for j, n in enumerate(("sgu_ln_g", "sgu_ln_b")):
                sp.dma_start(ln_gb[:, j, :], A[n][0].partition_broadcast(P)).then_inc(S("ln_in"), 16)
            for hp in (0, 1):
                rows = slice(64 * hp, 64 * hp + 64)
                sp.dma_start(g_bias[rows, :, :], A["sgu_b"][0][hp::2, :].partition_broadcast(64))\
                    .then_inc(S("ln_in"), 16)
                sp.dma_start(g_w00[rows, :], A["sgu_w"][0][hp::2, 0, 0].partition_broadcast(64),
                             allow_slow_non_contiguous=True)\
                    .then_inc(S("ln_in"), 16)

        def gmlp_tensor_start(pe):
            pe.wait_ge(S("ln_in"), 112)
            pe.wait_ge(S("rms"), 6)
            for g in range(8):
                m = nc.tensor.transpose(bank[6 + g // 4][:, (g % 4) * P:(g % 4 + 1) * P],
                                        gw_nat[:, g, :], ident)
                if g % 4 == 3:
                    m.then_inc(S("gwt"), 1)

        def gmlp_tensor(pe, n):
            if n == 0:
                pe.wait_ge(S("gwT"), 2)
                pe.wait_ge(S("gelu"), 1)
            elif n < 9:
                pe.wait_ge(S("vn"), n)
                pe.wait_ge(S("gmix"), n - 1)
                for g in range(8):
                    m = nc.tensor.matmul(
                        bank[7][64 * (g % 2):64 * (g % 2) + 64, (g // 2) * P:(g // 2 + 1) * P],
                        vn[:, (n - 1) % 2, 64 * g:64 * g + 64], gwT[:, g, :], start=True, stop=True)
                m.then_inc(S("mixed"), 1)
            if n < 9:
                tn = P if n < 8 else NS
                pe.wait_ge(S("vn0"), n)
                for j in range(4):
                    m = nc.tensor.transpose(bank[6][0:tn, j * P:(j + 1) * P],
                                            z[:, 12 + j, n * P:n * P + tn], ident)
                m.then_inc(S("vtok"), 1)
            else:
                pe.wait_ge(S("vn"), 9)
                pe.wait_ge(S("gmix"), 8)
                for j in range(4):
                    m = nc.tensor.transpose(bank[7][:, j * NS:(j + 1) * NS],
                                            vn[0:NS, 2, j * P:(j + 1) * P], ident[0:NS, 0:NS])
                m.then_inc(S("mixed"), 1)

        def gmlp_scalar(act):
            for j in (0, 1):
                act.wait_ge(evac[j], win_a["mm1"][j])
            nc.scalar.activation(z[:, 12:16, :], z[:, 12:16, :], ACT.Gelu_apprx_tanh).then_inc(S("gelu"), 1)
            nc.scalar.activation(z[:, 8:12, :], z[:, 8:12, :], ACT.Gelu_apprx_tanh).then_inc(S("gelu"), 1)
            for n in range(9):
                tn = P if n < 8 else NS
                act.wait_ge(S("gvar"), n + 1)
                nc.scalar.activation(g_stat[0:tn, n % 2, 6:7], g_stat[0:tn, n % 2, 7:8], ACT.Sqrt,
                                     bias=eps_t[0:tn, 1:2]).then_inc(S("gelu"), 1)

        def gmlp_vector_start(dve):
            dve.wait_ge(S("ln_in"), 112)
            for b in (0, 1):
                dve.wait_ge(S("gwt"), b + 1)
                nc.vector.tensor_tensor(gwT[:, 4 * b:4 * b + 4, :],
                                        bank[6 + b][:, :].rearrange("p (g t) -> p g t", g=4),
                                        cst[:, C_TRI:C_TRI + 1, :].to_broadcast([P, 4, P]), ALU.mult)\
                    .then_inc(S("gwT"), 1)

        def gmlp_mixed(dve, n):
            dve.wait_ge(S("mixed"), n + 1)
            b = n % 2
            if n < 8:
                link(nc.vector.tensor_tensor(
                    g_mix[:, b, :], bank[7][:, :], g_bias[:, :, :].rearrange("p k t -> p (k t)"),
                    ALU.add))
                us = z[:, 8:12, n * P:(n + 1) * P]
                nc.vector.tensor_tensor(us, g_mix[:, b, :].rearrange("p (k t) -> p k t", k=4), us,
                                        ALU.mult).then_inc(S("gmix"), 1)
            else:
                gm = g_mix[:, b, 0:4 * NS].rearrange("p (k t) -> p k t", k=4)
                link(nc.vector.tensor_tensor(
                    gm, bank[7][:, 0:4 * NS].rearrange("p (k t) -> p k t", k=4),
                    g_w00[:, :].unsqueeze(2).to_broadcast([P, 4, NS]), ALU.mult))
                link(nc.vector.tensor_tensor(
                    gm, gm, g_bias[:, :, 0:1].to_broadcast([P, 4, NS]), ALU.add))
                us = z[:, 8:12, SEQ:T]
                nc.vector.tensor_tensor(us, gm, us, ALU.mult).then_inc(S("gmix"), 1)

        def gmlp_vector(dve, n):
            if n == 0:
                dve.wait_ge(S("gelu"), 2)
                dve.wait_ge(S("x_stored"), 16)
            if n < 9:
                tn, b = (P if n < 8 else NS), n % 2
                v = vn[0:tn, b if n < 8 else 2, :]
                dve.wait_ge(S("vtok"), n + 1)
                link(nc.vector.bn_stats(g_stat[0:tn, b, 0:6], bank[6][0:tn, :]))
                link(nc.vector.bn_aggr(g_stat[0:tn, b, 6:8], g_stat[0:tn, b, 0:6]))
                nc.vector.tensor_copy(g_stat[0:tn, b, 0:1], g_stat[0:tn, b, 6:7]).then_inc(S("gvar"), 1)
                dve.wait_ge(S("gelu"), 2 + n + 1)
                link(nc.vector.reciprocal(g_stat[0:tn, b, 1:2], g_stat[0:tn, b, 6:7]))
                if 2 <= n < 8:
                    dve.wait_ge(S("mixed"), n - 1)
                nc.vector.tensor_scalar(v, bank[6][0:tn, :], g_stat[0:tn, b, 0:1], g_stat[0:tn, b, 1:2],
                                        ALU.subtract, ALU.mult).then_inc(S("vn0"), 1)
                dve.wait_ge(S("vn0"), n + 1)
                link(nc.vector.tensor_tensor(v, v, ln_gb[0:tn, 0, :], ALU.mult))
                nc.vector.tensor_tensor(v, v, ln_gb[0:tn, 1, :], ALU.add).then_inc(S("vn"), 1)
            if n > 0:
                gmlp_mixed(dve, n - 1)
            if n == 9:
                nc.vector.memset(lora_w[:, :, :], 0.0).then_inc(S("gmix"), 1)

        def pw(j):
            return P if j < NBT - 1 else NB - (NBT - 1) * P

        def shift_tensor(pe):
            pe.wait_ge(S("gwT"), 2)
            for j in range(NBT):
                m = nc.tensor.transpose(bank[4 + j // 4][0:NS + 1, (j % 4) * P:(j % 4) * P + pw(j)],
                                        z[0:pw(j), ZB[j], SEQ - 1:T], ident[0:pw(j), 0:pw(j)])
                if j % 4 == 3 or j == NBT - 1:
                    m.then_inc(S("shift_t"), 1)
            pe.wait_ge(S("prep_in"), 16)
            for j in range(NBT):
                m = nc.tensor.transpose(bank[3][0:pw(j), j * NS:(j + 1) * NS],
                                        shift_in[:, j * P:j * P + pw(j)], ident[0:NS, 0:NS])
            m.then_inc(S("shift_t"), 1)

        def prep_tensor(pe):
            win_done(pe)
            pe.wait_ge(S("gmix"), 9)
            shift_tensor(pe)
            pe.wait_ge(S("lora_in"), 32)
            pe.wait_ge(S("shift_a"), 5)
            for m in range(24):
                which, ht, t = m // 12, m % 12 // 3, m % 3
                pe.wait_ge(S("lora_ev"), max(m - 7, 0))
                nc.tensor.matmul(bank[m % 8][:, 0:344], lora_w[:, which, ht * P:(ht + 1) * P],
                                 z[:, 4, tslice(t)], start=True, stop=True).then_inc(S("lora"), 1)
            for m in range(12):
                ht, t = m // 3, m % 3
                pe.wait_ge(S("ksq"), ht + 1)
                pe.wait_ge(S("lora_ev"), min(24, m + 17))
                pe.wait_ge(S("kmax"), max(m - 7, 0))
                nc.tensor.matmul(bank[m % 8][:, 0:344], cst[:, C_BLK, :], diff[:, 4 + ht, tslice(t)],
                                 start=True, stop=True).then_inc(S("ksum"), 1)

        def shift_scalar(act):
            for b in range(4):
                act.wait_ge(S("shift_t"), b + 1)
                wd = 512 if b < 3 else NB - 3 * 512
                nc.scalar.activation(shift_out[:, b * 512:b * 512 + wd], bank[4 + b][0:NS + 1, 0:wd],
                                     ACT.Copy).then_inc(S("shift_a"), 1)

        def prep_scalar(act):
            act.wait_ge(S("mix_p"), 5)
            nc.scalar.activation(z[0:64, 4, :], z[0:64, 4, :], ACT.Tanh).then_inc(S("shift_a"), 1)
            for ht in range(4):
                act.wait_ge(S("kk0"), ht + 1)
                nc.scalar.activation(diff[:, 4 + ht, :], nkk[:, ht, :], ACT.Square).then_inc(S("ksq"), 1)
            for m in range(24):
                which, ht, t = m // 12, m % 12 // 3, m % 3
                if m == 12:
                    act.wait_ge(S("state_stored"), 32)
                    act.wait_ge(S("shifted"), 8)
                act.wait_ge(S("lora"), m + 1)
                dst, b = ((sg, "rwkv_w0"), (bvec, "rwkv_a0"))[which]
                nc.scalar.activation(dst[:, ht, tslice(t)], bank[m % 8][:, 0:344], ACT.Sigmoid,
                                     bias=v_col(b, ht)).then_inc(S("lora_ev"), 1)
            act.wait_ge(S("kmax"), 12)
            nc.scalar.activation(diff[:, 4:8, :], diff[:, 4:8, :], ACT.Ln, scale=float(2 ** 20))\
                .then_inc(S("kln"), 1)
            act.wait_ge(S("kln"), 1)
            nc.scalar.activation(diff[:, 4:8, :], diff[:, 4:8, :], ACT.Exp, scale=-0.5,
                                 bias=eps_t[:, 3:4]).then_inc(S("kln"), 1)

        def shift_vector(dve):
            dve.wait_ge(S("shift_t"), 5)
            nc.vector.tensor_copy(shiftT[:, 0:NBT - 1, :],
                                  bank[3][:, 0:(NBT - 1) * NS].rearrange("p (k t) -> p k t", t=NS))\
                .then_inc(S("shift_v"), 1)
            nc.vector.tensor_copy(shiftT[0:32, NBT - 1, :], bank[3][0:32, (NBT - 1) * NS:NBT * NS])\
                .then_inc(S("shift_v"), 1)
            dve.wait_ge(S("shift_v"), 2)

        def shift_pool(g):
            TT = nc.gpsimd.tensor_tensor
            g.wait_ge(S("shift_v"), 2)
            g.wait_ge(S("shift_t"), 4)
            for n, i in enumerate((4, 0, 1, 2, 3, 5, 6)):
                rows = P if i < 6 else 32
                d, zz = diff_p[0:rows, :], z[0:rows, i, :]
                g.wait_ge(S("mix_p"), 5 * n)
                TT(d[:, 1:SEQ], zz[:, 0:SEQ - 1], zz[:, 1:SEQ], ALU.subtract).then_inc(S("mix_p"), 1)
                TT(d[:, 0:1], cst[0:rows, C_STR, 0:1], zz[:, 0:1], ALU.subtract).then_inc(S("mix_p"), 1)
                TT(d[:, SEQ:T], shiftT[0:rows, 8 + i, :], zz[:, SEQ:T],
                   ALU.subtract).then_inc(S("mix_p"), 1)
                g.wait_ge(S("mix_p"), 5 * n + 3)
                TT(d, d, v_col("rwkv_mu", 8 + i)[0:rows].to_broadcast([rows, T]), ALU.mult)\
                    .then_inc(S("mix_p"), 1)
                g.wait_ge(S("mix_p"), 5 * n + 4)
                TT(zz, zz, d, ALU.add).then_inc(S("mix_p"), 1)

        def prep_vector(dve):
            done = 0
            for j0 in (4, 0):
                z0, d0 = ZB[j0], j0
                d, zz = diff[:, d0:d0 + 4, :], z[:, z0:z0 + 4, :]
                if j0 == 0:
                    dve.wait_ge(S("ya_stored"), 16)
                link(nc.vector.tensor_tensor(d[:, :, 1:SEQ], zz[:, :, 0:SEQ - 1], zz[:, :, 1:SEQ],
                                             ALU.subtract), False)
                link(nc.vector.tensor_scalar(d[:, :, 0:1], zz[:, :, 0:1], -1.0, None, ALU.mult), False)
                link(nc.vector.tensor_tensor(d[:, :, SEQ:T], shiftT[:, j0:j0 + 4, :],
                                             zz[:, :, SEQ:T], ALU.subtract))
                for j in range(4):
                    nc.vector.scalar_tensor_tensor(
                        out=z[:, z0 + j, :], in0=diff[:, d0 + j, :],
                        scalar=v_col("rwkv_mu", j0 + j), in1=z[:, z0 + j, :],
                        op0=ALU.mult, op1=ALU.add).then_inc(S("shifted"), 1)
                    done += 1
                if j0 == 4:
                    dve.wait_ge(S("shifted"), done)
                    dve.wait_ge(S("vchunk_stored"), 16)
                    for ht in range(4):
                        nc.vector.tensor_scalar(nkk[:, ht, :], z[:, 20 + ht, :],
                                                v_col("rwkv_k_k", ht), None,
                                                ALU.mult).then_inc(S("kk0"), 1)
            dve.wait_ge(S("shifted"), done)
            dve.wait_ge(S("gwt"), 2)
            link(nc.vector.memset(scan_mask[:, :], 1.0))
            link(nc.vector.memset(scan_mask[:, 0:SEQ:CH], 0.0), False)
            link(nc.vector.memset(scan_mask[:, SEQ:T], 0.0))
            dve.wait_ge(S("lora_ev"), 12)
            for ht in range(4):
                link(nc.vector.tensor_tensor_scan(cum[:, ht, :], scan_mask[:, :], sg[:, ht, :], 0.0,
                                                  ALU.mult, ALU.add), False)
            nc.vector.memset(st_T[:, 0, :, :], 0.0).then_inc(S("st0"), 1)
            nc.vector.memset(Us[:, :], 0.0).then_inc(S("st0"), 1)
            for m in range(12):
                ht, t = m // 3, m % 3
                dve.wait_ge(S("ksum"), m + 1)
                nc.vector.tensor_scalar(diff[:, 4 + ht, tslice(t)], bank[m % 8][:, 0:344],
                                        float(HN), 1e-24, ALU.mult, ALU.max).then_inc(S("kmax"), 1)
            dve.wait_ge(S("lora_ev"), 24)
            for ht in range(4):
                link(nc.vector.tensor_scalar(diff[:, ht, :], bvec[:, ht, :], 1.0,
                                             v_col("rwkv_k_a", ht), ALU.subtract, ALU.mult))
                link(nc.vector.scalar_tensor_tensor(out=z[:, 20 + ht, :], in0=diff[:, ht, :],
                                                    scalar=1.0, in1=z[:, 20 + ht, :], op0=ALU.add,
                                                    op1=ALU.mult), False)
            dve.wait_ge(S("kln"), 2)
            for t in range(3):
                link(nc.vector.scalar_tensor_tensor(out=nkk[:, :, tslice(t)], in0=nkk[:, :, tslice(t)],
                                                    scalar=-1.0, in1=diff[:, 4:8, tslice(t)],
                                                    op0=ALU.mult, op1=ALU.mult), t == 2)
            rates_vector(0)

        def rates_vector(t):
            link(nc.vector.scalar_tensor_tensor(out=bvec[:, :, tslice(t)], in0=nkk[:, :, tslice(t)],
                                                scalar=-1.0, in1=bvec[:, :, tslice(t)],
                                                op0=ALU.mult, op1=ALU.mult))

        NLV = LEVELS - 1

        def part(name, g):
            return mats[g // 2][name][:, 2 * (g % 2):2 * (g % 2) + 2, :]

        def pair(b):
            return bank[b][:, 0:256].rearrange("p (j t) -> p j t", j=2)

        def scale_scalar(act, n):
            c = slice(n * P, (n + 1) * P)
            act.wait_ge(S("ediff"), n + 1)
            nc.scalar.activation(ext[:, :, :], ext[:, :, :], ACT.Exp, scale=-DECAY)\
                .then_inc(S("exps"), 1)
            act.wait_ge(S("decm"), 2 * n)
            act.wait_ge(S("R_made"), n)
            nc.scalar.activation(dec[:, :, :], cum[:, :, c], ACT.Exp, scale=-DECAY).then_inc(S("exps"), 1)
            act.wait_ge(S("tok_t"), 3 * n)
            act.wait_ge(S("mix_p"), 25)
            nc.scalar.activation(vstage[:, :, :], z[:, 0:4, c], ACT.Copy).then_inc(S("v_staged"), 1)
            act.wait_ge(S("A_made"), n + 1)
            nc.scalar.activation(ext[:, :, :], cum[:, :, c], ACT.Exp, scale=DECAY).then_inc(S("exps"), 1)

        def chunk_scalar(act, n):
            c = slice(n * P, (n + 1) * P)
            if n == 0:
                scale_scalar(act, 0)
            act.wait_ge(S("tok_t"), 3 * n + 3)
            act.wait_ge(S("state_t"), 4 * n)
            act.wait_ge(S("out_t"), 2 * n)
            nc.scalar.activation(Vt[:, :], bank[6][:, :], ACT.Copy).then_inc(S("tok_ev"), 1)
            for q in (0, 1):
                for b in (0, 1):
                    act.wait_ge(S("pair"), 8 * n + 4 * q + b + 1)
                    if b == 0:
                        act.wait_ge(S("Loff_masked"), max(2 * NLV * n + q - 1, 0))
                        act.wait_ge(S("T_start"), 4 * n)
                    nc.scalar.activation(
                        LQ[q][:, :, b::2, :],
                        bank[4 * q + b][:, :].rearrange("p (j a t) -> p a j t", j=2, a=2),
                        ACT.Copy).then_inc(S("LQ_ev"), 1)
            for lv in range(NLV):
                for g in range(4):
                    act.wait_ge(S("Y_t"), 4 * (NLV * n + lv) + g + 1)
                    nc.scalar.activation(part("Y", g), pair(2 * g + 1 - lv % 2), ACT.Copy)\
                        .then_inc(S("Y_ev"), 1)
            if n < 7:
                scale_scalar(act, n + 1)
            for ck in (0, 1):
                r, e0 = slice(64 * ck, 64 * ck + 64), 4 * n + 2 * ck
                for q in (0, 1):
                    cols = slice(q * 256, q * 256 + 256)
                    act.wait_ge(S("X_t"), e0 + q + 1)
                    nc.scalar.activation(Xs[r, cols], bank[4 * q + 3][r, 0:256], ACT.Copy)\
                        .then_inc(S("X_ev"), 1)
                for q in (0, 1):
                    cols = slice(q * 256, q * 256 + 256)
                    act.wait_ge(S("U_t"), e0 + q + 1)
                    act.wait_ge(S("out_t"), 2 * n)
                    nc.scalar.activation(Us[r, cols], bank[4 * q][r, 0:256], ACT.Copy)\
                        .then_inc(S("U_ev"), 1)
            for q in (0, 1):
                act.wait_ge(S("out_t"), 2 * n + q + 1)
                nc.scalar.activation(
                    nkk[:, 2 * q:2 * q + 2, c],
                    bank[4 * q + 2][:, 0:256].rearrange("p (k t) -> p k t", k=2),
                    ACT.Copy).then_inc(S("out_ev"), 1)

        def chunk_pool(g, n):
            for ck in (0, 1):
                g.wait_ge(S("exps"), 3 * n + 2)
                g.wait_ge(S("state_made"), 4 * n)
                end = 64 * ck + 63
                nc.gpsimd.tensor_tensor(decm[:, ck], dec[:, :, end:end + 1].to_broadcast([P, 4, P]),
                                        cst[:, C_BLK:C_BLK + 1, :].to_broadcast([P, 4, P]),
                                        ALU.mult).then_inc(S("decm"), 1)
            for lv in range(1, NLV + 1):
                for q in (0, 1):
                    if lv == 1:
                        g.wait_ge(S("LQ_ev"), 4 * n + 2 * q + 2)
                    if lv == 2:
                        nc.gpsimd.tensor_tensor(mats[q]["QBT"], mats[q]["QBT"],
                                                cst[:, C_INC:C_INC + 1, :].to_broadcast([P, 4, P]),
                                                ALU.mult).then_inc(S("QB_masked"), 1)
                    if NLV * n + lv > 1:
                        g.wait_ge(S("Y_t"), 4 * (NLV * n + lv - 2) + 2 * q + 2)
                    nc.gpsimd.tensor_tensor(mats[q]["LoT"][:, :, :], mats[q]["LT"][:, :, :],
                                            cst[:, C_LVL + lv:C_LVL + lv + 1, :].to_broadcast([P, 4, P]),
                                            ALU.mult).then_inc(S("Loff_masked"), 1)

        def scale_vector(dve, n):
            c = slice(n * P, (n + 1) * P)
            TT = nc.vector.tensor_tensor
            dve.wait_ge(S("BK_made"), 2 * n)
            TT(ext[:, :, :], cum[:, :, c], sg[:, :, c], ALU.subtract).then_inc(S("ediff"), 1)
            dve.wait_ge(S("exps"), 3 * n + 1)
            dve.wait_ge(S("pair"), 8 * n)
            dve.wait_ge(S("tok_t"), 3 * n)
            dve.wait_ge(S("out_t"), max(2 * n - 2, 0))
            TT(AR[n % 2][:, 0, :, :], nkk[:, :, c], ext[:, :, :], ALU.mult).then_inc(S("A_made"), 1)
            dve.wait_ge(S("exps"), 3 * n + 2)
            TT(AR[n % 2][:, 1, :, :], z[:, 16:20, c], dec[:, :, :], ALU.mult).then_inc(S("R_made"), 1)
            dve.wait_ge(S("exps"), 3 * n + 3)
            TT(BK[:, 0, :, :], bvec[:, :, c], ext[:, :, :], ALU.mult).then_inc(S("BK_made"), 1)
            TT(BK[:, 1, :, :], z[:, 20:24, c], ext[:, :, :], ALU.mult).then_inc(S("BK_made"), 1)

        def chunk_vector(dve, n):
            TT = nc.vector.tensor_tensor
            if n == 0:
                scale_vector(dve, 0)
            for j, dst in enumerate((Bt, Kt)):
                dve.wait_ge(S("tok_t"), 3 * n + j + 1)
                dve.wait_ge(S("state_t"), 4 * n)
                nc.vector.tensor_copy(dst[:, :], bank[4 + j][:, :]).then_inc(S("tok_ev"), 1)

            def pv(b, a):
                return bank[b][:, :].rearrange("p (j a t) -> p j a t", j=2, a=2)[:, :, a, :]
            for q in (0, 1):
                m = mats[q]
                msk = lambda k: cst[:, k:k + 1, :].to_broadcast([P, 2, P])
                for b in (0, 1):
                    hs = slice(b, 4, 2)
                    dve.wait_ge(S("LQ_ev"), 4 * n + 2 * q + b + 1)
                    if b == 0:
                        dve.wait_ge(S("U_t"), 4 * n)
                        dve.wait_ge(S("X_t"), 4 * n)
                        dve.wait_ge(S("T_level"), 4 * NLV * n)
                    TT(m["TT"][:, hs, :], m["LT"][:, hs, :], msk(C_LVL), ALU.mult)\
                        .then_inc(S("T_start"), 1)
                    dve.wait_ge(S("T_start"), 4 * n + 2 * q + b + 1)
                    TT(m["TT"][:, hs, :], m["TT"][:, hs, :], msk(C_ID), ALU.add).then_inc(S("T_ident"), 1)
                for b in (0, 1):
                    hs = slice(b, 4, 2)
                    dve.wait_ge(S("pair"), 8 * n + 4 * q + 2 + b + 1)
                    TT(m["MT"][:, hs, :], pv(4 * q + 2 + b, 0), msk(C_STR), ALU.mult)\
                        .then_inc(S("kmat_masked"), 1)
                    TT(m["QKT"][:, hs, :], pv(4 * q + 2 + b, 1), msk(C_INC), ALU.mult)\
                        .then_inc(S("kmat_masked"), 1)
            for lv in range(NLV):
                for g in range(4):
                    dve.wait_ge(S("T_flip"), 4 * (NLV * n + lv) + g + 1)
                    nc.vector.tensor_copy(part("Ti", g), pair(2 * g + lv % 2)).then_inc(S("T_flip_ev"), 1)
                for g in range(4):
                    dve.wait_ge(S("D_t"), 4 * (NLV * n + lv) + g + 1)
                    TT(part("TT", g), part("TT", g), pair(2 * g + lv % 2), ALU.add)\
                        .then_inc(S("T_level"), 1)
            if n < 7:
                scale_vector(dve, n + 1)
            else:
                for ht in range(4):
                    nc.vector.scalar_tensor_tensor(
                        out=cum[:, ht, :], in0=z[:, 16 + ht, :], scalar=v_col("rwkv_r_k", ht),
                        in1=z[:, 20 + ht, :], op0=ALU.mult, op1=ALU.mult).then_inc(S("bo2"), 1)
            for ck in (0, 1):
                e0 = 4 * n + 2 * ck
                for q in (0, 1):
                    hs = slice(2 * q, 2 * q + 2)
                    dve.wait_ge(S("state_t"), e0 + q + 1)
                    dve.wait_ge(S("state_made"), max(e0 + q - 1, 0))
                    dve.wait_ge(S("out_t"), 2 * n)
                    TT(st_T[:, (2 * n + ck + 1) % 3, hs, :], st_T[:, (2 * n + ck) % 3, hs, :],
                       bank[4 * q + 1][:, 0:256].rearrange("p (k v) -> p k v", k=2), ALU.add)\
                        .then_inc(S("state_add"), 1)
                for q in (0, 1):
                    hs = slice(2 * q, 2 * q + 2)
                    new = st_T[:, (2 * n + ck + 1) % 3, hs, :]
                    dve.wait_ge(S("state_add"), e0 + q + 1)
                    dve.wait_ge(S("decm"), 2 * n + ck + 1)
                    nc.vector.scalar_tensor_tensor(out=new, in0=new, scalar=float(HN),
                                                   in1=decm[:, ck, hs, :], op0=ALU.mult,
                                                   op1=ALU.mult).then_inc(S("state_made"), 1)
            if n < 2:
                rates_vector(n + 1)

        def chunk_tensor(pe, n):
            mmul = nc.tensor.matmul
            heads = lambda q: [(j, (4 * q + j) // 2, (4 * q + j) % 2) for j in range(4)]
            pe.wait_ge(S("BK_made"), 2 * n + 2)
            pe.wait_ge(S("out_ev"), 2 * n)
            pe.wait_ge(S("state_add"), 4 * n)
            for j, src in enumerate((BK[:, 0], BK[:, 1], vstage[:, :, :])):
                if j == 2:
                    pe.wait_ge(S("v_staged"), n + 1)
                for ht in range(4):
                    m = nc.tensor.transpose(bank[4 + j][:, ht * P:(ht + 1) * P], src[:, ht, :], ident)
                m.then_inc(S("tok_t"), 1)
            for q in (0, 1):
                if q == 1:
                    pe.wait_ge(S("tok_ev"), 3 * n + 3)
                for side in (0, 1):
                    for j, ht, hp in sorted(heads(q), key=lambda x: x[2]):
                        r = slice(64 * hp, 64 * hp + 64)
                        m = mmul(bank[4 * q + 2 * side + hp][:, (j // 2) * 256:(j // 2) * 256 + 256],
                                 BK[r, side, ht, :], AR[n % 2][r, :, ht, :], start=True, stop=True)
                        if j >= 2:
                            m.then_inc(S("pair"), 1)
            for lv in range(NLV):
                for g in range(4):
                    q = g // 2
                    if lv == 0:
                        pe.wait_ge(S("T_ident"), 4 * n + 2 * q + 2)
                        pe.wait_ge(S("kmat_masked"), 8 * n + 4 * q + 4)
                        pe.wait_ge(S("LQ_ev"), 4 * n + 2 * q + 2)
                    else:
                        pe.wait_ge(S("T_level"), 4 * (NLV * n + lv - 1) + g + 1)
                    for j in (0, 1):
                        m = nc.tensor.transpose(bank[2 * g + lv % 2][:, j * P:(j + 1) * P],
                                                part("TT", g)[:, j, :], ident)
                    m.then_inc(S("T_flip"), 1)
                for g in range(4):
                    pe.wait_ge(S("Loff_masked"), 2 * (NLV * n + lv) + g // 2 + 1)
                    pe.wait_ge(S("T_flip_ev"), 4 * (NLV * n + lv) + g + 1)
                    for j in (0, 1):
                        m = mmul(bank[2 * g + 1 - lv % 2][:, j * P:(j + 1) * P],
                                 part("LoT", g)[:, j, :], part("Ti", g)[:, j, :], start=True, stop=True)
                    m.then_inc(S("Y_t"), 1)
                for g in range(4):
                    pe.wait_ge(S("Y_ev"), 4 * (NLV * n + lv) + g + 1)
                    for j in (0, 1):
                        m = mmul(bank[2 * g + lv % 2][:, j * P:(j + 1) * P],
                                 part("Y", g)[:, j, :], part("TT", g)[:, j, :], start=True, stop=True)
                    m.then_inc(S("D_t"), 1)
            pe.wait_ge(S("T_level"), 4 * NLV * (n + 1))

            def out_v(q):
                pe.wait_ge(S("out_ev"), max(2 * n + q - 1, 0))
                for j, ht, hp in heads(q):
                    hc = slice((4 * q + j) * 64, (4 * q + j + 1) * 64)
                    mmul(bank[4 * q + 2][64 * hp:64 * hp + 64, (j // 2) * P:(j // 2 + 1) * P],
                         Vt[:, hc], mats[q]["QKT"][:, j, :], start=j < 2, stop=False,
                         skip_group_check=True)

            def out_u(q):
                pe.wait_ge(S("QB_masked"), 2 * n + q + 1)
                for j, ht, hp in heads(q):
                    hc = slice((4 * q + j) * 64, (4 * q + j + 1) * 64)
                    mmul(bank[4 * q + 2][64 * hp:64 * hp + 64, (j // 2) * P:(j // 2 + 1) * P],
                         Us[:, hc], mats[q]["QBT"][:, j, :], start=False, stop=False,
                         skip_group_check=True)

            def out_state(q, ck):
                for k in (0, 1):
                    m = mmul(bank[4 * q + 2][:, k * P + 64 * ck:k * P + 64 * ck + 64],
                             st_T[:, (2 * n + ck) % 3, 2 * q + k, :],
                             AR[n % 2][:, 1, 2 * q + k, 64 * ck:64 * ck + 64],
                             start=False, stop=ck == 1, skip_group_check=True)
                return m
            for ck in (0, 1):
                t, e0 = slice(64 * ck, 64 * ck + 64), 4 * n + 2 * ck
                for q in (0, 1):
                    pe.wait_ge(S("state_made"), max(e0 + q - 1, 0))
                    pe.wait_ge(S("X_ev"), max(e0 - 1 + q, 0))
                    if n == 0 and ck == 0:
                        pe.wait_ge(S("st0"), 2)
                    for k in (0, 1):
                        ht = 2 * q + k
                        mmul(bank[4 * q + 3][t, k * P:(k + 1) * P], AR[n % 2][:, 0, ht, t],
                             st_T[:, (2 * n + ck) % 3, ht, :], start=True, stop=False)
                        for hp in (0, 1):
                            j = 2 * k + hp
                            hc = slice((2 * ht + hp) * 64, (2 * ht + hp + 1) * 64)
                            m = mmul(bank[4 * q + 3][t, j * 64:(j + 1) * 64], mats[q]["MT"][:, j, t],
                                     Vt[:, hc], start=False, stop=hp == 1)
                    m.then_inc(S("X_t"), 1)
                if ck == 0:
                    out_v(0)
                for q in (0, 1):
                    pe.wait_ge(S("X_ev"), e0 + q + 1)
                    pe.wait_ge(S("U_ev"), max(e0 + q - 1, 0))
                    for j, ht, hp in heads(q):
                        hc = slice((4 * q + j) * 64, (4 * q + j + 1) * 64)
                        m = mmul(bank[4 * q][t, j * 64:(j + 1) * 64], mats[q]["TT"][t, j, t], Xs[t, hc],
                                 start=True, stop=True)
                    m.then_inc(S("U_t"), 1)
                if ck == 0:
                    out_v(1)
                for q in (0, 1):
                    pe.wait_ge(S("U_ev"), e0 + q + 1)
                    pe.wait_ge(S("state_add"), max(e0 + q - 1, 0))
                    for k in (0, 1):
                        hc = slice((2 * q + k) * P, (2 * q + k + 1) * P)
                        o = bank[4 * q + 1][:, k * P:(k + 1) * P]
                        mmul(o, Kt[t, hc], Vt[t, hc], start=True, stop=False)
                        m = mmul(o, Bt[t, hc], Us[t, hc], start=False, stop=True)
                    m.then_inc(S("state_t"), 1)
                if ck == 0:
                    for q in (0, 1):
                        out_state(q, 0)
            for q in (0, 1):
                out_u(q)
                out_state(q, 1).then_inc(S("out_t"), 1)

        SMP = [lambda ht: smp_w[:, ht, :], lambda ht: nkk[:, ht, SEQ:T], lambda ht: bvec[:, ht, SEQ:T],
               lambda ht: z[:, 20 + ht, SEQ:T], lambda ht: z[:, 16 + ht, SEQ:T],
               lambda ht: z[:, ht, SEQ:T]]

        def sample_loads(sp):
            sp.wait_ge(S("out_ev"), 16)
            sp.dma_start(smp_S[:, :, :], A["state_rwkv"][0].rearrange("b h (w v) k -> (b h w) v k", w=2))\
                .then_inc(S("post_in"), 16)
            sp.wait_ge(S("decm"), 16)
            sp.dma_start(g2_w[:, 0, :], A["rwkv_g2"][0][0:P, :]).then_inc(S("post_in"), 16)
            sp.dma_start(g2_w[0:32, 1, :], A["rwkv_g2"][0][P:P + 32, :]).then_inc(S("post_in"), 16)
            sp.wait_ge(S("smp_a"), 8)
            sp.dma_start(smp_d.rearrange("i b n -> b i n"), smp_n[:, :, :]).then_inc(S("smp_in"), 16)
            sp.wait_ge(S("smp_in"), 16)
            for w in (0, 1):
                sp.dma_start(smp_v[w::2, 0:5, :], smp_d[0:5].rearrange("i b (h d) -> (b h) i d", h=HEADS))\
                    .then_inc(S("smp_in"), 16)
            sp.dma_start(smp_v[:, 5, 0:32], smp_d[5].rearrange("b (h d) -> (b h) d", d=32))\
                .then_inc(S("smp_in"), 16)
            sp.wait_ge(S("smp_a"), 2)
            for hp in (0, 1):
                r = slice(64 * hp, 64 * hp + 64)
                sp.dma_start(O["state_rwkv_prompt"][0, 0, hp::2].rearrange("h v k -> v h k"),
                             st_out[r, :, r]).then_inc(S("state_stored"), 16)
            sp.wait_ge(S("smp_v"), 1)
            sp.dma_start(smp_od.rearrange("b (h d) -> (b h) d", d=32), smp_o[:, 1, :])\
                .then_inc(S("smp_in"), 16)
            sp.dma_start(O["state_rwkv_sample"][0].rearrange("b h (w v) k -> (b h w) v k", w=2),
                         smp_S[:, :, :]).then_inc(S("state_stored"), 16)
            sp.wait_ge(S("smp_in"), 80)
            sp.dma_start(smp_on[:, :], smp_od).then_inc(S("smp_in"), 16)

        POST = ((0, 8), (8, 12))

        def ln_count(m):
            return m + 1 + (m >= 8)

        def post_scalar(act):
            act.wait_ge(S("out_ev"), 16)
            act.dma_start(mem_n[:, :, :], A["mem_prompt"][0].rearrange("(m p) d -> p m d", p=P))\
                .then_inc(S("mem_in"), 16)
            nc.scalar.activation(smp_w[:, :, :], sg[:, :, SEQ:T], ACT.Exp, scale=-DECAY)\
                .then_inc(S("smp_a"), 1)
            act.wait_ge(S("smp_t"), 1)
            nc.scalar.activation(st_out[:, :, :], bank[6][:, :].rearrange("p (k n) -> p k n", k=4),
                                 ACT.Copy).then_inc(S("smp_a"), 1)
            for i in range(6):
                act.wait_ge(S("smp_t"), i + 2)
                nc.scalar.activation(smp_n[:, i, :], bank[i][0:NS, :], ACT.Copy).then_inc(S("smp_a"), 1)
            act.dma_start(ya_in[:, :, :], y_save).then_inc(S("ya_in"), 16)
            act.wait_ge(S("mix_p"), 35)
            nc.scalar.activation(z[:, 5, :], z[:, 5, :], ACT.Sigmoid).then_inc(S("sgd"), 1)
            nc.scalar.activation(z[0:32, 6, :], z[0:32, 6, :], ACT.Sigmoid).then_inc(S("sgd"), 1)
            for m0, m1 in POST:
                for m in range(m0, m1 + 1):
                    if m < m1:
                        ht, t = m % 4, m // 4
                        act.wait_ge(S("gn_c"), m + 1)
                        act.wait_ge(S("gn_v"), max(m - 2, 0))
                        nc.scalar.activation(gn_sq[:, m % 3, :], nkk[:, ht, tslice(t)], ACT.Square)\
                            .then_inc(S("gn_q"), 1)
                    if m > m0:
                        ht, t = (m - 1) % 4, (m - 1) // 4
                        act.wait_ge(S("gn_v"), m)
                        nc.scalar.activation(sg[:, ht, tslice(t)], bank[2 + (m - 1) % 2][:, 0:344],
                                             ACT.Ln, bias=eps_t[:, 2:3]).then_inc(S("gn_l"), 1)
                act.wait_ge(S("gn_l"), ln_count(m1 - 1))
                c = slice(m0 * 86, m1 * 86)
                nc.scalar.activation(sg[:, :, c], sg[:, :, c], ACT.Exp, scale=-0.5)\
                    .then_inc(S("gn_l"), 1)
                if m0 == 0:
                    act.wait_ge(S("ya_in"), 16)
                    act.wait_ge(S("state_stored"), 80)
                    nc.scalar.activation(y_hi[:, 0:4, :], ya_in[:, :, :], ACT.Copy)\
                        .then_inc(S("yb_hi"), 1)
                for m in range(m0, m1):
                    ht, t = m % 4, m // 4
                    act.wait_ge(S("yb"), m + 1)
                    nc.scalar.activation(y_hi[:, 4 + ht, tslice(t)], nkk[:, ht, tslice(t)], ACT.Copy)\
                        .then_inc(S("yb_hi"), 1)
            for k in range(KD):
                act.dma_start(x[:, k, :], x_save[:, k, :])\
                    .then_inc(S("x_back0") if k == 0 else S("x_back1") if k < 4 else S("x_back2"), 16)

        def post_tensor(pe):
            pe.wait_ge(S("state_made"), 32)
            pe.wait_ge(S("out_ev"), 16)
            for ht in range(4):
                m = nc.tensor.transpose(bank[6][:, ht * P:(ht + 1) * P], st_T[:, 16 % 3, ht, :], ident)
            m.then_inc(S("smp_t"), 1)
            pe.wait_ge(S("smp_a"), 1)
            for i in range(6):
                for ht in range(4):
                    m = nc.tensor.transpose(bank[i][0:NS, ht * P:(ht + 1) * P], SMP[i](ht), ident)
                m.then_inc(S("smp_t"), 1)
            blk = cst[:, C_BLK, :]
            pe.wait_ge(S("smp_a"), 8)
            for m0, m1 in POST:
                if m0 == 8:
                    pe.wait_ge(S("smp_in"), 96)
                    pe.wait_ge(S("yb"), 8)
                    for ht in range(4):
                        tr = nc.tensor.transpose(bank[7][:, ht * NS:(ht + 1) * NS],
                                                 smp_on[:, ht * P:(ht + 1) * P], ident[0:NS, 0:NS])
                    tr.then_inc(S("smp_t"), 1)
                    pe.wait_ge(S("smp_v"), 2)
                for m in range(m0, m1 + 1):
                    if m < m1:
                        ht, t = m % 4, m // 4
                        pe.wait_ge(S("gn_c"), max(m - 1, 0))
                        nc.tensor.matmul(bank[m % 2][:, 0:344], blk, nkk[:, ht, tslice(t)],
                                         start=True, stop=True).then_inc(S("gn_m"), 1)
                    if m > m0:
                        pe.wait_ge(S("gn_q"), m)
                        if m >= 3:
                            pe.wait_ge(S("gn_l"), ln_count(m - 3))
                        nc.tensor.matmul(bank[2 + (m - 1) % 2][:, 0:344], blk, gn_sq[:, (m - 1) % 3, :],
                                         start=True, stop=True).then_inc(S("gn_v"), 1)
                pe.wait_ge(S("sgd"), 2)
                pe.wait_ge(S("post_in"), 48)
                for m in range(m0, m1):
                    ht, t = m % 4, m // 4
                    pe.wait_ge(S("bo2"), 4 + max(m - 1, 0))
                    nc.tensor.matmul(bank[4 + m % 2][:, 0:344], blk, cum[:, ht, tslice(t)],
                                     start=True, stop=True).then_inc(S("bo1"), 1)
                    pe.wait_ge(S("yb"), max(m - 1, 0))
                    nc.tensor.matmul(bank[6 + m % 2][:, 0:344], g2_w[:, 0, ht * P:(ht + 1) * P],
                                     z[:, 5, tslice(t)], start=True, stop=False)
                    nc.tensor.matmul(bank[6 + m % 2][:, 0:344], g2_w[0:32, 1, ht * P:(ht + 1) * P],
                                     z[0:32, 6, tslice(t)], start=False, stop=True).then_inc(S("g2"), 1)

        def smp_over_v(i):
            return smp_v[:, i:i + 1, :].to_broadcast([P, 32, HN])

        def smp_over_k(a):
            return a.unsqueeze(2).to_broadcast([P, 32, HN])

        def sample_pool(g):
            g.wait_ge(S("post_in"), 48)
            g.wait_ge(S("smp_in"), 64)
            nc.gpsimd.tensor_tensor(smp_vk[:, :, :], smp_over_k(smp_v[:, 5, 0:32]), smp_over_v(3),
                                    ALU.mult).then_inc(S("smp_p"), 1)
            g.wait_ge(S("smp_sa"), 1)
            nc.gpsimd.tensor_tensor(smp_S[:, :, :], smp_S[:, :, :], smp_over_v(0), ALU.mult)\
                .then_inc(S("smp_p"), 1)

        def sample_vector(dve):
            TT = nc.vector.tensor_tensor
            dve.wait_ge(S("post_in"), 48)
            dve.wait_ge(S("smp_in"), 64)
            TT(smp_t[:, :, :], smp_S[:, :, :], smp_over_v(1), ALU.mult).then_inc(S("smp_sa"), 1)
            dve.wait_ge(S("smp_sa"), 1)
            link(nc.vector.tensor_reduce(smp_o[:, 0, :], smp_t[:, :, :], AX.X, ALU.add))
            link(TT(smp_t[:, :, :], smp_over_k(smp_o[:, 0, :]), smp_over_v(2), ALU.mult))
            dve.wait_ge(S("smp_p"), 1)
            link(TT(smp_t[:, :, :], smp_t[:, :, :], smp_vk[:, :, :], ALU.add))
            dve.wait_ge(S("smp_p"), 2)
            link(TT(smp_S[:, :, :], smp_S[:, :, :], smp_t[:, :, :], ALU.add))
            link(TT(smp_t[:, :, :], smp_S[:, :, :], smp_over_v(4), ALU.mult))
            nc.vector.tensor_reduce(smp_o[:, 1, :], smp_t[:, :, :], AX.X, ALU.add)\
                .then_inc(S("smp_v"), 1)

        def post_vector(dve):
            TT, STT = nc.vector.tensor_tensor, nc.vector.scalar_tensor_tensor
            for m0, m1 in POST:
                if m0 == 8:
                    dve.wait_ge(S("smp_t"), 8)
                    nc.vector.tensor_copy(nkk[:, :, SEQ:T], bank[7][:, 0:4 * NS].rearrange(
                        "p (k t) -> p k t", k=4)).then_inc(S("smp_v"), 1)
                    dve.wait_ge(S("smp_v"), 2)
                for m in range(m0, m1):
                    ht, t = m % 4, m // 4
                    dve.wait_ge(S("gn_m"), m + 1)
                    TT(nkk[:, ht, tslice(t)], nkk[:, ht, tslice(t)], bank[m % 2][:, 0:344],
                       ALU.subtract).then_inc(S("gn_c"), 1)
                if m0 == 0:
                    sample_vector(dve)
                dve.wait_ge(S("gn_l"), ln_count(m1 - 1) + 1)
                for ht in range(4):
                    c = slice(m0 * 86, m1 * 86)
                    link(STT(out=nkk[:, ht, c], in0=nkk[:, ht, c], scalar=v_col("rwkv_gn_g", ht),
                             in1=sg[:, ht, c], op0=ALU.mult, op1=ALU.mult), ht == 3)
                for m in range(m0, m1):
                    ht, t = m % 4, m // 4
                    o = nkk[:, ht, tslice(t)]
                    dve.wait_ge(S("bo1"), m + 1)
                    STT(out=cum[:, ht, tslice(t)], in0=bank[4 + m % 2][:, 0:344], scalar=float(HN),
                        in1=z[:, ht, tslice(t)], op0=ALU.mult, op1=ALU.mult).then_inc(S("bo2"), 1)
                    dve.wait_ge(S("bo2"), 4 + m + 1)
                    link(STT(out=o, in0=o, scalar=v_col("rwkv_gn_b", ht), in1=cum[:, ht, tslice(t)],
                             op0=ALU.add, op1=ALU.add))
                    dve.wait_ge(S("g2"), m + 1)
                    TT(o, o, bank[6 + m % 2][:, 0:344], ALU.mult).then_inc(S("yb"), 1)

        def post_pool(g):
            g.wait_ge(S("yb"), 1)
            g.wait_ge(S("yb_hi"), 1)
            nc.gpsimd.tensor_tensor(y_lo[:, 0:4, :], ya_in[:, :, :], y_hi[:, 0:4, :].bitcast(F),
                                    ALU.subtract).then_inc(S("yb_lo"), 1)
            for m in range(12):
                ht, t = m % 4, m // 4
                g.wait_ge(S("yb_hi"), m + 2)
                nc.gpsimd.tensor_tensor(y_lo[:, 4 + ht, tslice(t)], nkk[:, ht, tslice(t)],
                                        y_hi[:, 4 + ht, tslice(t)].bitcast(F), ALU.subtract)\
                    .then_inc(S("yb_lo"), 1)

        def mem_scalar_a(act):
            act.wait_ge(S("mem_in"), 16)
            for m in (0, 1):
                act.wait_ge(S("msq"), m)
                nc.scalar.activation(mem_sq[:, :], mem_n[:, m, :], ACT.Square,
                                     accum_out=mem_st[:, m, 0:1]).then_inc(S("msq"), 1)
            act.wait_ge(S("msq"), 2)
            nc.scalar.activation(mem_st[:, :, 1:2], mem_st[:, :, 0:1], ACT.Sqrt, scale=1.0 / D,
                                 bias=eps_t[:, 0:1]).then_inc(S("msq"), 1)

        def mem_vector_a(dve):
            dve.wait_ge(S("msq"), 3)
            link(nc.vector.reciprocal(mem_st[:, :, 2:3], mem_st[:, :, 1:2]))
            for m in (0, 1):
                nc.vector.tensor_scalar(mem_n[:, m, :], mem_n[:, m, :], mem_st[:, m, 2:3], None,
                                        ALU.mult).then_inc(S("mnorm"), 1)

        def mem_tensor_a(pe):
            pe.wait_ge(S("mnorm"), 2)
            for j in (0, 1):
                pe.wait_ge(evac[j], memk["mm0"][j])
            for k in range(KD):
                for m in (0, 1):
                    i = nc.tensor.transpose(bank[k // 2][:, (k % 2) * 256 + m * P:(k % 2) * 256 + (m + 1) * P],
                                            mem_n[:, m, k * P:(k + 1) * P], ident)
                if k % 2:
                    i.then_inc(S("memT"), 1)

        def mem_scalar_b(act):
            for k in range(KD):
                act.wait_ge(S("memT"), k // 2 + 1)
                if k % 2:
                    act.wait_ge(S("mem_lo"), k)
                nc.scalar.activation(mem_hi[:, k, :], bank[k // 2][:, (k % 2) * 256:(k % 2) * 256 + 256],
                                     ACT.Copy, scale=v_col("mem_norm", k)).then_inc(S("mem_hi"), 1)

        def mem_vector_b(dve):
            for k in range(KD):
                dve.wait_ge(S("mem_hi"), k + 1)
                nc.vector.scalar_tensor_tensor(
                    out=mem_lo[:, k, :], in0=bank[k // 2][:, (k % 2) * 256:(k % 2) * 256 + 256],
                    scalar=v_col("mem_norm", k), in1=mem_hi[:, k, :].bitcast(F),
                    op0=ALU.mult, op1=ALU.subtract).then_inc(S("mem_lo"), 1)

        def plain_evac(dve, ph, dst, normed=False):
            def one(i, s, st, t, count):
                t0, tn = ph["toks"][t]
                dve.wait_ge(mm[st], count)
                o = dst[:, ds(2 * i + s, 1), t0:t0 + tn]
                src = bank[3 * st + t][:, 0:tn].rearrange("p (a n) -> p a n", a=1)
                if normed:
                    nc.vector.tensor_tensor(o, src, rstd[:, t:t + 1, :], ALU.mult).then_inc(evac[st], 1)
                else:
                    nc.vector.tensor_copy(o, src).then_inc(evac[st], 1)
            each_tile(dve, ph, one)

        def nat_tensor(pe):
            for j in (0, 1):
                pe.wait_ge(evac[j], memv["mm1"][j])
            for m in (0, 1):
                pe.wait_ge(S("nat_a"), 2 * m)
                pe.wait_ge(S("nat_b"), 2 * m)
                for g, src in ((0, kT), (2, vT)):
                    for k in range(KD):
                        i = nc.tensor.transpose(bank[g + k // 4][:, (k % 4) * P:(k % 4 + 1) * P],
                                                src[:, k, m * P:(m + 1) * P], ident)
                        if k % 4 == 3:
                            i.then_inc(S("nat"), 1)

        def nat_scalar(act):
            for m in (0, 1):
                for b in (0, 1):
                    act.wait_ge(S("nat"), 4 * m + b + 1)
                    nc.scalar.activation(mk_n[:, m, b * 512:b * 512 + 512], bank[b][:, :], ACT.Copy)\
                        .then_inc(S("nat_a"), 1)

        def nat_vector(dve):
            for m in (0, 1):
                for b in (0, 1):
                    dve.wait_ge(S("nat"), 4 * m + 2 + b + 1)
                    nc.vector.tensor_copy(v_n[:, m, b * 512:b * 512 + 512], bank[2 + b][:, :])\
                        .then_inc(S("nat_b"), 1)

        def nat_out(sp):
            sp.wait_ge(S("nat_a"), 4)
            sp.dma_start(O["mem_k_prompt"][0, 0].rearrange("(m p) h d -> p m (h d)", p=P), mk_n[:, :, :])\
                .then_inc(S("mem_stored"), 16)
            sp.wait_ge(S("nat_b"), 4)
            sp.dma_start(O["mem_v_prompt"][0, 0].rearrange("(m p) h d -> p m (h d)", p=P), v_n[:, :, :])\
                .then_inc(S("mem_stored"), 16)

        SC = float(XD) ** -0.5
        cache_in = [S("cache_in0"), S("cache_in1")]

        def cache_loads(sp, name, n):
            if n < 2:
                sp.wait_ge(S("mem_stored"), 32) if name == "k" else sp.wait_ge(S("s_dot"), 8 * (7 + n))
            else:
                sp.wait_ge(S("s_dot") if name == "k" else S("o_smp"), (8 if name == "k" else 1) * (n - 1))
            sp.dma_start(cache[n % 2][:, :, :],
                         A[f"cache_mem_{name}"][0, n].rearrange("(m p) h d -> p m (h d)", p=P))\
                .then_inc(cache_in[n % 2], 16)

        def att_scores_pe(pe, n):
            c = slice(n * P, (n + 1) * P)
            pe.wait_ge(S("exp"), 4 * n)
            for h in range(XH):
                for d in (0, 1):
                    m = nc.tensor.matmul(bank[h // 2][:, (h % 2) * 256:(h % 2) * 256 + 256],
                                         qT[:, 2 * h + d, c], kT[:, 2 * h + d, :],
                                         start=d == 0, stop=d == 1)
                if h % 2:
                    m.then_inc(S("score"), 1)

        def att_query_pe(pe, n):
            pe.wait_ge(S("s_dot"), 8 * n)
            for k in range(KD):
                m = nc.tensor.matmul(bank[6 + k // 4][:, (k % 4) * P:(k % 4 + 1) * P],
                                     qT[:, k, SEQ + n:SEQ + n + 1].to_broadcast([P, P]), ident,
                                     start=True, stop=True)
            m.then_inc(S("q_bc"), 1)

        def att_out_pe(pe, n):
            b = n % 2
            pe.wait_ge(S("pnorm"), n + 1)
            pe.wait_ge(S("pT"), 2 * n)
            for h in range(XH):
                for m in (0, 1):
                    i = nc.tensor.transpose(bank[2 + h // 2][:, (h % 2) * 256 + m * P:(h % 2) * 256 + (m + 1) * P],
                                            prob[b][:, h, m * P:(m + 1) * P], ident)
                if h % 2:
                    i.then_inc(S("pTt"), 1)
            pe.wait_ge(S("o_lo"), 2 * n)
            for g in (0, 1):
                pe.wait_ge(S("pT"), 2 * n + g + 1)
                for h in (2 * g, 2 * g + 1):
                    for d in (0, 1):
                        for m in (0, 1):
                            i = nc.tensor.matmul(bank[4 + g][:, ((h % 2) * 2 + d) * P:((h % 2) * 2 + d + 1) * P],
                                                 v_n[:, m, h * XD + d * P:h * XD + (d + 1) * P],
                                                 probT[b][:, 2 * h + m, :], start=m == 0, stop=m == 1)
                i.then_inc(S("pv"), 1)

        def att_tensor(pe):
            for j in (0, 1):
                pe.wait_ge(evac[j], xaq["mm1"][j])
            for n in range(9):
                if n < 8:
                    att_scores_pe(pe, n)
                if n < 4:
                    att_query_pe(pe, 2 * n)
                if n == 4:
                    pe.wait_ge(S("s_dot"), 64)
                    for m in (0, 1):
                        i = nc.tensor.transpose(bank[6][0:32, m * P:(m + 1) * P], s_smp[:, :, m], ident)
                    i.then_inc(S("srow"), 1)
                if n:
                    att_out_pe(pe, n - 1)
                if n < 4:
                    att_query_pe(pe, 2 * n + 1)
                if n == 4:
                    pe.wait_ge(S("srow_v"), 2)
                    for m in (0, 1):
                        i = nc.tensor.transpose(bank[7][:, m * 32:(m + 1) * 32],
                                                p_smp[:, m * P:(m + 1) * P], ident[0:32, 0:32])
                    i.then_inc(S("srow"), 1)
                for b in (2 * n - 10, 2 * n - 9) if n > 4 else ():
                    pe.wait_ge(S("srow_v"), 4)
                    pe.wait_ge(cache_in[b % 2], 64 + 16 * (b // 2 + 1))
                    for h in range(XH):
                        for m in (0, 1):
                            i = nc.tensor.matmul(
                                bank[6 + h // 2][0:NS, (h % 2) * XD:(h % 2 + 1) * XD],
                                pT_smp[m].rearrange("p b x -> p (b x)")[
                                    :, 32 * b + 8 * h:32 * b + 8 * h + NS], cache[b % 2][:, m, h * XD:(h + 1) * XD],
                                start=b == 0 and m == 0 and h % 2 == 0, stop=b == NS - 1 and m == 1,
                                skip_group_check=True)
                    i.then_inc(S("o_smp"), 1)
            pe.wait_ge(S("o_rows"), 2)
            pe.wait_ge(S("o_hi"), 16)
            pe.wait_ge(S("exp"), 32)
            for k in range(KD):
                i = nc.tensor.transpose(bank[0][:, k * NS:(k + 1) * NS], o_rows[:, k * P:(k + 1) * P],
                                        ident[0:NS, 0:NS])
            i.then_inc(S("srow"), 1)

        def att_scalar(act):
            for n in range(9):
                if n < 8:
                    b = n % 2
                    act.wait_ge(S("nmax"), n + 1)
                    act.wait_ge(S("pTt"), 2 * max(n - 1, 0))
                    act.wait_ge(S("pnorm"), max(n - 1, 0))
                    for h in range(XH):
                        nc.scalar.activation(prob[b][:, h, :], bank[h // 2][:, (h % 2) * 256:(h % 2) * 256 + 256],
                                             ACT.Exp, scale=SC, bias=att[:, b, 0, h:h + 1],
                                             accum_out=att[:, b, 1, h:h + 1]).then_inc(S("exp"), 1)
                if n == 4:
                    act.wait_ge(S("srow_v"), 1)
                    nc.scalar.activation(p_smp[:, :], bank[6][0:32, 0:NMEM], ACT.Exp, scale=SC,
                                         bias=s_row[:, 0:1], accum_out=s_row[:, 1:2])\
                        .then_inc(S("srow_e"), 1)
                if n:
                    m = n - 1
                    c = slice(m * P, (m + 1) * P)
                    for g in (0, 1):
                        act.wait_ge(S("pTt"), 2 * m + g + 1)
                        act.wait_ge(S("pv"), 2 * max(m - 1, 0))
                        nc.scalar.activation(probT[m % 2][:, 4 * g:4 * g + 4, :],
                                             bank[2 + g][:, :].rearrange("p (k t) -> p k t", k=4),
                                             ACT.Copy).then_inc(S("pT"), 1)
                    for g in (0, 1):
                        act.wait_ge(S("pv"), 2 * m + g + 1)
                        nc.scalar.activation(o_hi[:, 4 * g:4 * g + 4, c],
                                             bank[4 + g][:, :].rearrange("p (k t) -> p k t", k=4),
                                             ACT.Copy).then_inc(S("o_hi"), 1)
            act.wait_ge(S("o_smp"), 8)
            nc.scalar.activation(o_rows[:, 0:512], bank[6][0:NS, :], ACT.Copy).then_inc(S("o_rows"), 1)
            act.wait_ge(S("srow"), 3)
            nc.scalar.activation(o_hi[:, :, SEQ:T], bank[0][:, 0:64].rearrange("p (k b) -> p k b", k=KD),
                                 ACT.Copy).then_inc(S("o_hi"), 1)

        def att_vector(dve):
            def dots(n):
                b = n % 2
                dve.wait_ge(S("q_bc"), n + 1)
                dve.wait_ge(cache_in[b], 16 * (n // 2 + 1))
                for m in (0, 1):
                    for h in range(XH):
                        dve.wait_ge(S("s_dot"), 8 * n + 4 * m + h)
                        nc.vector.scalar_tensor_tensor(
                            out=s_junk[:, :], in0=cache[b][:, m, h * XD:(h + 1) * XD], scalar=1.0,
                            in1=bank[6 + h // 2][:, (h % 2) * 256:(h % 2) * 256 + 256],
                            op0=ALU.mult, op1=ALU.mult,
                            accum_out=s_smp[:, n * XH + h, m:m + 1]).then_inc(S("s_dot"), 1)

            for j in (0, 1):
                dve.wait_ge(evac[j], xaq["mm1"][j])
            for n in range(9):
                if n < 8:
                    b = n % 2
                    for g in (0, 1):
                        dve.wait_ge(S("score"), 2 * n + g + 1)
                        dve.wait_ge(S("exp"), 4 * max(n - 1, 0))
                        link(nc.vector.tensor_reduce(
                            att[:, b, 3, 2 * g:2 * g + 2],
                            bank[g][:, :].rearrange("p (h m) -> p h m", h=2), AX.X, ALU.max))
                    nc.vector.tensor_scalar(att[:, b, 0, :], att[:, b, 3, :], -SC, None, ALU.mult)\
                        .then_inc(S("nmax"), 1)
                    if n < 4:
                        dots(2 * n)
                    dve.wait_ge(S("exp"), 4 * n + 4)
                    link(nc.vector.reciprocal(att[:, b, 2, :], att[:, b, 1, :]))
                    nc.vector.tensor_tensor(prob[b][:, :, :], prob[b][:, :, :],
                                            att[:, b, 2, :].unsqueeze(2).to_broadcast([P, XH, NMEM]),
                                            ALU.mult).then_inc(S("pnorm"), 1)
                    if n < 4:
                        dots(2 * n + 1)
                    if n == 4:
                        dve.wait_ge(S("srow"), 1)
                        link(nc.vector.tensor_reduce(s_row[:, 2:3], bank[6][0:32, 0:NMEM], AX.X, ALU.max))
                        nc.vector.tensor_scalar(s_row[:, 0:1], s_row[:, 2:3], -SC, None, ALU.mult)\
                            .then_inc(S("srow_v"), 1)
                        dve.wait_ge(S("srow_e"), 1)
                        link(nc.vector.reciprocal(s_row[:, 3:4], s_row[:, 1:2]))
                        nc.vector.tensor_scalar(p_smp[:, :], p_smp[:, :], s_row[:, 3:4], None, ALU.mult)\
                            .then_inc(S("srow_v"), 1)
                    if n == 5:
                        dve.wait_ge(S("srow"), 2)
                        link(nc.vector.memset(pT_smp[0][:, :, :], 0.0), False)
                        link(nc.vector.memset(pT_smp[1][:, :, :], 0.0))
                        for m in (0, 1):
                            nc.vector.tensor_copy(
                                pT_smp[m][:, :, 0:32:8],
                                bank[7][:, m * 32:m * 32 + 32].rearrange("p (b h) -> p b h", b=NS))\
                                .then_inc(S("srow_v"), 1)
                if n:
                    m = n - 1
                    c = slice(m * P, (m + 1) * P)
                    for g in (0, 1):
                        dve.wait_ge(S("o_hi"), 2 * m + g + 1)
                        nc.vector.tensor_tensor(o_lo[:, 4 * g:4 * g + 4, c],
                                                bank[4 + g][:, :].rearrange("p (k t) -> p k t", k=4),
                                                o_hi[:, 4 * g:4 * g + 4, c].bitcast(F), ALU.subtract)\
                            .then_inc(S("o_lo"), 1)
            dve.wait_ge(S("o_smp"), 8)
            nc.vector.tensor_copy(o_rows[:, 512:D], bank[7][0:NS, :]).then_inc(S("o_rows"), 1)
            dve.wait_ge(S("o_hi"), 17)
            nc.vector.tensor_tensor(o_lo[:, :, SEQ:T], bank[0][:, 0:64].rearrange("p (k b) -> p k b", k=KD),
                                    o_hi[:, :, SEQ:T].bitcast(F), ALU.subtract).then_inc(S("o_lo"), 1)

        def blk_rows(n):
            return P if n < 8 else NS

        def final_tensor(pe):
            for j in (0, 1):
                pe.wait_ge(evac[j], ffn2[-1][1]["mm1"][j])
            for n in range(9):
                pe.wait_ge(S("y_normed"), 2 * max(n - 2, 0))
                for k in range(KD):
                    m = nc.tensor.transpose(
                        bank[2 * (n % 3) + k // 4][0:blk_rows(n), (k % 4) * P:(k % 4 + 1) * P],
                        x[:, k, n * P:n * P + blk_rows(n)], ident)
                    if k % 4 == 3:
                        m.then_inc(S("yt"), 1)

        def final_scalar(act):
            for n in range(9):
                r = slice(0, blk_rows(n))
                for h in (0, 1):
                    act.wait_ge(S("yt"), 2 * n + h + 1)
                    act.wait_ge(S("y_sq"), 3 * n if h == 0 else max(3 * n - 1, 0))
                    nc.scalar.activation(fin_sq[r, h, :], bank[2 * (n % 3) + h][r, :], ACT.Square,
                                         accum_out=fin_st[r, n, h:h + 1]).then_inc(S("y_sq"), 1)
                act.wait_ge(S("y_ms"), n + 1)
                nc.scalar.activation(fin_st[r, n, 3:4], fin_st[r, n, 2:3], ACT.Sqrt,
                                     bias=eps_t[r, 0:1], scale=1.0 / D).then_inc(S("y_sq"), 1)

        def final_vector(dve):
            dve.wait_ge(S("fin_in"), 16)
            for n in range(9):
                r = slice(0, blk_rows(n))
                dve.wait_ge(S("y_sq"), 3 * n + 2)
                nc.vector.tensor_tensor(fin_st[r, n, 2:3], fin_st[r, n, 0:1], fin_st[r, n, 1:2],
                                        ALU.add).then_inc(S("y_ms"), 1)
                dve.wait_ge(S("y_sq"), 3 * n + 3)
                link(nc.vector.reciprocal(fin_st[r, n, 2:3], fin_st[r, n, 3:4]))
                for h in (0, 1):
                    nc.vector.scalar_tensor_tensor(
                        out=y_nat[r, n, 512 * h:512 * h + 512], in0=bank[2 * (n % 3) + h][r, :],
                        scalar=fin_st[r, n, 2:3], in1=fin_g[r, 512 * h:512 * h + 512],
                        op0=ALU.mult, op1=ALU.mult).then_inc(S("y_normed"), 1)

        def final_out(sp):
            for n in range(9):
                sp.wait_ge(S("y_normed"), 2 * n + 2)
                if n < 8:
                    sp.dma_start(O["y_prompt"][0, n * P:(n + 1) * P, :], y_nat[:, n, :])\
                        .then_inc(S("y_stored"), 16)
                else:
                    sp.dma_start(O["y_sample"][:, 0, :], y_nat[0:NS, n, :]).then_inc(S("y_stored"), 16)
            sp.wait_ge(S("y_stored"), 144)
            sp.wait_ge(S("mem_stored"), 32)
            sp.wait_ge(S("state_stored"), 80)

        smp_d = nc.dram_tensor("smp_d", (6, NS, BW), F, kind="Internal").ap()
        smp_od = nc.dram_tensor("smp_od", (NS, BW), F, kind="Internal").ap()
        x_save = nc.dram_tensor("x_save", (P, KD, T), F, kind="Internal").ap()
        y_save = nc.dram_tensor("y_save", (P, 4, T), F, kind="Internal").ap()

        block = ctx.enter_context(nc.Block())

        @block.sync
        def _(sp):
            sp.dma_start(cst[:], A["constants"]).then_inc(S("cst_in"), 16)
            sp.dma_start(xnat_s[0:NS, :], A["x_sample"][:, 0, :]).then_inc(S("x_in1"), 16)
            for n in range(8):
                sp.dma_start(xnat[:, n, :], A["x_prompt"][0, n * P:(n + 1) * P, :])\
                    .then_inc(S("x_in0") if n < 1 else S("x_in1") if n < 4 else S("x_in2"), 16)
            for a, b in ffn1:
                load_weights(sp, a)
                load_weights(sp, b)
            load_weights(sp, win_a)
            gmlp_loads(sp)
            load_weights(sp, win_b)
            load_weights(sp, win_c)
            load_weights(sp, win_d)
            sp.wait_ge(S("vn"), 9)
            sp.dma_start(O["chunk_v_sample"][0, :, 0, :], vn[0:NS, 2, :]).then_inc(S("vchunk_stored"), 16)
            load_weights(sp, win_e)
            sp.wait_ge(S("gmix"), 9)
            sp.wait_ge(S("gmix"), 10)
            sp.dma_start(lora_w[0:64, 0, :], A["rwkv_w2"][0]).then_inc(S("lora_in"), 16)
            sp.dma_start(lora_w[64:128, 1, :], A["rwkv_a2"][0]).then_inc(S("lora_in"), 16)
            sp.dma_start(y_save, z[:, 8:12, :]).then_inc(S("ya_stored"), 16)
            win_done(sp)
            sp.dma_start(shift_in[:, :], A["state_shift"][0, :, 0, :]).then_inc(S("prep_in"), 16)
            sp.wait_ge(S("shift_a"), 4)
            sp.dma_start(O["state_shift_prompt"][0, :, 0, :], shift_out[0:1, :]).then_inc(S("state_stored"), 16)
            sp.dma_start(O["state_shift_sample"][0, :, 0, :], shift_out[1:NS + 1, :])\
                .then_inc(S("state_stored"), 16)
            sp.wait_ge(S("ya_stored"), 16)
            sp.wait_ge(S("vchunk_stored"), 16)
            sp.wait_ge(S("state_stored"), 32)
            sample_loads(sp)
            load_weights(sp, wout)
            for ph in (memk, memv):
                load_weights(sp, ph)
            load_weights(sp, xaq)
            for n in range(8):
                cache_loads(sp, "k", n)
            for n in range(8):
                cache_loads(sp, "v", n)
            load_weights(sp, xao)
            sp.wait_ge(S("o_lo"), 17)
            sp.dma_start(fin_g[:, :], A["final_norm"].partition_broadcast(P)).then_inc(S("fin_in"), 16)
            for a, b in ffn2:
                load_weights(sp, a)
                load_weights(sp, b)
            final_out(sp)

        @block.gpsimd
        def _(g):
            nc.gpsimd.memset(eps_t[:, 0:1], 1e-6).then_inc(S("const"), 1)
            nc.gpsimd.memset(eps_t[:, 1:2], 1e-5).then_inc(S("const"), 1)
            nc.gpsimd.memset(eps_t[:, 2:3], 64e-5).then_inc(S("const"), 1)
            nc.gpsimd.memset(eps_t[:, 3:4], LOG_SHIFT / 2).then_inc(S("const"), 1)
            g.wait_ge(S("vz"), 1)
            for name, k in VROWS:
                r0, src = VAT[name], A[name]
                src = src[0] if name != "final_norm" else src
                if name == "rwkv_mu":
                    g.dma_start(vnat[r0:r0 + k - 1, :],
                                src[0:(k - 1) * P].rearrange("(k p) -> k p", p=P)).then_inc(S("v_in"), 16)
                    g.dma_start(vnat[r0 + k - 1:r0 + k, 0:NB - (k - 1) * P],
                                src[(k - 1) * P:NB].rearrange("(k p) -> k p", k=1)).then_inc(S("v_in"), 16)
                elif name == "rwkv_r_k":
                    g.dma_start(vnat[r0:r0 + k, :], src.rearrange("(k a) p -> k (a p)", a=2))\
                        .then_inc(S("v_in"), 16)
                else:
                    g.dma_start(vnat[r0:r0 + k, :], src.rearrange("(k p) -> k p", p=P))\
                        .then_inc(S("v_in"), 16)
            g.wait_ge(S("cst_in"), 16)
            for a, b in ffn1:
                split_weights(g, a)
                split_weights(g, b)
            for ph in win:
                split_weights(g, ph)
            shift_pool(g)
            g.wait_ge(S("mix_p"), 35)
            for n in range(8):
                chunk_pool(g, n)
            sample_pool(g)
            post_pool(g)
            for ph in (wout, memk, memv, xaq, xao, *(p for ab in ffn2 for p in ab)):
                split_weights(g, ph, high=ph not in (memk, memv))

        NVDMA = 16 * (len(VROWS) + 1)

        @block.tensor
        def _(pe):
            pe.wait_ge(S("cst_in"), 16)
            for n in range(8):
                pe.wait_ge(*((S("x_in0"), 16) if n < 1 else (S("x_in1"), 64) if n < 4 else (S("x_in2"), 64)))
                b = 2 * (n % 4)
                if n >= 4:
                    pe.wait_ge(S("xt_a"), n - 3)
                    pe.wait_ge(S("xt_b"), n - 3)
                for k in range(KD):
                    m = nc.tensor.transpose(bank[b + k // 4][:, (k % 4) * P:(k % 4 + 1) * P],
                                            xnat[:, n, k * P:(k + 1) * P], ident)
                    if k % 4 == 3:
                        m.then_inc(S("xt"), 1)
                if n == 2:
                    pe.wait_ge(S("v_in"), NVDMA)
                    nc.tensor.transpose(bank[7][:, 0:NVEC], vnat[0:NVEC, :], ident[0:NVEC, 0:NVEC])\
                        .then_inc(S("vt"), 1)
                    pe.wait_ge(S("vz"), 2)
            pe.wait_ge(S("xt_a"), 5)
            for k in range(KD):
                m = nc.tensor.transpose(bank[0][:, k * NS:(k + 1) * NS],
                                        xnat_s[0:NS, k * P:(k + 1) * P], ident[0:NS, 0:NS])
            m.then_inc(S("xt"), 1)
            pe.wait_ge(S("xt_a"), 9)
            pe.wait_ge(S("xt_b"), 8)
            for a, b in ffn1:
                if a["f0"] == 0:
                    multiply(pe, a, tile_ready=lambda t: pe.wait_ge(S("x_lo"), KD * (t + 1)),
                             after_first=lambda: rms_tensor(pe, 0))
                else:
                    multiply(pe, a)
                multiply(pe, b, lambda h, b=b: pe.wait_ge(
                    S("hid_lo"), 3 * (b["f1"] - b["kt"] + (min(4, b["kt"]) if h == 0 else b["kt"]))))
            for ph in win:
                if ph is win_a:
                    multiply(pe, ph, lambda h: pe.wait_ge(S("x_lo"), 24 + 12 * (h + 1)),
                             after_first=lambda: rms_tensor(pe, 1))
                else:
                    if ph is win_b:
                        gmlp_tensor_start(pe)
                    multiply(pe, ph, after=gmlp_steps(ph, lambda n: gmlp_tensor(pe, n)))
            prep_tensor(pe)
            for n in range(8):
                chunk_tensor(pe, n)
            post_tensor(pe)
            pe.wait_ge(S("yb_lo"), 1)
            multiply(pe, wout, lambda h: pe.wait_ge(S("yb_lo"), 13))
            mem_tensor_a(pe)
            rms_tensor(pe, 2)
            pe.wait_ge(S("mem_lo"), KD)
            multiply(pe, memk)
            multiply(pe, memv)
            nat_tensor(pe)
            pe.wait_ge(S("nat_a"), 4)
            pe.wait_ge(S("nat_b"), 4)
            multiply(pe, xaq)
            att_tensor(pe)
            pe.wait_ge(S("o_lo"), 17)
            multiply(pe, xao)
            for a, b in ffn2:
                if a is ffn2[0][0]:
                    multiply(pe, a, lambda h: pe.wait_ge(S("x_lo"), 72 + 12 * (h + 1)),
                             after_first=lambda: rms_tensor(pe, 3))
                else:
                    multiply(pe, a)
                multiply(pe, b, lambda h, b=b: pe.wait_ge(
                    S("hid_lo"), 3 * (b["f1"] - b["kt"] + (min(4, b["kt"]) if h == 0 else b["kt"]))))
            final_tensor(pe)


        @block.scalar
        def _(act):
            for t in range(3):
                for n in range(3 * t, min(3 * t + 3, 8)):
                    act.wait_ge(S("xt"), 2 * n + 1)
                    nc.scalar.activation(x[:, 0:4, n * P:(n + 1) * P],
                                         bank[2 * (n % 4)][:, :].rearrange("p (k n) -> p k n", k=4),
                                         ACT.Copy).then_inc(S("xt_a"), 1)
                if t == 2:
                    act.wait_ge(S("xt"), 17)
                    nc.scalar.activation(x[:, :, SEQ:T],
                                         bank[0][:, 0:KD * NS].rearrange("p (k n) -> p k n", k=KD),
                                         ACT.Copy).then_inc(S("xt_a"), 1)
                act.wait_ge(S("vz"), 2)
                act.wait_ge(S("xt_a"), 3 * t + 3)
                act.wait_ge(S("xt_b"), min(3 * t + 3, 8))
                for k in range(KD):
                    split_scalar(act, 0, "ln_ffn1", h_hi, k, t, KD * t + k)
            rms_scalar(act, 0)
            prev = None
            for a, b in ffn1:
                gu_scalar(act, a, prev)
                prev = b
            residual_scalar(act, 1, "ln_mix", ffn1[-1][1], h_hi)
            act.dma_start(x_save, x[:, :, :]).then_inc(S("x_stored"), 16)
            rms_scalar(act, 1)
            gmlp_scalar(act)
            shift_scalar(act)
            prep_scalar(act)
            for n in range(8):
                chunk_scalar(act, n)
            post_scalar(act)
            mem_scalar_a(act)
            residual_scalar(act, 2, "ln_xattn", wout, h_hi)
            mem_scalar_b(act)
            rms_scalar(act, 2)
            for ph in (memk, memv):
                split_weights(act, ph, low=False)
            nat_scalar(act)
            nat_out(act)
            att_scalar(act)
            residual_scalar(act, 3, "ln_ffn2", xao, h2_hi)
            rms_scalar(act, 3)
            prev = None
            for a, b in ffn2:
                gu_scalar(act, a, prev)
                prev = b
            final_scalar(act)

        @block.vector
        def _(dve):
            nc.vector.memset(vnat[:, :], 0.0).then_inc(S("vz"), 1)
            for t in range(3):
                for n in range(3 * t, min(3 * t + 3, 8)):
                    dve.wait_ge(S("xt"), 2 * n + 2)
                    nc.vector.tensor_copy(x[:, 4:8, n * P:(n + 1) * P],
                                          bank[2 * (n % 4) + 1][:, :].rearrange("p (k n) -> p k n", k=4))\
                        .then_inc(S("xt_b"), 1)
                if t == 0:
                    dve.wait_ge(S("vt"), 1)
                    nc.vector.tensor_copy(vec[:, :], bank[7][:, 0:NVEC]).then_inc(S("vz"), 1)
                    dve.wait_ge(S("vz"), 2)
                for k in range(KD):
                    split_vector(dve, 0, "ln_ffn1", h_hi, h_lo, k, t, KD * t + k)
            rms_vector(dve, 0)
            for a, b in ffn1:
                gu_vector(dve, a)
                if b is ffn1[-1][1]:
                    residual_vector(dve, 1, "ln_mix", b, h_hi, h_lo, 0.5)
                else:
                    add_to_x(dve, b, 0.5)
            rms_vector(dve, 1)
            z_evac(dve)
            shift_vector(dve)
            prep_vector(dve)
            for n in range(8):
                chunk_vector(dve, n)
            post_vector(dve)
            mem_vector_a(dve)
            residual_vector(dve, 2, "ln_xattn", wout, h_hi, h_lo, 1.0)
            mem_vector_b(dve)
            rms_vector(dve, 2)
            plain_evac(dve, memk, kT)
            plain_evac(dve, memv, vT)
            nat_vector(dve)
            plain_evac(dve, xaq, qT, normed=True)
            att_vector(dve)
            residual_vector(dve, 3, "ln_ffn2", xao, h2_hi, h2_lo, 1.0)
            rms_vector(dve, 3)
            for a, b in ffn2:
                gu_vector(dve, a)
                add_to_x(dve, b, 0.5)
            final_vector(dve)


_IN = ["x_prompt", "x_sample", "state_rwkv", "state_shift", "cache_mem_k", "cache_mem_v", "mem_prompt",
       "ln_ffn1", "ffn1_gate", "ffn1_up", "ffn1_down", "ln_mix", "w_in", "w_out", "sgu_w", "sgu_b",
       "sgu_ln_g", "sgu_ln_b", "rwkv_mu", "rwkv_w0", "rwkv_w2", "rwkv_a0", "rwkv_a2", "rwkv_g2",
       "rwkv_k_k", "rwkv_k_a", "rwkv_r_k", "rwkv_gn_g", "rwkv_gn_b", "ln_xattn", "mem_norm", "xa_q",
       "xa_k", "xa_v", "xa_o", "ln_ffn2", "ffn2_gate", "ffn2_up", "ffn2_down", "final_norm"]
_OUT = [("y_prompt", (1, SEQ, D)), ("y_sample", (NS, 1, D)),
        ("state_rwkv_prompt", (1, 1, HEADS, HN, HN)), ("state_shift_prompt", (1, 1, 1, NB)),
        ("mem_k_prompt", (1, 1, NMEM, XH, XD)), ("mem_v_prompt", (1, 1, NMEM, XH, XD)),
        ("state_rwkv_sample", (1, NS, HEADS, HN, HN)), ("state_shift_sample", (1, NS, 1, NB)),
        ("chunk_v_sample", (1, NS, 1, AW))]


def kernel(**inputs):
    import concourse.bacc as bacc
    from concourse.bass_utils import run_bass_kernel_spmd

    nc = bacc.Bacc("TRN2", target_bir_lowering=False, num_devices=1)
    arrays = {f"in_{n}": np.ascontiguousarray(inputs[n]) for n in _IN}
    arrays["in_constants"] = constants()
    A = {k[3:]: nc.dram_tensor(k, a.shape, mybir.dt.from_np(a.dtype), kind="ExternalInput").ap()
         for k, a in arrays.items()}
    O = {n: nc.dram_tensor(f"out_{n}", s, mybir.dt.float32, kind="ExternalOutput").ap() for n, s in _OUT}
    program(nc, A, O)
    r = run_bass_kernel_spmd(nc, [arrays], core_ids=[0])
    return tuple(r.results[0][f"out_{n}"] for n, _ in _OUT)
```
